# Optimizing a Trainium2 kernel written in Bass

```python
import math
import jax, jax.numpy as jnp
from jax import lax
import numpy as np

D_MODEL = 1024
BATCH = 1
SEQ = 256
DEPTH = 2

CHUNK = 64
D_MIX = D_MODEL
D_LRU = D_MIX // 2
LRU_BLOCKS = 8
LRU_BLOCK = D_LRU // LRU_BLOCKS
CONV_WIDTH = 4
LRU_C = 8.0
D_ATTN = D_MIX - D_LRU
HEAD_DIM = 64
N_Q_HEADS = D_ATTN // HEAD_DIM
N_KV_HEADS = 2
Q_PER_KV = N_Q_HEADS // N_KV_HEADS
D_KV = N_KV_HEADS * HEAD_DIM
WINDOW = 128
WINDOW_CHUNKS = WINDOW // CHUNK
BAND = WINDOW_CHUNKS * CHUNK
ROT_DIM = HEAD_DIM // 4
ROPE_THETA = 500000.0
MASK_VALUE = -1e30
OFF_GATE = D_LRU
OFF_Q = 2 * D_LRU
OFF_K = OFF_Q + D_ATTN
OFF_V = OFF_K + D_KV
D_IN = OFF_V + D_KV
D_FF = 2816
N_EXPERTS = 8
TOP_K = 2
D_FF_EXPERT = 2816
MOE_BLOCK = 256
N_DENSE = (DEPTH + 1) // 2
N_MOE = DEPTH // 2
DEEPNORM_ALPHA = (2 * DEPTH) ** 0.25
DEEPNORM_BETA = (8 * DEPTH) ** -0.25
LN_EPS = 1e-5

kernel_name = 'hybrid_rglru_swa_moe_deepnorm'

F32 = jnp.float32

def layer_norm(x, g, b):
    xf = x.astype(F32)
    mu = jnp.mean(xf, axis=-1, keepdims=True)
    var = jnp.mean(jnp.square(xf - mu), axis=-1, keepdims=True)
    return ((xf - mu) * lax.rsqrt(var + LN_EPS) * g.astype(F32) + b.astype(F32)).astype(x.dtype)

def causal_depthwise_conv(u, w, b):
    y = lax.conv_general_dilated(u, w[:, None, :].astype(u.dtype), window_strides=(1,),
                                 padding=[(CONV_WIDTH - 1, 0)],
                                 dimension_numbers=('NWC', 'WIO', 'NWC'),
                                 feature_group_count=u.shape[-1])
    return y + b.astype(u.dtype)

def rg_lru(u, wa, ba, wx, bx, lam):
    B, S, _ = u.shape
    uf = u.astype(F32)
    ub = uf.reshape(B, S, LRU_BLOCKS, LRU_BLOCK)
    r = jax.nn.sigmoid(jnp.einsum('bshi,hij->bshj', ub, wa.astype(F32)).reshape(B, S, D_LRU) + ba.astype(F32))
    i = jax.nn.sigmoid(jnp.einsum('bshi,hij->bshj', ub, wx.astype(F32)).reshape(B, S, D_LRU) + bx.astype(F32))
    log_a = -LRU_C * r * jax.nn.softplus(-lam.astype(F32))
    a = jnp.exp(log_a)
    b = jnp.sqrt(-jnp.expm1(2.0 * log_a)) * (i * uf)

    def combine(c1, c2):
        a1, b1 = c1
        a2, b2 = c2
        return a1 * a2, a2 * b1 + b2

    _, h = lax.associative_scan(combine, (a, b), axis=1)
    return h.astype(u.dtype)

def rope_partial(t, cos, sin):
    half = ROT_DIM // 2
    c = cos[None, :, None, :].astype(t.dtype)
    s = sin[None, :, None, :].astype(t.dtype)
    t1 = t[..., :half]
    t2 = t[..., half:ROT_DIM]
    return jnp.concatenate([t1 * c - t2 * s, t2 * c + t1 * s, t[..., ROT_DIM:]], axis=-1)

def chunk_window_attention(q, k, v, sink):
    B, S = q.shape[:2]
    nc = S // CHUNK
    qc = q.reshape(B, nc, CHUNK, N_KV_HEADS, Q_PER_KV, HEAD_DIM)

    def band(t):
        t = t.reshape(B, nc, CHUNK, N_KV_HEADS, HEAD_DIM)
        tp = jnp.pad(t, ((0, 0), (WINDOW_CHUNKS - 1, 0), (0, 0), (0, 0), (0, 0)))
        return jnp.concatenate([tp[:, j:j + nc] for j in range(WINDOW_CHUNKS)], axis=2)

    kb = band(k)
    vb = band(v)
    scores = jnp.einsum('bcqgrd,bckgd->bcgrqk', qc, kb).astype(F32) * (1.0 / math.sqrt(HEAD_DIM))
    key_chunk = (jnp.arange(nc)[:, None] - (WINDOW_CHUNKS - 1)
                 + (jnp.arange(BAND) // CHUNK)[None, :])
    valid = (key_chunk >= 0)[None, :, None, None, None, :]
    scores = jnp.where(valid, scores, MASK_VALUE)
    sk = sink.astype(F32).reshape(1, 1, N_KV_HEADS, Q_PER_KV, 1, 1)
    m = jnp.maximum(jnp.max(scores, axis=-1, keepdims=True), sk)
    p = jnp.exp(scores - m)
    p = p / (jnp.sum(p, axis=-1, keepdims=True) + jnp.exp(sk - m))
    out = jnp.einsum('bcgrqk,bckgd->bcqgrd', p.astype(v.dtype), vb)
    return out.reshape(B, S, N_Q_HEADS * HEAD_DIM)

def hybrid_mixer(x, w_in, conv_w, conv_b, wa, ba, wx, bx, lam, sink, w_out, cos, sin):
    B, S, _ = x.shape
    proj = x @ w_in
    u = proj[..., :OFF_GATE]
    gate = proj[..., OFF_GATE:OFF_Q]
    q = proj[..., OFF_Q:OFF_K].reshape(B, S, N_Q_HEADS, HEAD_DIM)
    k = proj[..., OFF_K:OFF_V].reshape(B, S, N_KV_HEADS, HEAD_DIM)
    v = proj[..., OFF_V:].reshape(B, S, N_KV_HEADS, HEAD_DIM)
    y_lru = jax.nn.gelu(gate) * rg_lru(causal_depthwise_conv(u, conv_w, conv_b), wa, ba, wx, bx, lam)
    y_attn = chunk_window_attention(rope_partial(q, cos, sin), rope_partial(k, cos, sin), v, sink)
    return jnp.concatenate([y_lru, y_attn], axis=-1) @ w_out

def swiglu(x, wg, wu, wd):
    return (jax.nn.silu(x @ wg) * (x @ wu)) @ wd

def moe_swiglu(x, router_w, router_b, wg, wu, wd):
    B, S, D = x.shape
    n_tok = B * S
    n_assign = n_tok * TOP_K
    n_blocks = n_assign // MOE_BLOCK + N_EXPERTS
    n_rows = n_blocks * MOE_BLOCK
    xt = x.reshape(n_tok, D)
    logits = xt.astype(F32) @ router_w.astype(F32) + router_b.astype(F32)
    top_logit, top_idx = lax.top_k(logits, TOP_K)
    top_w = jax.nn.softmax(top_logit, axis=-1)
    e_flat = top_idx.reshape(-1)
    tok_flat = jnp.arange(n_assign, dtype=jnp.int32) // TOP_K
    w_flat = top_w.reshape(-1)
    order = jnp.argsort(e_flat)
    e_sorted = e_flat[order]
    tok_sorted = tok_flat[order]
    w_sorted = w_flat[order]
    counts = jnp.sum(jax.nn.one_hot(e_flat, N_EXPERTS, dtype=jnp.int32), axis=0)
    starts = jnp.cumsum(counts) - counts
    padded = (counts + MOE_BLOCK - 1) // MOE_BLOCK * MOE_BLOCK
    pstarts = jnp.cumsum(padded) - padded
    pends = pstarts + padded
    dest = pstarts[e_sorted] + jnp.arange(n_assign, dtype=jnp.int32) - starts[e_sorted]
    row_tok = jnp.zeros((n_rows,), jnp.int32).at[dest].set(tok_sorted)
    row_w = jnp.zeros((n_rows,), F32).at[dest].set(w_sorted)
    block_start = jnp.arange(n_blocks, dtype=jnp.int32) * MOE_BLOCK
    block_e = jnp.minimum(jnp.sum(block_start[:, None] >= pends[None, :], axis=1), N_EXPERTS - 1)

    def expert_block(args):
        tok, w, e = args
        xb = xt[tok]
        h = jax.nn.silu(xb @ wg[e]) * (xb @ wu[e])
        return (h @ wd[e]).astype(F32) * w[:, None]

    y = lax.map(expert_block, (row_tok.reshape(n_blocks, MOE_BLOCK),
                               row_w.reshape(n_blocks, MOE_BLOCK), block_e))
    out = jnp.zeros((n_tok, D), F32).at[row_tok].add(y.reshape(n_rows, D))
    return out.astype(x.dtype).reshape(B, S, D)

def setup_inputs(seed: int = 0) -> dict:
    key = jax.random.key(seed)
    ks = jax.random.split(key, 24)

    def nrm(k, shape, scale):
        return jax.random.normal(k, shape, F32) * scale

    x = nrm(ks[0], (BATCH, SEQ, D_MODEL), 1.0)
    ln1_g = 1.0 + nrm(ks[1], (DEPTH, D_MODEL), 0.02)
    ln1_b = nrm(ks[2], (DEPTH, D_MODEL), 0.02)
    w_in = nrm(ks[3], (DEPTH, D_MODEL, D_IN), D_MODEL ** -0.5)
    w_in = w_in.at[..., OFF_V:].multiply(DEEPNORM_BETA)
    conv_w = nrm(ks[4], (DEPTH, CONV_WIDTH, D_LRU), CONV_WIDTH ** -0.5)
    conv_b = nrm(ks[5], (DEPTH, D_LRU), 0.02)
    lru_wa = nrm(ks[6], (DEPTH, LRU_BLOCKS, LRU_BLOCK, LRU_BLOCK), LRU_BLOCK ** -0.5)
    lru_ba = nrm(ks[7], (DEPTH, D_LRU), 0.02)
    lru_wx = nrm(ks[8], (DEPTH, LRU_BLOCKS, LRU_BLOCK, LRU_BLOCK), LRU_BLOCK ** -0.5)
    lru_bx = nrm(ks[9], (DEPTH, D_LRU), 0.02)
    a_c = jax.random.uniform(ks[10], (DEPTH, D_LRU), F32, 0.9, 0.999)
    sig = a_c ** (1.0 / LRU_C)
    lru_lambda = jnp.log(sig) - jnp.log1p(-sig)
    attn_sink = nrm(ks[11], (DEPTH, N_Q_HEADS), 0.5)
    w_out = nrm(ks[12], (DEPTH, D_MIX, D_MODEL), D_MIX ** -0.5 * DEEPNORM_BETA)
    ln2_g = 1.0 + nrm(ks[13], (DEPTH, D_MODEL), 0.02)
    ln2_b = nrm(ks[14], (DEPTH, D_MODEL), 0.02)
    ffn_w_gate = nrm(ks[15], (N_DENSE, D_MODEL, D_FF), D_MODEL ** -0.5)
    ffn_w_up = nrm(ks[16], (N_DENSE, D_MODEL, D_FF), D_MODEL ** -0.5)
    ffn_w_down = nrm(ks[17], (N_DENSE, D_FF, D_MODEL), D_FF ** -0.5 * DEEPNORM_BETA)
    router_w = nrm(ks[18], (N_MOE, D_MODEL, N_EXPERTS), D_MODEL ** -0.5)
    router_b = nrm(ks[19], (N_MOE, N_EXPERTS), 0.01)
    exp_w_gate = nrm(ks[20], (N_MOE, N_EXPERTS, D_MODEL, D_FF_EXPERT), D_MODEL ** -0.5)
    exp_w_up = nrm(ks[21], (N_MOE, N_EXPERTS, D_MODEL, D_FF_EXPERT), D_MODEL ** -0.5)
    exp_w_down = nrm(ks[22], (N_MOE, N_EXPERTS, D_FF_EXPERT, D_MODEL), D_FF_EXPERT ** -0.5 * DEEPNORM_BETA)
    return {'x': x, 'ln1_g': ln1_g, 'ln1_b': ln1_b, 'w_in': w_in, 'conv_w': conv_w, 'conv_b': conv_b,
            'lru_wa': lru_wa, 'lru_ba': lru_ba, 'lru_wx': lru_wx, 'lru_bx': lru_bx, 'lru_lambda': lru_lambda,
            'attn_sink': attn_sink, 'w_out': w_out, 'ln2_g': ln2_g, 'ln2_b': ln2_b,
            'ffn_w_gate': ffn_w_gate, 'ffn_w_up': ffn_w_up, 'ffn_w_down': ffn_w_down,
            'router_w': router_w, 'router_b': router_b,
            'exp_w_gate': exp_w_gate, 'exp_w_up': exp_w_up, 'exp_w_down': exp_w_down}

def reference(x, ln1_g, ln1_b, w_in, conv_w, conv_b, lru_wa, lru_ba, lru_wx, lru_bx, lru_lambda,
              attn_sink, w_out, ln2_g, ln2_b, ffn_w_gate, ffn_w_up, ffn_w_down,
              router_w, router_b, exp_w_gate, exp_w_up, exp_w_down):
    S = x.shape[1]
    pos = jnp.arange(S, dtype=F32)
    inv_freq = ROPE_THETA ** (-jnp.arange(0, ROT_DIM, 2, dtype=F32) / ROT_DIM)
    ang = pos[:, None] * inv_freq[None, :]
    cos = jnp.cos(ang)
    sin = jnp.sin(ang)
    for l in range(DEPTH):
        mix = hybrid_mixer(x, w_in[l], conv_w[l], conv_b[l], lru_wa[l], lru_ba[l], lru_wx[l], lru_bx[l],
                           lru_lambda[l], attn_sink[l], w_out[l], cos, sin)
        x = layer_norm(DEEPNORM_ALPHA * x + mix, ln1_g[l], ln1_b[l])
        if l % 2 == 0:
            j = l // 2
            ffn = swiglu(x, ffn_w_gate[j], ffn_w_up[j], ffn_w_down[j])
        else:
            j = l // 2
            ffn = moe_swiglu(x, router_w[j], router_b[j], exp_w_gate[j], exp_w_up[j], exp_w_down[j])
        x = layer_norm(DEEPNORM_ALPHA * x + ffn, ln2_g[l], ln2_b[l])
    return x


_drawn_inputs = setup_inputs


def setup_inputs(seed=0):
    import zlib

    import numpy as np

    out = dict(_drawn_inputs(seed))
    spreads = {}
    factors = {'lru_ba': 34.864, 'lru_bx': 39.525, 'attn_sink': 29.456, 'router_b': 8.0}
    for name, (base, spread) in spreads.items():
        noise = np.random.default_rng([zlib.crc32(name.encode()), seed]).standard_normal(out[name].shape)
        drawn = base * np.exp(spread * noise) if base else spread * noise
        out[name] = __import__('jax').numpy.asarray(drawn.astype(out[name].dtype))
    for name, factor in factors.items():
        out[name] = (out[name] * factor).astype(out[name].dtype)
    return out
```

```python
from contextlib import ExitStack

import numpy as np

import concourse.bass as bass
from concourse import mybir

F32 = mybir.dt.float32
F32R = mybir.dt.float32r
I32 = mybir.dt.int32
U32 = mybir.dt.uint32
ALU = mybir.AluOpType
ACT = mybir.ActivationFunctionType
AX = mybir.AxisListType.X

P = 128
T = 256
NT = T // P
D = 1024
KT = D // P
DEPTH = 2
DLRU = 512
CT = DLRU // P
TAPS = 4
HD = 64
NH = 8
NKV = 2
CH = 64
ROT = 16
F = 2816
FC = 256
NCH = F // FC
NE = 8
ALPHA = float((2 * DEPTH) ** 0.25)
EPS = 1e-5
BIG = 1.0e6

PW = 2048
RING = 11
SPLIT = 3
MIXP = 11
FFP = 3 * NCH
STREAM = 2 * MIXP + FFP
NPIECE = STREAM + NE * FFP

FFORDER = [("A", 0), ("B", 0)]
for _c in range(1, NCH):
    FFORDER += [("A", _c), ("B", _c), ("D", _c - 1)]
FFORDER += [("D", NCH - 1)]
STEP = {kc: i for i, kc in enumerate(FFORDER)}
H_AT = {STEP[("B", c)] + 1: c for c in range(NCH)}
T_AFTER = {(STEP[("A", 1)] if c == 0 else STEP[("D", c - 1)]): c for c in range(NCH)}
HT_AT = {i + 1: c for i, c in T_AFTER.items()}

SCAT_AFTER = {1: 0, 3: 1}
ACC_AT = {2: 0, 4: 1}
ST_AFTER = 8
ST_AT = 9
S_AT = 11
GATHER_AFTER = {14: 0, 17: 1}
XG_AT = FFP - 2

CHANW = TAPS * CT + 4 * CT
PARW = CHANW + 2 * NH


class Steps:

    def __init__(self, eng, sem):
        self.eng, self.sem, self.base, self.k = eng, sem, 0, 0

    def link(self, ins):
        self.k += 1
        ins.then_inc(self.sem, 1)
        self.eng.wait_ge(self.sem, self.base + self.k)


def build(nc, W, x_d, par_d, wbd_d, gb_d, cst_d, rt_d, out_d):
    with ExitStack() as ctx:
        def sb(name, shape, dt=F32):
            return ctx.enter_context(nc.sbuf_tensor(name, shape, dt))

        def sem(name):
            return ctx.enter_context(nc.semaphore(name))

        raw = sb("raw", [P, RING, PW])
        whi = sb("whi", [P, SPLIT, PW], F32R)
        wlo = sb("wlo", [P, SPLIT, PW], F32R)
        x = sb("x", [P, NT, D])
        ah = sb("ah", [P, KT * T], F32R)
        al = sb("al", [P, KT * T], F32R)
        hth = sb("hth", [P, NT, FC], F32R)
        htl = sb("htl", [P, NT, FC], F32R)
        scr = sb("scr", [P, 10384])
        ident = sb("ident", [P, P])
        par = sb("par", [P, DEPTH, PARW])
        cs = sb("cs", [P, NT, 2, ROT])
        nsp = sb("nsp", [P, 5, CT])
        nb = sb("nb", [P, 2, CT])
        sm = sb("sm", [P, 3, 16])
        bnst = sb("bnst", [P, NT, 2, 6])
        mv = sb("mv", [P, NT, 2])
        rstd = sb("rstd", [P, NT])
        njob_i = sb("njob_i", [P, 1], I32)

        xTh = ah[:, :].rearrange("p (k t) -> p k t", k=KT)
        xTl = al[:, :].rearrange("p (k t) -> p k t", k=KT)
        xgh = ah[:, 0:KT * P].rearrange("p (k s) -> p k s", k=KT)
        xgl = al[:, 0:KT * P].rearrange("p (k s) -> p k s", k=KT)

        def region(first, n, pat=None, **kw):
            r = scr[:, first:first + n]
            return r.rearrange(pat, **kw) if pat else r
        wbd = region(0, 1024, pat="p (g c n) -> p g c n", g=2, c=CT)
        avec = region(0, 1024, pat="p (c t) -> p c t", c=CT)
        up = region(1024, 1040, pat="p (c t) -> p c t", c=CT)
        tmp = region(1024, 1024, pat="p (c t) -> p c t", c=CT)
        uc = region(2064, 1024, pat="p (c t) -> p c t", c=CT)
        ri = region(3088, 2048, pat="p (g c t) -> p g c t", g=2, c=CT)
        pt = region(3088, 2048, pat="p (b r q) -> p b r q", b=4, r=4)
        gel = region(5136, 1024, pat="p (c t) -> p c t", c=CT)
        qkv = region(6160, 1536, pat="p (t n) -> p t n", t=NT)
        kd = region(7696, 512, pat="p (t g n) -> p t g n", t=NT, g=NKV)
        pr = region(6160, 2048, pat="p (b r k) -> p b r k", b=4, r=4)
        gb = region(6160, 2048, pat="p (a n) -> p a n", a=2)
        qT = region(8208, 1024, pat="p (r t) -> p r t", r=4)
        ropa = region(8208, 320, pat="p (t h n) -> p t h n", t=NT, h=10)
        ropb = region(8528, 320, pat="p (t h n) -> p t h n", t=NT, h=10)
        kT = region(9232, 640, pat="p (g t) -> p g t", g=NKV)
        vo = region(9872, 256, pat="p (t n) -> p t n", t=NT)
        ve = region(10128, 256, pat="p (t n) -> p t n", t=NT)
        hs = region(0, NT * FC, pat="p (t n) -> p t n", t=NT)
        acc = region(0, 2048, pat="p (t n) -> p t n", t=NT)
        ysb = region(2048, 1024)
        S = region(3072, 256, pat="p (t n) -> p t n", t=NT)
        ST = region(3328, 256, pat="p (t n) -> p t n", t=NT)
        he = region(3584, 256)
        tri = region(3840, 128)
        ones = region(3968, 128)
        iota = region(4096, 128)
        rw = region(4224, 64, pat="p (k e) -> p k e", k=KT)
        rb = region(4288, 8)
        lg = region(4304, 16, pat="p (t e) -> p t e", t=NT)
        mx8 = region(4320, 16, pat="p (t e) -> p t e", t=NT)
        ix8 = region(4336, 16, pat="p (t e) -> p t e", t=NT)
        ixf = region(4352, 16, pat="p (t e) -> p t e", t=NT)
        oh = region(4368, 32, pat="p (a t e) -> p a t e", a=2, t=NT)
        mk = region(4400, 16, pat="p (t e) -> p t e", t=NT)
        tw = region(4416, 8, pat="p (a t) -> p a t", a=4)
        wt = region(4432, 2 * 18, pat="p (t e) -> p t e", t=NT)
        ps_ = region(4480, 2 * 18, pat="p (t e) -> p t e", t=NT)
        wc = region(4520, 2)
        pc = region(4522, 2)
        cnt = region(4528, 8)
        cm = region(4536, 2)
        RTW = 128 * 3 + 64 + 8
        rtab = region(3840, RTW)

        bank = ctx.enter_context(nc.psum_tensor("bank", [P, 8, 512], F32))

        raw_in = [sem(f"raw_in{s}") for s in range(RING)]
        hi_rdy = sem("hi_rdy")
        lo_rdy = sem("lo_rdy")
        used = sem("piece_used")
        x_in = sem("x_in")
        par_in = sem("par_in")
        wbd_in = sem("wbd_in")
        gb_in = sem("gb_in")
        rt_in = sem("rt_in")
        x_rdy = sem("x_rdy")
        xT_ps = sem("xT_ps")
        xTh_rdy = sem("xTh_rdy")
        xTl_rdy = sem("xTl_rdy")
        u_sb = sem("u_sb")
        uc_rdy = sem("uc_rdy")
        qkv_sb = sem("qkv_sb")
        gate_ps = sem("gate_ps")
        gate_e = sem("gate_e")
        gelu_rdy = sem("gelu_rdy")
        nsp_e = sem("nsp_e")
        nsp_rdy = sem("nsp_rdy")
        rope_rdy = sem("rope_rdy")
        qT_ps = sem("qT_ps")
        qT_sb = sem("qT_sb")
        ri_rdy = sem("ri_rdy")
        at_rdy = sem("at_rdy")
        v_rdy = sem("v_rdy")
        sq_rdy = sem("sq_rdy")
        ylru_rdy = sem("ylru_rdy")
        yh_rdy = sem("yh_rdy")
        yl_rdy = sem("yl_rdy")
        s_ps = sem("s_ps")
        s_sub = sem("s_sub")
        s_exp = sem("s_exp")
        p_rdy = sem("p_rdy")
        pt_ps = sem("pt_ps")
        pt_sb = sem("pt_sb")
        o_ps = sem("o_ps")
        var_rdy = sem("var_rdy")
        std_rdy = sem("std_rdy")
        gb_used = sem("gb_used")
        silu_rdy = sem("silu_rdy")
        h_rdy = sem("h_rdy")
        hT_ps = sem("hT_ps")
        hTh_rdy = sem("hTh_rdy")
        hTl_rdy = sem("hTl_rdy")
        lg_ps = sem("lg_ps")
        tw_in = sem("tw_in")
        tw_e = sem("tw_e")
        mk_rdy = sem("mk_rdy")
        pos_ps = sem("pos_ps")
        tab_rdy = sem("tab_rdy")
        S_rdy = sem("S_rdy")
        xg_ps = sem("xg_ps")
        xgh_rdy = sem("xgh_rdy")
        xgl_rdy = sem("xgl_rdy")
        st_ps = sem("st_ps")
        st_sb = sem("st_sb")
        y_sb = sem("y_sb")
        sc_ps = sem("sc_ps")
        acc_rdy = sem("acc_rdy")
        dve_step = sem("dve_step")
        dve_tail = sem("dve_tail")
        out_done = sem("out_done")

        block = ctx.enter_context(nc.Block())

        def xbank(t, g):
            return 6 * t + g

        @block.sync
        def _(sp):
            for t in range(NT):
                sp.dma_start(x[:, t, :], x_d[t]).then_inc(x_in, 16)
            sp.dma_start(ident[:], cst_d[:, 0:P]).then_inc(par_in, 16)
            for s in range(RING):
                sp.dma_start(raw[:, s, :], W[s]).then_inc(raw_in[s], 16)
                if s == 0:
                    sp.dma_start(par[:], par_d).then_inc(par_in, 16)
                    sp.dma_start(cs[:], cst_d[:, P:P + 64].rearrange("p (t a n) -> p t a n", t=NT, a=2)).then_inc(par_in, 16)
            rounds = NPIECE // RING
            with sp.Fori(1, rounds) as r:
                for s in range(RING):
                    sp.wait_ge(lo_rdy, r * RING + (s + 1 - RING))
                    sp.dma_start(raw[:, s, :], W[bass.ds(r * RING + s, 1)].rearrange("a p n -> (a p) n")
                                 ).then_inc(raw_in[s], 16)
            sp.wait_ge(tab_rdy, 1)
            njob = sp.value_load(njob_i[0:1, 0:1], min_val=NE, max_val=2 * NE)
            with sp.If(njob > NE):
                with sp.Fori(rounds, njob * (FFP // RING) + STREAM // RING) as r:
                    for s in range(RING):
                        sp.wait_ge(lo_rdy, r * RING + (s + 1 - RING))
                        sp.dma_start(raw[:, s, :],
                                     W[bass.ds(r * RING + (s - NE * FFP), 1)].rearrange("a p n -> (a p) n")
                                     ).then_inc(raw_in[s], 16)
            for s in range(2):
                sp.wait_ge(lo_rdy, njob * FFP + (STREAM + s + 1 - RING))
                sp.dma_start(raw[:, s, :], W[STREAM + s]).then_inc(raw_in[s], 16)
            for t in range(NT):
                sp.wait_ge(x_rdy, 2 * DEPTH * NT - NT + t + 1)
                sp.dma_start(out_d[t], x[:, t, :]).then_inc(out_done, 16)
            sp.wait_ge(out_done, 16 * NT)

        @block.gpsimd
        def _(pool):
            for l in range(DEPTH):
                if l:
                    pool.wait_ge(ylru_rdy, l)
                    pool.wait_ge(x_rdy, 2 * l * NT)
                pool.dma_start(scr[:, 0:1024], wbd_d[l]).then_inc(wbd_in, 16)
                pool.wait_ge(pt_ps, 4 * (l + 1))
                pool.dma_start(scr[:, 6160:6160 + 2048], gb_d[2 * l]).then_inc(gb_in, 16)
                pool.wait_ge(gb_used, 2 * l + 1)
                pool.dma_start(scr[:, 6160:6160 + 2048], gb_d[2 * l + 1]).then_inc(gb_in, 16)
                if l == DEPTH - 1:
                    pool.dma_start(rtab, rt_d).then_inc(rt_in, 16)

        @block.tensor
        def _(pe):
            def piece(p):
                pe.wait_ge(lo_rdy, p + 1)

            def transpose_x(ph):
                for t in range(NT):
                    if ph == 0:
                        if t == 0:
                            pe.wait_ge(x_in, 16 * NT)
                            pe.wait_ge(par_in, 48)
                    else:
                        pe.wait_ge(x_rdy, NT * (ph - 1) + t + 1)
                    for g in range(2):
                        for k in range(4):
                            last = nc.tensor.transpose(bank[:, xbank(t, g), k * P:(k + 1) * P],
                                                       x[:, t, (4 * g + k) * P:(4 * g + k + 1) * P], ident[:])
                        last.then_inc(xT_ps, 1)

            def three(out, sh, sl, mh, ml, first, last):
                nc.tensor.matmul(out, sh, mh, start=first, stop=False, skip_group_check=True)
                nc.tensor.matmul(out, sh, ml, start=False, stop=False, skip_group_check=True)
                return nc.tensor.matmul(out, sl, mh, start=False, stop=last, skip_group_check=True)

            def mixer(l):
                p0 = l * (MIXP + FFP)
                transpose_x(2 * l)
                pe.wait_ge(xTl_rdy, 4 * (2 * l + 1))

                def wslot(p):
                    s = p % SPLIT
                    return (whi[:, s, :].rearrange("p (k n) -> p k n", k=KT),
                            wlo[:, s, :].rearrange("p (k n) -> p k n", k=KT))

                def channels(p, b):
                    piece(p)
                    wh, wl = wslot(p)
                    for c in range(2):
                        for k in range(KT):
                            last = three(bank[:, b, c * T:(c + 1) * T], wh[:, k, c * P:(c + 1) * P],
                                         wl[:, k, c * P:(c + 1) * P], xTh[:, k, :], xTl[:, k, :], k == 0, k == KT - 1)
                    last.then_inc(used, 1)

                def rows(p, b):
                    piece(p)
                    wh, wl = wslot(p)
                    for t in range(NT):
                        for k in range(KT):
                            last = three(bank[:, b, t * 256:(t + 1) * 256], xTh[:, k, t * P:(t + 1) * P],
                                         xTl[:, k, t * P:(t + 1) * P], wh[:, k, :], wl[:, k, :], k == 0, k == KT - 1)
                    last.then_inc(used, 1)

                channels(p0, 0)
                channels(p0 + 1, 1)
                rows(p0 + 2, 2)
                rows(p0 + 3, 3)
                rows(p0 + 4, 4)
                pe.wait_ge(wbd_in, 16 * (l + 1))
                pe.wait_ge(qkv_sb, 3 * l + 1)
                for cp in range(2):
                    pe.wait_ge(uc_rdy, CT * l + 2 * cp + 2)
                    for g in range(2):
                        b = cp if g == 0 else (7, 2)[cp]
                        for c in range(2):
                            last = nc.tensor.matmul(bank[:, b, c * T:(c + 1) * T], wbd[:, g, 2 * cp + c, :],
                                                    uc[:, 2 * cp + c, :], start=True, stop=True)
                        last.then_inc(gate_ps, 1)
                channels(p0 + 5, 5)
                channels(p0 + 6, 6)
                pe.wait_ge(rope_rdy, l + 1)
                for b in range(2):
                    for r in range(2):
                        for t in range(NT):
                            last = nc.tensor.transpose(bank[:, 3 + b, r * T + t * P:r * T + (t + 1) * P],
                                                       qkv[:, t, (2 * b + r) * P:(2 * b + r + 1) * P], ident[:])
                    last.then_inc(qT_ps, 1)
                pe.wait_ge(gelu_rdy, 2 * l + 1)
                for g in range(NKV):
                    for t in range(NT):
                        last = nc.tensor.transpose(bank[:, 5, g * T + t * P:g * T + (t + 1) * P],
                                                   kd[:, t, g, :], ident[:])
                last.then_inc(qT_ps, 1)
                pe.wait_ge(gate_e, 4 * (l + 1))
                pe.wait_ge(qT_sb, 3 * (l + 1))
                for b in range(4):
                    t, s = b // 2, b % 2
                    d0 = s * HD
                    for r in range(4):
                        g = r // 2
                        q = 2 * t
                        o = (0, 1, 2, 7)[b]
                        dst = bank[:, o, r * P:(r + 1) * P]
                        nc.tensor.matmul(dst[0:64, 0:64], qT[d0:d0 + HD, r, q * CH:(q + 1) * CH],
                                         kT[d0:d0 + HD, g, (q + 1) * CH:(q + 2) * CH],
                                         start=True, stop=True)
                        if t:
                            nc.tensor.matmul(dst[0:64, 64:128], qT[d0:d0 + HD, r, q * CH:(q + 1) * CH],
                                             kT[d0:d0 + HD, g, q * CH:(q + 1) * CH],
                                             start=True, stop=True)
                        last = nc.tensor.matmul(dst[64:128, :], qT[d0:d0 + HD, r, (q + 1) * CH:(q + 2) * CH],
                                                kT[d0:d0 + HD, g, (q + 1) * CH:(q + 3) * CH],
                                                start=True, stop=True)
                    last.then_inc(s_ps, 1)
                pe.wait_ge(gelu_rdy, 2 * l + 2)
                for b in range(4):
                    pe.wait_ge(p_rdy, 4 * l + b + 1)
                    for r in range(4):
                        last = nc.tensor.transpose(bank[:, 3 + b, r * P:(r + 1) * P], pr[:, b, r, :], ident[:])
                    last.then_inc(pt_ps, 1)
                pe.wait_ge(pt_sb, 4 * (l + 1))
                for g in range(NKV):
                    for s in range(2):
                        for t in range(NT):
                            for half, v in ((0, ve), (1, vo)):
                                dst = bank[s * HD:(s + 1) * HD, g, :].rearrange("p (r t) -> p r t", r=2)
                                c0 = t * P + half * CH
                                last = nc.tensor.matmul(dst[:, :, c0:c0 + CH], v[:, t, g * HD:(g + 1) * HD],
                                                        pt[:, 2 * t + s, 2 * g:2 * g + 2, half * CH:(half + 1) * CH],
                                                        start=True, stop=True)
                    last.then_inc(o_ps, 1)
                for j in range(4):
                    p = p0 + 7 + j
                    if j == 0:
                        pe.wait_ge(yl_rdy, 3 * l + 1)
                    if j == 2:
                        pe.wait_ge(yl_rdy, 3 * l + 2)
                    if j == 3:
                        pe.wait_ge(yl_rdy, 3 * l + 3)
                    piece(p)
                    down(p, xTh, xTl, 2 * j, j == 0, j == 3, NT)

            def down(p, th, tl, k0, first, last_piece, nt):
                wh = whi[:, p % SPLIT, :].rearrange("p (k n) -> p k n", k=2)
                wl = wlo[:, p % SPLIT, :].rearrange("p (k n) -> p k n", k=2)
                downmm(wh, wl, th, tl, k0, first, last_piece, nt)

            def downmm(wh, wl, th, tl, k0, first, last_piece, nt):
                for t in range(nt):
                    for k in range(2):
                        sh = th[:, k0 + k, t * P:(t + 1) * P] if th is xTh else th[:, t, k * P:(k + 1) * P]
                        sl = tl[:, k0 + k, t * P:(t + 1) * P] if tl is xTl else tl[:, t, k * P:(k + 1) * P]
                        st, en = first and k == 0, last_piece and k == 1
                        dst = [bank[:, 2 + 2 * t + n, :] for n in range(2)]
                        for n in range(2):
                            nc.tensor.matmul(dst[n], sh, wh[:, k, n * 512:(n + 1) * 512], start=st, stop=False,
                                             skip_group_check=True)
                        for n in range(2):
                            nc.tensor.matmul(dst[n], sh, wl[:, k, n * 512:(n + 1) * 512], start=False, stop=False,
                                             skip_group_check=True)
                        for n in range(2):
                            last = nc.tensor.matmul(dst[n], sl, wh[:, k, n * 512:(n + 1) * 512], start=False, stop=en,
                                                    skip_group_check=True)
                last.then_inc(used, 1)

            def gate_up(slot, half, th, tl, nt):
                wh = whi[:, slot, :].rearrange("p (k n) -> p k n", k=4)
                wl = wlo[:, slot, :].rearrange("p (k n) -> p k n", k=4)
                for t in range(nt):
                    for k in range(4):
                        kk = 4 * half + k
                        last = three(bank[:, t, :], th[:, kk, t * P:(t + 1) * P], tl[:, kk, t * P:(t + 1) * P],
                                     wh[:, k, :], wl[:, k, :], kk == 0, kk == KT - 1)
                last.then_inc(used, 1)

            def transpose_h(src, nt):
                for t in range(nt):
                    for k in range(2):
                        last = nc.tensor.transpose(bank[:, 6 + t, k * P:(k + 1) * P], src(t, k), ident[:])
                last.then_inc(hT_ps, 1)

            def dense():
                transpose_x(1)
                pe.wait_ge(xTl_rdy, 8)
                for i, (kind, c) in enumerate(FFORDER):
                    p = MIXP + i
                    piece(p)
                    if kind == "A" and c:
                        pe.wait_ge(h_rdy, c)
                    if kind == "D":
                        pe.wait_ge(hTl_rdy, c + 1)
                        down(p, hth, htl, 0, c == 0, c == NCH - 1, NT)
                    else:
                        gate_up(p % SPLIT, "AB".index(kind), xTh, xTl, NT)
                    if i in T_AFTER:
                        pe.wait_ge(h_rdy, T_AFTER[i] + 1)
                        if T_AFTER[i]:
                            pe.wait_ge(hTl_rdy, T_AFTER[i])
                        transpose_h(lambda t, k: hs[:, t, k * P:(k + 1) * P], NT)

            def gather(b):
                for k in range(4):
                    for t in range(NT):
                        kk = 4 * b + k
                        last = nc.tensor.matmul(bank[:, 4 + b, k * P:(k + 1) * P], x[:, t, kk * P:(kk + 1) * P],
                                                S[:, t, :], start=(t == 0), stop=(t == 1))
                last.then_inc(xg_ps, 1)

            def scatter(t):
                for n, b in ((0, 7), (1, 1)):
                    last = nc.tensor.matmul(bank[:, b, :], ST[:, t, :], ysb[:, n * 512:(n + 1) * 512],
                                            start=True, stop=True)
                last.then_inc(sc_ps, 1)

            def router():
                transpose_x(3)
                pe.wait_ge(xTl_rdy, 16)
                pe.wait_ge(rt_in, 16)
                for t in range(NT):
                    for k in range(KT):
                        for n, a in enumerate((xTh, xTl)):
                            last = nc.tensor.matmul(bank[:, 2, t * NE:(t + 1) * NE],
                                                    a[:, k, t * P:(t + 1) * P].bitcast(F32), rw[:, k, :],
                                                    start=(k == 0 and n == 0), stop=(k == KT - 1 and n == 1))
                last.then_inc(lg_ps, 1)
                pe.wait_ge(mk_rdy, 1)
                nc.tensor.matmul(bank[:, 3, 0:NE], tri, mk[:, 0, :], start=True, stop=True)
                nc.tensor.matmul(bank[:, 3, NE:2 * NE], ones, mk[:, 0, :], start=True, stop=False)
                nc.tensor.matmul(bank[:, 3, NE:2 * NE], tri, mk[:, 1, :], start=False, stop=True)
                nc.tensor.matmul(bank[:, 3, 2 * NE:3 * NE], ones, mk[:, 0, :], start=True, stop=False)
                nc.tensor.matmul(bank[:, 3, 2 * NE:3 * NE], ones, mk[:, 1, :], start=False,
                                 stop=True).then_inc(pos_ps, 1)

            mixer(0)
            dense()
            mixer(1)
            router()
            pe.wait_ge(S_rdy, 1)
            gather(0)
            gather(1)
            pe.wait_ge(tab_rdy, 1)
            njob = pe.value_load(njob_i[0:1, 0:1], min_val=NE, max_val=2 * NE)
            hb = NCH
            with pe.Fori(0, njob) as j:
                pe.wait_ge(xgl_rdy, j + 1)
                for i, (kind, c) in enumerate(FFORDER):
                    slot = (STREAM + i) % SPLIT
                    pe.wait_ge(lo_rdy, j * FFP + (STREAM + i + 1))
                    if kind == "A" and c:
                        pe.wait_ge(h_rdy, j * NCH + (hb + c))
                    if kind == "D":
                        if c == 0:
                            pe.wait_ge(y_sb, j + 1)
                        pe.wait_ge(hTl_rdy, j * NCH + (hb + c + 1))
                        downmm(whi[:, slot, :].rearrange("p (k n) -> p k n", k=2),
                               wlo[:, slot, :].rearrange("p (k n) -> p k n", k=2),
                               hth, htl, 0, c == 0, c == NCH - 1, 1)
                    else:
                        gate_up(slot, "AB".index(kind), xgh, xgl, 1)
                    if i in SCAT_AFTER:
                        t = SCAT_AFTER[i]
                        if t == 0:
                            pe.wait_ge(y_sb, j + 1)
                            pe.wait_ge(st_sb, j + 1)
                        else:
                            pe.wait_ge(acc_rdy, j * NT + 1)
                        scatter(t)
                    if i in T_AFTER:
                        pe.wait_ge(h_rdy, j * NCH + (hb + T_AFTER[i] + 1))
                        pe.wait_ge(hTl_rdy, j * NCH + (hb + T_AFTER[i]))
                        transpose_h(lambda t, k: he[:, k * P:(k + 1) * P], 1)
                    if i == ST_AFTER:
                        pe.wait_ge(acc_rdy, j * NT + 2)
                        for t in range(NT):
                            last = nc.tensor.transpose(bank[:, 7, t * P:(t + 1) * P], S[:, t, :], ident[:])
                        last.then_inc(st_ps, 1)
                    if i in GATHER_AFTER:
                        pe.wait_ge(S_rdy, j + 2)
                        gather(GATHER_AFTER[i])
            pe.wait_ge(y_sb, njob + 1)
            pe.wait_ge(st_sb, njob + 1)
            scatter(0)
            pe.wait_ge(acc_rdy, njob * NT + 1)
            scatter(1)

        @block.scalar
        def _(act):
            def hi(p):
                act.wait_ge(raw_in[p % RING], 16 * (p // RING + 1))
                if p >= SPLIT:
                    act.wait_ge(used, p - SPLIT + 1)
                nc.scalar.activation(whi[:, p % SPLIT, :], raw[:, p % RING, :], ACT.Copy).then_inc(hi_rdy, 1)

            def split_x(ph):
                for n in range(4):
                    t, g = n // 2, n % 2
                    act.wait_ge(xT_ps, 4 * ph + n + 1)
                    nc.scalar.activation(xTh[:, 4 * g:4 * g + 4, t * P:(t + 1) * P],
                                         bank[:, xbank(t, g), :].rearrange("p (k t) -> p k t", k=4),
                                         ACT.Copy).then_inc(xTh_rdy, 1)

            def std(ph):
                for t in range(NT):
                    act.wait_ge(var_rdy, NT * ph + t + 1)
                    nc.scalar.activation(rstd[:, t:t + 1], mv[:, t, 1:2], ACT.Sqrt).then_inc(std_rdy, 1)

            def mixer(l):
                p0 = l * (MIXP + FFP)
                hi(p0 + 2)
                split_x(2 * l)
                act.wait_ge(par_in, 48)
                act.wait_ge(nsp_rdy, 2 * l + 1)
                nc.scalar.activation(nsp[:, 2, :], nsp[:, 1, :], ACT.Exp, scale=-1.0).then_inc(nsp_e, 1)
                for j in range(2):
                    act.wait_ge(used, p0 + j + 1)
                    nc.scalar.activation(up[:, 2 * j:2 * j + 2, TAPS:TAPS + T],
                                         bank[:, j, :].rearrange("p (c t) -> p c t", c=2), ACT.Copy).then_inc(u_sb, 1)
                    hi(p0 + 3 + j)
                for j in range(3):
                    act.wait_ge(used, p0 + 3 + j)
                    nc.scalar.activation(qkv[:, :, j * 256:(j + 1) * 256],
                                         bank[:, 2 + j, :].rearrange("p (t n) -> p t n", t=NT),
                                         ACT.Copy).then_inc(qkv_sb, 1)
                    hi(p0 + 5 + j)
                act.wait_ge(nsp_rdy, 2 * l + 1)
                for cp in range(2):
                    for g in range(2):
                        b = cp if g == 0 else (7, 2)[cp]
                        act.wait_ge(gate_ps, 4 * l + 2 * cp + g + 1)
                        for c in range(2):
                            last = nc.scalar.activation(ri[:, g, 2 * cp + c, :], bank[:, b, c * T:(c + 1) * T], ACT.Exp,
                                                        bias=nb[:, g, 2 * cp + c:2 * cp + c + 1], scale=-1.0)
                        last.then_inc(gate_e, 1)
                for j in range(2):
                    act.wait_ge(used, p0 + 6 + j)
                    nc.scalar.activation(gel[:, 2 * j:2 * j + 2, :],
                                         bank[:, 5 + j, :].rearrange("p (c t) -> p c t", c=2),
                                         ACT.Gelu_apprx_tanh).then_inc(gelu_rdy, 1)
                    hi(p0 + 8 + j)
                for b in range(2):
                    act.wait_ge(qT_ps, 3 * l + b + 1)
                    nc.scalar.activation(qT[:, 2 * b:2 * b + 2, :], bank[:, 3 + b, :].rearrange("p (r t) -> p r t", r=2),
                                         ACT.Copy).then_inc(qT_sb, 1)
                act.wait_ge(qT_ps, 3 * l + 3)
                nc.scalar.activation(kT[:, :, CH:CH + T], bank[:, 5, :].rearrange("p (g t) -> p g t", g=NKV),
                                     ACT.Copy).then_inc(qT_sb, 1)
                act.wait_ge(ri_rdy, l + 1)
                act.wait_ge(nsp_rdy, 2 * l + 2)
                for c in range(CT):
                    nc.scalar.activation(avec[:, c, :], ri[:, 0, c, :], ACT.Exp, scale=nsp[:, 0, c:c + 1])
                for c in range(CT):
                    last = nc.scalar.activation(tmp[:, c, :], ri[:, 0, c, :], ACT.Tanh, scale=nsp[:, 1, c:c + 1])
                last.then_inc(at_rdy, 1)
                act.wait_ge(v_rdy, l + 1)
                nc.scalar.activation(ri[:, 0], tmp[:], ACT.Sqrt, scale=2.0).then_inc(sq_rdy, 1)
                for b in range(4):
                    act.wait_ge(s_sub, 5 * l + b + 1)
                    nc.scalar.activation(pr[:, b], pr[:, b], ACT.Exp).then_inc(s_exp, 1)
                act.wait_ge(s_sub, 5 * l + 5)
                nc.scalar.activation(sm[:, 2, :], sm[:, 2, :], ACT.Exp).then_inc(s_exp, 1)
                act.wait_ge(ylru_rdy, l + 1)
                act.wait_ge(used, p0 + 7)
                nc.scalar.activation(ah[:, 0:CT * T], tmp[:].rearrange("p c t -> p (c t)"), ACT.Copy).then_inc(yh_rdy, 1)
                for b in range(4):
                    act.wait_ge(pt_ps, 4 * l + b + 1)
                    nc.scalar.activation(pt[:, b], bank[:, 3 + b, :].rearrange("p (r q) -> p r q", r=4),
                                         ACT.Copy).then_inc(pt_sb, 1)
                for g in range(2):
                    act.wait_ge(o_ps, 2 * l + g + 1)
                    nc.scalar.activation(xTh[:, 4 + 2 * g:6 + 2 * g, :],
                                         bank[:, g, :].rearrange("p (r t) -> p r t", r=2), ACT.Copy).then_inc(yh_rdy, 1)
                for j in range(3):
                    hi(p0 + 10 + j)
                std(2 * l)

            def dense():
                split_x(1)
                for i in range(FFP):
                    if i in H_AT:
                        c = H_AT[i]
                        act.wait_ge(used, MIXP + STEP[("B", c)] + 1)
                        if c:
                            act.wait_ge(hT_ps, c)
                        for t in range(NT):
                            nc.scalar.activation(hs[:, t, :], bank[:, t, 0:FC], ACT.Silu).then_inc(silu_rdy, 1)
                    if i in HT_AT:
                        c = HT_AT[i]
                        act.wait_ge(hT_ps, c + 1)
                        if c:
                            act.wait_ge(used, MIXP + STEP[("D", c - 1)] + 1)
                        nc.scalar.activation(hth[:], bank[:, 6:8, 0:FC], ACT.Copy).then_inc(hTh_rdy, 1)
                    hi(MIXP + i + 2)
                std(1)

            hi(0)
            hi(1)
            mixer(0)
            dense()
            mixer(1)
            split_x(3)
            act.wait_ge(tw_in, 1)
            nc.scalar.activation(tw[:, 1, :], tw[:, 0, :], ACT.Exp).then_inc(tw_e, 1)

            def split_rows(j):
                act.wait_ge(xg_ps, 2 * j + 2)
                nc.scalar.activation(xgh, bank[:, 4:6, :].rearrange("p b (k s) -> p (b k) s", k=4),
                                     ACT.Copy).then_inc(xgh_rdy, 1)

            split_rows(0)
            act.wait_ge(tab_rdy, 1)
            njob = act.value_load(njob_i[0:1, 0:1], min_val=NE, max_val=2 * NE)
            hb = NCH
            with act.Fori(0, njob) as j:
                for i in range(FFP):
                    if i == 0:
                        act.wait_ge(used, j * FFP + STREAM)
                        nc.scalar.activation(ysb, bank[:, 2:4, :].rearrange("p b n -> p (b n)"),
                                             ACT.Copy).then_inc(y_sb, 1)
                    if i in H_AT:
                        c = H_AT[i]
                        act.wait_ge(used, j * FFP + (STREAM + STEP[("B", c)] + 1))
                        act.wait_ge(hT_ps, j * NCH + (hb + c))
                        nc.scalar.activation(he, bank[:, 0, 0:FC], ACT.Silu).then_inc(silu_rdy, 1)
                    if i in HT_AT:
                        c = HT_AT[i]
                        act.wait_ge(hT_ps, j * NCH + (hb + c + 1))
                        nc.scalar.activation(hth[:, 0, :], bank[:, 6, 0:FC], ACT.Copy).then_inc(hTh_rdy, 1)
                    if i == ST_AT:
                        act.wait_ge(st_ps, j + 1)
                        nc.scalar.activation(ST, bank[:, 7, 0:2 * P].rearrange("p (t n) -> p t n", t=NT),
                                             ACT.Copy).then_inc(st_sb, 1)
                    if i == XG_AT:
                        split_rows(j + 1)
                    q = STREAM + i + 2
                    act.wait_ge(raw_in[q % RING], j * (16 * FFP // RING) + 16 * (q // RING + 1))
                    act.wait_ge(used, j * FFP + (q - SPLIT + 1))
                    nc.scalar.activation(whi[:, q % SPLIT, :], raw[:, q % RING, :], ACT.Copy).then_inc(hi_rdy, 1)
            act.wait_ge(used, njob * FFP + STREAM)
            nc.scalar.activation(ysb, bank[:, 2:4, :].rearrange("p b n -> p (b n)"), ACT.Copy).then_inc(y_sb, 1)
            std(3)

        @block.vector
        def _(dve):
            chain = Steps(dve, dve_step)
            link = chain.link
            V = nc.vector

            def lo(p):
                dve.wait_ge(hi_rdy, p + 1)
                V.tensor_tensor(wlo[:, p % SPLIT, :], raw[:, p % RING, :], whi[:, p % SPLIT, :].bitcast(F32),
                                ALU.subtract).then_inc(lo_rdy, 1)

            def split_x(ph):
                for n in range(4):
                    t, g = n // 2, n % 2
                    dve.wait_ge(xTh_rdy, 4 * ph + n + 1)
                    V.tensor_tensor(xTl[:, 4 * g:4 * g + 4, t * P:(t + 1) * P],
                                    bank[:, xbank(t, g), :].rearrange("p (k t) -> p k t", k=4),
                                    xTh[:, 4 * g:4 * g + 4, t * P:(t + 1) * P].bitcast(F32),
                                    ALU.subtract).then_inc(xTl_rdy, 1)

            def norm(ph, last_piece, from_acc=False):
                if last_piece is not None:
                    dve.wait_ge(used, last_piece)
                for t in range(NT):
                    src = acc if from_acc else x
                    for n in range(2):
                        sl = x[:, t, n * 512:(n + 1) * 512]
                        if not from_acc:
                            link(V.scalar_tensor_tensor(sl, sl, ALPHA, bank[:, 2 + 2 * t + n, :], ALU.mult, ALU.add))
                        V.bn_stats(bnst[:, t, n, :], src[:, t, n * 512:(n + 1) * 512]).then_inc(chain.sem, 1)
                        chain.k += 1
                    dve.wait_ge(chain.sem, chain.base + chain.k)
                    link(V.bn_aggr(mv[:, t, :], bnst[:, t].rearrange("p a b -> p (a b)")))
                    V.tensor_scalar_add(mv[:, t, 1:2], mv[:, t, 1:2], EPS).then_inc(var_rdy, 1)
                dve.wait_ge(gb_in, 16 * (ph + 1))
                for t in range(NT):
                    src = acc if from_acc else x
                    dve.wait_ge(std_rdy, NT * ph + t + 1)
                    link(V.reciprocal(rstd[:, t:t + 1], rstd[:, t:t + 1]))
                    link(V.tensor_scalar(x[:, t, :], src[:, t, :], mv[:, t, 0:1], rstd[:, t:t + 1], ALU.subtract, ALU.mult))
                    link(V.tensor_tensor(x[:, t, :], x[:, t, :], gb[:, 0, :], ALU.mult))
                    V.tensor_tensor(x[:, t, :], x[:, t, :], gb[:, 1, :], ALU.add).then_inc(x_rdy, 1)
                dve.wait_ge(x_rdy, NT * (ph + 1))
                V.memset(rstd[:, 0:1], 0.0).then_inc(gb_used, 1)

            def mixer(l):
                p0 = l * (MIXP + FFP)
                pl = par[:, l, :]
                if l == 0:
                    dve.wait_ge(par_in, 48)
                lam = pl[:, TAPS * CT + 3 * CT:TAPS * CT + 4 * CT]
                bias = pl[:, TAPS * CT + CT:TAPS * CT + 3 * CT].rearrange("p (g c) -> p g c", g=2)
                link(V.tensor_scalar(nb[:], bias, -1.0, None, ALU.mult))
                link(V.tensor_scalar(nsp[:, 0, :], lam, -1.0, None, ALU.mult))
                V.tensor_tensor(nsp[:, 1, :], nsp[:, 0, :], lam, ALU.max).then_inc(nsp_rdy, 1)
                V.memset(up[:, :, 0:TAPS], 0.0).then_inc(chain.sem, 1)
                V.memset(kT[:, :, 0:CH], 0.0).then_inc(chain.sem, 1)
                V.memset(ve[CH:P, 0, :], 0.0).then_inc(chain.sem, 1)
                chain.k += 3
                lo(p0 + 2)
                split_x(2 * l)
                dve.wait_ge(nsp_e, l + 1)
                y, s, s2, q = nsp[:, 2, :], nsp[:, 3, :], nsp[:, 4, :], nsp[:, 1, :]
                link(V.tensor_scalar(s2, y, 2.0, None, ALU.add))
                link(V.reciprocal(s2, s2))
                link(V.tensor_tensor(s, y, s2, ALU.mult))
                link(V.tensor_tensor(s2, s, s, ALU.mult))
                link(V.tensor_scalar(q, s2, 1.0 / 17.0, 1.0 / 15.0, ALU.mult, ALU.add))
                for n in (13, 11, 9, 7, 5, 3, 1):
                    link(V.tensor_tensor(q, q, s2, ALU.mult))
                    link(V.tensor_scalar(q, q, 1.0 / n, None, ALU.add))
                link(V.tensor_tensor(q, q, s, ALU.mult))
                link(V.tensor_scalar(s, nsp[:, 0, :], 0.0, 8.0, ALU.max, ALU.mult))
                link(V.scalar_tensor_tensor(q, q, 16.0, s, ALU.mult, ALU.add))
                V.tensor_scalar(nsp[:, 0, :], q, -1.0, None, ALU.mult).then_inc(nsp_rdy, 1)
                for j in range(2):
                    dve.wait_ge(u_sb, 2 * l + j + 1)
                    for tap in range(TAPS):
                        for c in (2 * j, 2 * j + 1):
                            w = pl[:, tap * CT + c:tap * CT + c + 1]
                            src = up[:, c, 1 + tap:1 + tap + T]
                            if tap == 0:
                                V.tensor_scalar(uc[:, c, :], src, w, pl[:, TAPS * CT + c:TAPS * CT + c + 1],
                                                ALU.mult, ALU.add).then_inc(chain.sem, 1)
                                chain.k += 1
                            else:
                                dve.wait_ge(chain.sem, chain.base + chain.k - 1)
                                ins = V.scalar_tensor_tensor(uc[:, c, :], src, w, uc[:, c, :], ALU.mult, ALU.add)
                                if tap == TAPS - 1:
                                    ins.then_inc(uc_rdy, 1)
                                    if c % 2 == 0:
                                        dve.wait_ge(chain.sem, chain.base + chain.k)
                                else:
                                    ins.then_inc(chain.sem, 1)
                                    chain.k += 1
                    lo(p0 + 3 + j)
                lo(p0 + 5)
                lo(p0 + 6)
                lo(p0 + 7)
                dve.wait_ge(qkv_sb, 3 * (l + 1))
                heads = qkv[:, :, 0:10 * HD].rearrange("p t (h d) -> p t h d", h=10)
                for t in range(NT):
                    for a, dst in ((0, ropa), (1, ropb)):
                        tab = cs[:, t, a, :].unsqueeze(1).broadcast_to([P, 10, ROT])
                        link(V.tensor_tensor(dst[:, t], heads[:, t, :, 0:ROT], tab, ALU.mult))
                for t in range(NT):
                    link(V.tensor_tensor(heads[:, t, :, 0:8], ropa[:, t, :, 0:8], ropb[:, t, :, 8:16], ALU.subtract))
                    link(V.tensor_tensor(heads[:, t, :, 8:16], ropa[:, t, :, 8:16], ropb[:, t, :, 0:8], ALU.add))
                    for g in range(NKV):
                        src = qkv[:, t, 512 + g * HD:512 + (g + 1) * HD].unsqueeze(1).broadcast_to([P, 2, HD])
                        link(V.tensor_copy(kd[:, t, g, :].rearrange("p (a d) -> p a d", a=2), src))
                link(V.tensor_copy(vo[:], qkv[:, :, 640:768]))
                link(V.tensor_copy(ve[0:CH, :, :], qkv[0:CH, :, 640:768]))
                V.tensor_copy(ve[CH:P, 1, :], qkv[CH:P, 0, 640:768]).then_inc(rope_rdy, 1)
                dve.wait_ge(gate_e, 4 * (l + 1))
                link(V.tensor_scalar(ri[:], ri[:], 1.0, None, ALU.add))
                V.reciprocal(ri[:], ri[:]).then_inc(ri_rdy, 1)
                dve.wait_ge(ri_rdy, l + 1)
                link(V.tensor_tensor(ri[:, 1], ri[:, 1], uc[:], ALU.mult))
                lo(p0 + 8)
                lo(p0 + 9)
                dve.wait_ge(at_rdy, l + 1)
                link(V.tensor_scalar(ri[:, 0], tmp[:], 1.0, None, ALU.add))
                link(V.reciprocal(ri[:, 0], ri[:, 0]))
                V.tensor_tensor(tmp[:], tmp[:], ri[:, 0], ALU.mult).then_inc(v_rdy, 1)
                sink = pl[:, CHANW:CHANW + 16]
                for b in range(4):
                    o = (0, 1, 2, 7)[b]
                    sc = bank[:, o, :].rearrange("p (r k) -> p r k", r=4)
                    dve.wait_ge(s_ps, 4 * l + b + 1)
                    if b < 2:
                        link(V.memset(sc[0:CH, :, CH:P], -8.0e30))
                    m = sm[:, 0, 4 * b:4 * b + 4]
                    link(V.tensor_reduce(m, sc, AX, ALU.max))
                    link(V.scalar_tensor_tensor(m, m, 0.125, sink[:, 4 * b:4 * b + 4], ALU.mult, ALU.max))
                    V.scalar_tensor_tensor(pr[:, b], sc, 0.125, m.unsqueeze(2).broadcast_to([P, 4, P]),
                                           ALU.mult, ALU.subtract).then_inc(s_sub, 1)
                V.tensor_tensor(sm[:, 2, :], sink, sm[:, 0, :], ALU.subtract).then_inc(s_sub, 1)
                dve.wait_ge(sq_rdy, l + 1)
                link(V.tensor_tensor(ri[:, 1], ri[:, 1], ri[:, 0], ALU.mult))
                for c in range(CT):
                    V.tensor_tensor_scan(tmp[:, c, :], avec[:, c, :], ri[:, 1, c, :], 0.0, ALU.mult,
                                         ALU.add).then_inc(chain.sem, 1)
                    chain.k += 1
                dve.wait_ge(chain.sem, chain.base + chain.k)
                dve.wait_ge(gelu_rdy, 2 * (l + 1))
                V.tensor_tensor(tmp[:], tmp[:], gel[:], ALU.mult).then_inc(ylru_rdy, 1)
                dve.wait_ge(s_exp, 5 * (l + 1))
                for b in range(4):
                    d = sm[:, 1, 4 * b:4 * b + 4]
                    link(V.tensor_reduce(d, pr[:, b], AX, ALU.add))
                    link(V.tensor_tensor(d, d, sm[:, 2, 4 * b:4 * b + 4], ALU.add))
                    link(V.reciprocal(d, d))
                    V.tensor_tensor(pr[:, b], pr[:, b], d.unsqueeze(2).broadcast_to([P, 4, P]),
                                    ALU.mult).then_inc(p_rdy, 1)
                dve.wait_ge(yh_rdy, 3 * l + 1)
                V.tensor_tensor(al[:, 0:CT * T], tmp[:].rearrange("p c t -> p (c t)"), ah[:, 0:CT * T].bitcast(F32),
                                ALU.subtract).then_inc(yl_rdy, 1)
                for g in range(2):
                    dve.wait_ge(yh_rdy, 3 * l + 2 + g)
                    V.tensor_tensor(xTl[:, 4 + 2 * g:6 + 2 * g, :], bank[:, g, :].rearrange("p (r t) -> p r t", r=2),
                                    xTh[:, 4 + 2 * g:6 + 2 * g, :].bitcast(F32), ALU.subtract).then_inc(yl_rdy, 1)
                for j in range(3):
                    lo(p0 + 10 + j)
                norm(2 * l, p0 + MIXP)

            def dense():
                split_x(1)
                for i in range(FFP):
                    if i in H_AT:
                        c = H_AT[i]
                        for t in range(NT):
                            dve.wait_ge(silu_rdy, NT * c + t + 1)
                            ins = V.tensor_tensor(hs[:, t, :], hs[:, t, :], bank[:, t, FC:2 * FC], ALU.mult)
                        ins.then_inc(h_rdy, 1)
                    if i in HT_AT:
                        c = HT_AT[i]
                        dve.wait_ge(hTh_rdy, c + 1)
                        V.tensor_tensor(htl[:], bank[:, 6:8, 0:FC], hth[:].bitcast(F32), ALU.subtract).then_inc(hTl_rdy, 1)
                    lo(MIXP + i + 2)
                norm(1, MIXP + FFP)

            lo(0)
            lo(1)
            mixer(0)
            dense()
            mixer(1)
            split_x(3)
            link(V.memset(ST, 0.0))
            V.memset(wt[:], 0.0).then_inc(st_sb, 1)
            dve.wait_ge(st_sb, 1)
            link(V.memset(ps_[:], 4 * BIG))
            dve.wait_ge(rt_in, 16)
            link(V.tensor_scalar(acc[:], x[:], ALPHA, None, ALU.mult))
            dve.wait_ge(lg_ps, 1)
            link(V.tensor_tensor(lg[:], bank[:, 2, 0:2 * NE].rearrange("p (t e) -> p t e", t=NT),
                                 rb.unsqueeze(1).broadcast_to([P, NT, NE]), ALU.add))
            for t in range(NT):
                link(V.max(mx8[:, t, :], lg[:, t, :]))
                link(V.max_index(ix8[:, t, :].bitcast(U32), mx8[:, t, :], lg[:, t, :]))
            V.tensor_tensor(tw[:, 0, :], mx8[:, :, 1], mx8[:, :, 0], ALU.subtract).then_inc(tw_in, 1)
            link(V.tensor_copy(ixf[:], ix8[:].bitcast(U32)))
            for a in range(2):
                for t in range(NT):
                    link(V.tensor_scalar(oh[:, a, t, :], iota[:, 0:NE], ixf[:, t, a:a + 1], None, ALU.is_equal))
            V.tensor_tensor(mk[:], oh[:, 0], oh[:, 1], ALU.add).then_inc(mk_rdy, 1)
            dve.wait_ge(tw_e, 1)
            link(V.tensor_scalar(tw[:, 2, :], tw[:, 1, :], 1.0, None, ALU.add))
            link(V.reciprocal(tw[:, 2, :], tw[:, 2, :]))
            link(V.tensor_tensor(tw[:, 3, :], tw[:, 1, :], tw[:, 2, :], ALU.mult))
            for t in range(NT):
                link(V.tensor_scalar(wt[:, t, 1:1 + NE], oh[:, 0, t, :], tw[:, 2, t:t + 1], None, ALU.mult))
                link(V.scalar_tensor_tensor(wt[:, t, 1:1 + NE], oh[:, 1, t, :], tw[:, 3, t:t + 1], wt[:, t, 1:1 + NE],
                                            ALU.mult, ALU.add))
            link(V.tensor_copy(wt[:, :, 1 + NE:1 + 2 * NE], wt[:, :, 1:1 + NE]))
            dve.wait_ge(pos_ps, 1)
            link(V.tensor_scalar(oh[:, 0], mk[:], -BIG, BIG, ALU.mult, ALU.add))
            link(V.tensor_tensor(ps_[:, :, 0:NE], bank[:, 3, 0:2 * NE].rearrange("p (t e) -> p t e", t=NT),
                                 oh[:, 0], ALU.add))
            link(V.tensor_scalar(ps_[:, :, NE:2 * NE], ps_[:, :, 0:NE], -float(P), None, ALU.add))
            link(V.tensor_reduce(cm[:, 0:1], bank[:, 3, 2 * NE:3 * NE], AX, ALU.max))
            link(V.tensor_scalar(cm[:, 0:1], cm[:, 0:1], float(P), float(NE), ALU.is_gt, ALU.mult))
            link(V.tensor_scalar(cm[:, 0:1], cm[:, 0:1], float(NE), None, ALU.add))
            V.tensor_copy(njob_i[:], cm[:, 0:1]).then_inc(tab_rdy, 1)

            def one_hot(j):
                link(V.tensor_copy(pc.unsqueeze(2), ps_[:, :, bass.ds(j, 1)]))
                for t in range(NT):
                    ins = V.tensor_scalar(S[:, t, :], iota, pc[:, t:t + 1], None, ALU.is_equal)
                ins.then_inc(S_rdy, 1)

            def split_rows(j):
                dve.wait_ge(xgh_rdy, j + 1)
                V.tensor_tensor(xgl, bank[:, 4:6, :].rearrange("p b (k s) -> p (b k) s", k=4), xgh.bitcast(F32),
                                ALU.subtract).then_inc(xgl_rdy, 1)

            def add_up(j, t):
                dve.wait_ge(sc_ps, j * NT + (t + 1))
                for n, b in ((0, 7), (1, 1)):
                    sl = acc[:, t, n * 512:(n + 1) * 512]
                    ins = V.scalar_tensor_tensor(sl, bank[:, b, :], wc[:, t:t + 1], sl, ALU.mult, ALU.add)
                ins.then_inc(acc_rdy, 1)

            one_hot(0)
            split_rows(0)
            dve.wait_ge(tab_rdy, 1)
            njob = dve.value_load(njob_i[0:1, 0:1], min_val=NE, max_val=2 * NE)
            hb, sb0 = NCH, NT * NCH
            c0 = chain.k
            LINKS = 2
            with dve.Fori(0, njob) as j:
                chain.base, chain.k = j * LINKS + c0, 0
                for i in range(FFP):
                    if i == 1:
                        link(V.tensor_copy(wc.unsqueeze(2), wt[:, :, bass.ds(j, 1)]))
                    if i in H_AT:
                        c = H_AT[i]
                        dve.wait_ge(silu_rdy, j * NCH + (sb0 + c + 1))
                        V.tensor_tensor(he, he, bank[:, 0, FC:2 * FC], ALU.mult).then_inc(h_rdy, 1)
                    if i in HT_AT:
                        c = HT_AT[i]
                        dve.wait_ge(hTh_rdy, j * NCH + (hb + c + 1))
                        V.tensor_tensor(htl[:, 0, :], bank[:, 6, 0:FC], hth[:, 0, :].bitcast(F32),
                                        ALU.subtract).then_inc(hTl_rdy, 1)
                    if i in ACC_AT:
                        add_up(j, ACC_AT[i])
                    if i == S_AT:
                        dve.wait_ge(st_ps, j + 1)
                        one_hot(j + 1)
                    if i == XG_AT:
                        split_rows(j + 1)
                    q = STREAM + i + 2
                    dve.wait_ge(hi_rdy, j * FFP + (q + 1))
                    V.tensor_tensor(wlo[:, q % SPLIT, :], raw[:, q % RING, :], whi[:, q % SPLIT, :].bitcast(F32),
                                    ALU.subtract).then_inc(lo_rdy, 1)
                assert chain.k == LINKS
            chain.sem, chain.base, chain.k = dve_tail, 0, 0
            link(V.tensor_copy(wc.unsqueeze(2), wt[:, :, bass.ds(njob, 1)]))
            for t in range(NT):
                add_up(njob, t)
            dve.wait_ge(acc_rdy, njob * NT + NT)
            norm(3, None, from_acc=True)


def pack_weights(v):
    W = np.empty((NPIECE, P, PW), np.float32)
    at = 0

    def ff(wg, wu, wd, at):
        g = wg.reshape(2, 4, P, NCH, FC)
        u = wu.reshape(2, 4, P, NCH, FC)
        d = wd.reshape(NCH, 2, P, D)
        for i, (kind, c) in enumerate(FFORDER):
            if kind == "D":
                W[at + i] = d[c].transpose(1, 0, 2).reshape(P, PW)
            else:
                h = "AB".index(kind)
                dst = W[at + i].reshape(P, 4, 2, FC)
                dst[:, :, 0] = g[h, :, :, c].transpose(1, 0, 2)
                dst[:, :, 1] = u[h, :, :, c].transpose(1, 0, 2)

    for l in range(DEPTH):
        wi = v["w_in"][l].reshape(KT, P, 7, 256)
        for j in (0, 1, 4, 5, 6, 2, 3):
            W[at] = wi[:, :, j].transpose(1, 0, 2).reshape(P, PW)
            at += 1
        wo = v["w_out"][l].reshape(4, 2, P, D)
        for j in range(4):
            W[at] = wo[j].transpose(1, 0, 2).reshape(P, PW)
            at += 1
        if l == 0:
            ff(v["ffn_w_gate"][0], v["ffn_w_up"][0], v["ffn_w_down"][0], at)
            at += FFP
        else:
            for e in range(NE):
                ff(v["exp_w_gate"][0, e], v["exp_w_up"][0, e], v["exp_w_down"][0, e], at)
                at += FFP
    return W


def kernel(**inputs):
    import concourse.bacc as bacc
    from concourse.bass_utils import run_bass_kernel_spmd as run

    v = {k: np.asarray(a) for k, a in inputs.items()}
    W = pack_weights(v)
    x = v["x"].reshape(NT, P, D)
    par = np.zeros((P, DEPTH, PARW), np.float32)
    wbd = np.zeros((DEPTH, P, 2, CT, P), np.float32)
    for l in range(DEPTH):
        cols = [v["conv_w"][l].reshape(TAPS * CT, P), v["conv_b"][l].reshape(CT, P), v["lru_ba"][l].reshape(CT, P),
                v["lru_bx"][l].reshape(CT, P), v["lru_lambda"][l].reshape(CT, P)]
        par[:, l, 0:CHANW] = np.concatenate(cols, 0).T
        s = v["attn_sink"][l].reshape(4, 2).T.reshape(8)
        par[:, l, CHANW:CHANW + 8] = s
        par[:, l, CHANW + 8:CHANW + 16] = s
        for g, name in enumerate(("lru_wa", "lru_wx")):
            for h in range(8):
                r = 64 * (h % 2)
                wbd[l, r:r + 64, g, h // 2, r:r + 64] = v[name][l, h]
    gb = np.empty((2 * DEPTH, P, 2, D), np.float32)
    for l in range(DEPTH):
        for a in range(2):
            gb[2 * l + a, :, 0] = v[f"ln{a + 1}_g"][l]
            gb[2 * l + a, :, 1] = v[f"ln{a + 1}_b"][l]
    cst = np.zeros((P, P + 64), np.float32)
    cst[:, 0:P] = np.eye(P)
    inv = (500000.0 ** (-np.arange(0, ROT, 2, dtype=np.float32) / np.float32(ROT))).astype(np.float32)
    ang = (np.arange(T, dtype=np.float32)[:, None] * inv[None, :]).reshape(NT, P, ROT // 2)
    tab = cst[:, P:].reshape(P, NT, 2, 2, ROT // 2)
    for a, fn in enumerate((np.cos, np.sin)):
        tab[:, :, a] = fn(ang).transpose(1, 0, 2)[:, :, None, :]
    rt = np.zeros((P, 3 * P + KT * NE + NE), np.float32)
    rt[:, 0:P] = np.triu(np.ones((P, P)), 1)
    rt[:, P:2 * P] = 1.0
    rt[:, 2 * P:3 * P] = np.arange(P)
    rt[:, 3 * P:3 * P + KT * NE] = v["router_w"][0].reshape(KT, P, NE).transpose(1, 0, 2).reshape(P, KT * NE)
    rt[:, 3 * P + KT * NE:] = v["router_b"][0]

    nc = bacc.Bacc("TRN2", target_bir_lowering=False, num_devices=1)
    arrays = {"W": W, "x_d": x, "par_d": par, "wbd_d": wbd.reshape(DEPTH, P, 1024),
              "gb_d": gb.reshape(2 * DEPTH, P, 2 * D), "cst_d": cst, "rt_d": rt}
    arrays = {k: np.ascontiguousarray(a) for k, a in arrays.items()}
    aps = [nc.dram_tensor(k, a.shape, F32, kind="ExternalInput").ap() for k, a in arrays.items()]
    out = nc.dram_tensor("out_d", (NT, P, D), F32, kind="ExternalOutput").ap()
    build(nc, *aps, out)
    r = run(nc, [arrays], core_ids=[0])
    return r.results[0]["out_d"].reshape(1, T, D)
```

```python
from contextlib import ExitStack

import numpy as np

import concourse.bass as bass
from concourse import mybir

F32 = mybir.dt.float32
F32R = mybir.dt.float32r
I32 = mybir.dt.int32
U32 = mybir.dt.uint32
ALU = mybir.AluOpType
ACT = mybir.ActivationFunctionType
AX = mybir.AxisListType.X

P = 128
T = 256
NT = T // P
D = 1024
KT = D // P
DEPTH = 2
DLRU = 512
CT = DLRU // P
TAPS = 4
HD = 64
NH = 8
NKV = 2
CH = 64
ROT = 16
F = 2816
FC = 256
NCH = F // FC
NE = 8
ALPHA = float((2 * DEPTH) ** 0.25)
EPS = 1e-5
BIG = 1.0e6

PW = 2048
RING = 11
SPLIT = 3
MIXP = 11
FFP = 3 * NCH
STREAM = 2 * MIXP + FFP
NPIECE = STREAM + NE * FFP

FFORDER = [("A", 0), ("B", 0)]
for _c in range(1, NCH):
    FFORDER += [("A", _c), ("B", _c), ("D", _c - 1)]
FFORDER += [("D", NCH - 1)]
STEP = {kc: i for i, kc in enumerate(FFORDER)}
H_AT = {STEP[("B", c)] + 1: c for c in range(NCH)}
T_AFTER = {(STEP[("A", 1)] if c == 0 else STEP[("D", c - 1)]): c for c in range(NCH)}
HT_AT = {i + 1: c for i, c in T_AFTER.items()}

SCAT_AFTER = {1: 0, 3: 1}
ACC_AT = {2: 0, 4: 1}
ST_AFTER = 8
ST_AT = 9
S_AT = 11
GATHER_AFTER = {14: 0, 17: 1}
XG_AT = FFP - 2

CHANW = TAPS * CT + 4 * CT
PARW = CHANW + 2 * NH


class Steps:

    def __init__(self, eng, sem):
        self.eng, self.sem, self.base, self.k = eng, sem, 0, 0

    def link(self, ins):
        self.k += 1
        ins.then_inc(self.sem, 1)
        self.eng.wait_ge(self.sem, self.base + self.k)


def build(nc, W, x_d, par_d, wbd_d, gb_d, cst_d, rt_d, out_d):
    with ExitStack() as ctx:
        def sb(name, shape, dt=F32):
            return ctx.enter_context(nc.sbuf_tensor(name, shape, dt))

        def sem(name):
            return ctx.enter_context(nc.semaphore(name))

        raw = sb("raw", [P, RING, PW])
        whi = sb("whi", [P, SPLIT, PW], F32R)
        wlo = sb("wlo", [P, SPLIT, PW], F32R)
        x = sb("x", [P, NT, D])
        ah = sb("ah", [P, KT * T], F32R)
        al = sb("al", [P, KT * T], F32R)
        hth = sb("hth", [P, NT, FC], F32R)
        htl = sb("htl", [P, NT, FC], F32R)
        ident = sb("ident", [P, P])
        par = sb("par", [P, DEPTH, PARW])
        cs = sb("cs", [P, NT, 2, ROT])
        nsp = sb("nsp", [P, 5, DEPTH, CT])
        sm = sb("sm", [P, 4, 16])
        bnst = sb("bnst", [P, NT, 2, 6])
        mv = sb("mv", [P, NT, 2])
        rstd = sb("rstd", [P, NT])
        njob_i = sb("njob_i", [P, 1], I32)
        with nc.sbuf_tensor("scr", [P, 10384], F32) as scr:
            pass
        rtab = sb("rtab", [P, 3 * P + KT * NE + NE])
        msc = sb("msc", [P, 224])
        S = sb("S", [P, NT, P], F32R)
        ST = sb("ST", [P, NT, P], F32R)
        yh = sb("yh", [P, D], F32R)
        yl = sb("yl", [P, D], F32R)
        he = sb("he", [P, FC])
        acc = sb("acc", [P, NT, D])
        xnh = sb("xnh", [P, NT, D], F32R)
        xnl = sb("xnl", [P, NT, D], F32R)

        xTh = ah[:, :].rearrange("p (k t) -> p k t", k=KT)
        xTl = al[:, :].rearrange("p (k t) -> p k t", k=KT)
        xgh = ah[:, 0:KT * P].rearrange("p (k s) -> p k s", k=KT)
        xgl = al[:, 0:KT * P].rearrange("p (k s) -> p k s", k=KT)

        def region(first, n, pat=None, **kw):
            r = scr[:, first:first + n]
            return r.rearrange(pat, **kw) if pat else r
        wbd = region(0, 1024, pat="p (g c n) -> p g c n", g=2, c=CT)
        avec = region(0, 1024, pat="p (c t) -> p c t", c=CT)
        up = region(1024, 1040, pat="p (c t) -> p c t", c=CT)
        tmp = region(1024, 1024, pat="p (c t) -> p c t", c=CT)
        uc = region(2064, 1024, pat="p (c t) -> p c t", c=CT)
        ri = region(3088, 2048, pat="p (g c t) -> p g c t", g=2, c=CT)
        pt = region(3088, 2048, pat="p (b r q) -> p b r q", b=4, r=4)
        gel = region(5136, 1024, pat="p (c t) -> p c t", c=CT)
        qkv = region(6160, 1536, pat="p (t n) -> p t n", t=NT)
        kd = region(7696, 512, pat="p (t g n) -> p t g n", t=NT, g=NKV)
        pr = region(6160, 2048, pat="p (b r k) -> p b r k", b=4, r=4)
        gb = region(6160, 2048, pat="p (a n) -> p a n", a=2)
        qT = region(8208, 1024, pat="p (r t) -> p r t", r=4)
        ropa = region(8208, 320, pat="p (t h n) -> p t h n", t=NT, h=10)
        ropb = region(8528, 320, pat="p (t h n) -> p t h n", t=NT, h=10)
        kT = region(9232, 640, pat="p (g t) -> p g t", g=NKV)
        vo = region(9872, 256, pat="p (t n) -> p t n", t=NT)
        ve = region(10128, 256, pat="p (t n) -> p t n", t=NT)
        hs = region(0, NT * FC, pat="p (t n) -> p t n", t=NT)
        tri = rtab[:, 0:P]
        ones = rtab[:, P:2 * P]
        iota = rtab[:, 2 * P:3 * P]
        rw = rtab[:, 3 * P:3 * P + KT * NE]
        rb = rtab[:, 3 * P + KT * NE:]
        rwh = hth[:, 0, 0:KT * NE]
        rwl = htl[:, 0, 0:KT * NE]

        def small(first, n, pat=None, **kw):
            r = msc[:, first:first + n]
            return r.rearrange(pat, **kw) if pat else r
        lg = small(0, 16, "p (t e) -> p t e", t=NT)
        mx8 = small(16, 16, "p (t e) -> p t e", t=NT)
        ix8 = small(32, 16, "p (t e) -> p t e", t=NT)
        ixf = small(48, 16, "p (t e) -> p t e", t=NT)
        oh = small(64, 32, "p (a t e) -> p a t e", a=2, t=NT)
        mk = small(96, 16, "p (t e) -> p t e", t=NT)
        tw = small(112, 8, "p (a t) -> p a t", a=4)
        wt = small(120, 2 * 18, "p (t e) -> p t e", t=NT)
        ps_ = small(156, 2 * 18, "p (t e) -> p t e", t=NT)
        wc = small(192, 2)
        pc = small(194, 2)
        cm = small(196, 2)
        far = small(200, 16, "p (t e) -> p t e", t=NT)
        gbx = x[:, :, :]

        bank = ctx.enter_context(nc.psum_tensor("bank", [P, 8, 512], F32))

        raw_in = [sem(f"raw_in{s}") for s in range(RING)]
        hi_rdy = sem("hi_rdy")
        lo_rdy = sem("lo_rdy")
        used = sem("piece_used")
        x_in = [sem(f"x_in{t}") for t in range(NT)]
        ident_in = sem("ident_in")
        cs_in = sem("cs_in")
        par_in = sem("par_in")
        wbd_in = sem("wbd_in")
        gb_in = sem("gb_in")
        rt_in = sem("rt_in")
        x_rdy = sem("x_rdy")
        xT_ps = sem("xT_ps")
        xTh_rdy = sem("xTh_rdy")
        xTl_rdy = sem("xTl_rdy")
        u_sb = sem("u_sb")
        uc_rdy = sem("uc_rdy")
        qkv_sb = sem("qkv_sb")
        gate_ps = sem("gate_ps")
        sig_rdy = sem("sig_rdy")
        gelu_rdy = sem("gelu_rdy")
        nsp_e = sem("nsp_e")
        nsp_rdy = sem("nsp_rdy")
        rope_rdy = sem("rope_rdy")
        qT_ps = sem("qT_ps")
        qT_sb = sem("qT_sb")
        at_rdy = sem("at_rdy")
        v_rdy = sem("v_rdy")
        sq_rdy = sem("sq_rdy")
        ylru_rdy = sem("ylru_rdy")
        yh_rdy = sem("yh_rdy")
        yl_rdy = sem("yl_rdy")
        s_ps = sem("s_ps")
        s_max = sem("s_max")
        s_exp = sem("s_exp")
        es_rdy = sem("es_rdy")
        y0_ps = sem("y0_ps")
        rw_h = sem("rw_h")
        rw_l = sem("rw_l")
        yh_sb = sem("yh_sb")
        xn_h = sem("xn_h")
        xn_l = sem("xn_l")
        acc0_rdy = sem("acc0_rdy")
        p_rdy = sem("p_rdy")
        pt_ps = sem("pt_ps")
        pt_sb = sem("pt_sb")
        o_ps = sem("o_ps")
        var_rdy = sem("var_rdy")
        std_rdy = sem("std_rdy")
        silu_rdy = sem("silu_rdy")
        h_rdy = sem("h_rdy")
        hT_ps = sem("hT_ps")
        hTh_rdy = sem("hTh_rdy")
        hTl_rdy = sem("hTl_rdy")
        lg_ps = sem("lg_ps")
        tw_in = sem("tw_in")
        tw_e = sem("tw_e")
        mk_rdy = sem("mk_rdy")
        pos_ps = sem("pos_ps")
        tab_rdy = sem("tab_rdy")
        S_rdy = sem("S_rdy")
        xg_ps = sem("xg_ps")
        xgh_rdy = sem("xgh_rdy")
        xgl_rdy = sem("xgl_rdy")
        st_ps = sem("st_ps")
        st_sb = sem("st_sb")
        yl_sb = sem("yl_sb")
        sc_ps = sem("sc_ps")
        acc_rdy = sem("acc_rdy")
        dve_step = sem("dve_step")
        dve_tail = sem("dve_tail")
        yh_last = sem("yh_last")
        yl_last = sem("yl_last")
        out_done = sem("out_done")

        block = ctx.enter_context(nc.Block())

        SB = (0, 1, 7, 6)
        LB = (7, 1, 0, 6)

        def xbank(t, g):
            return 6 * t + g

        @block.sync
        def _(sp):
            sp.dma_start(x[:, 0, :], x_d[0]).then_inc(x_in[0], 16)
            sp.dma_start(ident[:], cst_d[:, 0:P]).then_inc(ident_in, 16)
            sp.dma_start(x[:, 1, :], x_d[1]).then_inc(x_in[1], 16)
            for s in range(RING):
                sp.dma_start(raw[:, s, :], W[s]).then_inc(raw_in[s], 16)
            rounds = NPIECE // RING
            with sp.Fori(1, rounds) as r:
                for s in range(RING):
                    sp.wait_ge(lo_rdy, r * RING + (s + 1 - RING))
                    sp.dma_start(raw[:, s, :], W[bass.ds(r * RING + s, 1)].rearrange("a p n -> (a p) n")
                                 ).then_inc(raw_in[s], 16)
            sp.wait_ge(tab_rdy, 1)
            njob = sp.value_load(njob_i[0:1, 0:1], min_val=NE, max_val=2 * NE)
            with sp.If(njob > NE):
                with sp.Fori(rounds, njob * (FFP // RING) + STREAM // RING) as r:
                    for s in range(RING):
                        sp.wait_ge(lo_rdy, r * RING + (s + 1 - RING))
                        sp.dma_start(raw[:, s, :],
                                     W[bass.ds(r * RING + (s - NE * FFP), 1)].rearrange("a p n -> (a p) n")
                                     ).then_inc(raw_in[s], 16)
            for s in range(2):
                sp.wait_ge(lo_rdy, njob * FFP + (STREAM + s + 1 - RING))
                sp.dma_start(raw[:, s, :], W[STREAM + s]).then_inc(raw_in[s], 16)
            for t in range(NT):
                sp.wait_ge(x_rdy, 2 * DEPTH * NT - NT + t + 1)
                sp.dma_start(out_d[t], acc[:, t, :]).then_inc(out_done, 16)
            sp.wait_ge(out_done, 16 * NT)

        @block.gpsimd
        def _(pool):
            pool.dma_start(par[:], par_d).then_inc(par_in, 16)
            pool.dma_start(cs[:], cst_d[:, P:P + 64].rearrange("p (t a n) -> p t a n", t=NT, a=2)).then_inc(cs_in, 16)
            for l in range(DEPTH):
                if l:
                    pool.wait_ge(x_rdy, 2 * l * NT)
                pool.dma_start(scr[:, 0:1024], wbd_d[l]).then_inc(wbd_in, 16)
                if l == DEPTH - 1:
                    pool.wait_ge(ylru_rdy, DEPTH)
                    pool.dma_start(rtab[:], rt_d).then_inc(rt_in, 16)
                pool.wait_ge(pt_ps, 4 * (l + 1))
                pool.dma_start(gb.rearrange("p a n -> p (a n)"), gb_d[2 * l]).then_inc(gb_in, 16)
                pool.wait_ge(x_rdy, NT * (2 * l + 1))
                if l == 0:
                    pool.dma_start(gb.rearrange("p a n -> p (a n)"), gb_d[1]).then_inc(gb_in, 16)
                else:
                    pool.wait_ge(acc0_rdy, NT)
                    pool.dma_start(gbx.rearrange("p a n -> p (a n)"), gb_d[3]).then_inc(gb_in, 16)

        @block.tensor
        def _(pe):
            def piece(p):
                pe.wait_ge(lo_rdy, p + 1)

            def transpose_x(ph, t):
                if ph == 0:
                    pe.wait_ge(x_in[t], 16)
                    pe.wait_ge(ident_in, 16)
                else:
                    pe.wait_ge(x_rdy, NT * (ph - 1) + t + 1)
                for g in range(2):
                    for k in range(4):
                        last = nc.tensor.transpose(bank[:, xbank(t, g), k * P:(k + 1) * P],
                                                   x[:, t, (4 * g + k) * P:(4 * g + k + 1) * P], ident[:])
                    last.then_inc(xT_ps, 1)

            def split_ready(ph, t):
                pe.wait_ge(xTl_rdy, 4 * ph + 2 * t + 2)

            def three(out, sh, sl, mh, ml, first, last):
                nc.tensor.matmul(out, sh, mh, start=first, stop=False, skip_group_check=True)
                nc.tensor.matmul(out, sh, ml, start=False, stop=False, skip_group_check=True)
                return nc.tensor.matmul(out, sl, mh, start=False, stop=last, skip_group_check=True)

            def mixer(l):
                p0 = l * (MIXP + FFP)

                def wslot(p):
                    s = p % SPLIT
                    return (whi[:, s, :].rearrange("p (k n) -> p k n", k=KT),
                            wlo[:, s, :].rearrange("p (k n) -> p k n", k=KT))

                def channels(p, b):
                    piece(p)
                    wh, wl = wslot(p)
                    for c in range(2):
                        for k in range(KT):
                            last = three(bank[:, b, c * T:(c + 1) * T], wh[:, k, c * P:(c + 1) * P],
                                         wl[:, k, c * P:(c + 1) * P], xTh[:, k, :], xTl[:, k, :], k == 0, k == KT - 1)
                    last.then_inc(used, 1)

                def rows(p, b, t):
                    piece(p)
                    wh, wl = wslot(p)
                    for k in range(KT):
                        last = three(bank[:, b, t * 256:(t + 1) * 256], xTh[:, k, t * P:(t + 1) * P],
                                     xTl[:, k, t * P:(t + 1) * P], wh[:, k, :], wl[:, k, :], k == 0, k == KT - 1)
                    if t == NT - 1:
                        last.then_inc(used, 1)

                def gates(cp):
                    pe.wait_ge(wbd_in, 16 * (l + 1))
                    pe.wait_ge(uc_rdy, CT * l + 2 * cp + 2)
                    for g in range(2):
                        b = cp if g == 0 else 7 - cp
                        for c in range(2):
                            last = nc.tensor.matmul(bank[:, b, c * T:(c + 1) * T], wbd[:, g, 2 * cp + c, :],
                                                    uc[:, 2 * cp + c, :], start=True, stop=True)
                        last.then_inc(gate_ps, 1)

                for t in range(NT):
                    transpose_x(2 * l, t)
                    split_ready(2 * l, t)
                    rows(p0, 2, t)
                channels(p0 + 1, 0)
                channels(p0 + 2, 1)
                for t in range(NT):
                    rows(p0 + 3, 3, t)
                gates(0)
                for t in range(NT):
                    rows(p0 + 4, 4, t)
                gates(1)
                channels(p0 + 5, 5)
                pe.wait_ge(rope_rdy, l + 1)
                for b in range(2):
                    for r in range(2):
                        for t in range(NT):
                            last = nc.tensor.transpose(bank[:, 3 + b, r * T + t * P:r * T + (t + 1) * P],
                                                       qkv[:, t, (2 * b + r) * P:(2 * b + r + 1) * P], ident[:])
                    last.then_inc(qT_ps, 1)
                for g in range(NKV):
                    for t in range(NT):
                        last = nc.tensor.transpose(bank[:, 2, g * T + t * P:g * T + (t + 1) * P],
                                                   kd[:, t, g, :], ident[:])
                last.then_inc(qT_ps, 1)
                pe.wait_ge(sig_rdy, 4 * (l + 1))
                channels(p0 + 6, 6)
                pe.wait_ge(qT_sb, 3 * (l + 1))
                for b in range(4):
                    t, s = b // 2, b % 2
                    d0 = s * HD
                    if SB[b] == 6:
                        pe.wait_ge(gelu_rdy, 2 * (l + 1))
                    for r in range(4):
                        g = r // 2
                        q = 2 * t
                        dst = bank[:, SB[b], r * P:(r + 1) * P]
                        nc.tensor.matmul(dst[0:64, 0:64], qT[d0:d0 + HD, r, q * CH:(q + 1) * CH],
                                         kT[d0:d0 + HD, g, (q + 1) * CH:(q + 2) * CH],
                                         start=True, stop=True)
                        if t:
                            nc.tensor.matmul(dst[0:64, 64:128], qT[d0:d0 + HD, r, q * CH:(q + 1) * CH],
                                             kT[d0:d0 + HD, g, q * CH:(q + 1) * CH],
                                             start=True, stop=True)
                        last = nc.tensor.matmul(dst[64:128, :], qT[d0:d0 + HD, r, (q + 1) * CH:(q + 2) * CH],
                                                kT[d0:d0 + HD, g, (q + 1) * CH:(q + 3) * CH],
                                                start=True, stop=True)
                    last.then_inc(s_ps, 1)
                pe.wait_ge(gelu_rdy, 2 * l + 1)
                pe.wait_ge(yl_rdy, 3 * l + 1)
                for j in range(2):
                    piece(p0 + 7 + j)
                    down(p0 + 7 + j, xTh, xTl, 2 * j, j == 0, False, NT)
                for b in range(4):
                    pe.wait_ge(p_rdy, 4 * l + b + 1)
                    for r in range(4):
                        last = nc.tensor.transpose(bank[:, SB[b], r * P:(r + 1) * P], pr[:, b, r, :], ident[:])
                    last.then_inc(pt_ps, 1)
                pe.wait_ge(pt_sb, 4 * (l + 1))
                for g in range(NKV):
                    for s in range(2):
                        for t in range(NT):
                            for half, v in ((0, ve), (1, vo)):
                                dst = bank[s * HD:(s + 1) * HD, g, :].rearrange("p (r t) -> p r t", r=2)
                                c0 = t * P + half * CH
                                last = nc.tensor.matmul(dst[:, :, c0:c0 + CH], v[:, t, g * HD:(g + 1) * HD],
                                                        pt[:, 2 * t + s, 2 * g:2 * g + 2, half * CH:(half + 1) * CH],
                                                        start=True, stop=True)
                    last.then_inc(o_ps, 1)
                for j in range(2, 4):
                    pe.wait_ge(yl_rdy, 3 * l + j)
                    piece(p0 + 7 + j)
                    down(p0 + 7 + j, xTh, xTl, 2 * j, False, j == 3, NT)

            def down(p, th, tl, k0, first, last_piece, nt):
                wh = whi[:, p % SPLIT, :].rearrange("p (k n) -> p k n", k=2)
                wl = wlo[:, p % SPLIT, :].rearrange("p (k n) -> p k n", k=2)
                downmm(wh, wl, th, tl, k0, first, last_piece, nt)

            def downmm(wh, wl, th, tl, k0, first, last_piece, nt):
                for t in range(nt):
                    for k in range(2):
                        sh = th[:, k0 + k, t * P:(t + 1) * P] if th is xTh else th[:, t, k * P:(k + 1) * P]
                        sl = tl[:, k0 + k, t * P:(t + 1) * P] if tl is xTl else tl[:, t, k * P:(k + 1) * P]
                        st, en = first and k == 0, last_piece and k == 1
                        dst = [bank[:, 2 + 2 * t + n, :] for n in range(2)]
                        for n in range(2):
                            nc.tensor.matmul(dst[n], sh, wh[:, k, n * 512:(n + 1) * 512], start=st, stop=False,
                                             skip_group_check=True)
                        for n in range(2):
                            nc.tensor.matmul(dst[n], sh, wl[:, k, n * 512:(n + 1) * 512], start=False, stop=False,
                                             skip_group_check=True)
                        for n in range(2):
                            last = nc.tensor.matmul(dst[n], sl, wh[:, k, n * 512:(n + 1) * 512], start=False, stop=en,
                                                    skip_group_check=True)
                    if last_piece and t == 0 and nt == NT:
                        last.then_inc(y0_ps, 1)
                last.then_inc(used, 1)

            def gate_up(slot, half, th, tl, tiles, final):
                wh = whi[:, slot, :].rearrange("p (k n) -> p k n", k=4)
                wl = wlo[:, slot, :].rearrange("p (k n) -> p k n", k=4)
                for t in tiles:
                    for k in range(4):
                        kk = 4 * half + k
                        last = three(bank[:, t, :], th[:, kk, t * P:(t + 1) * P], tl[:, kk, t * P:(t + 1) * P],
                                     wh[:, k, :], wl[:, k, :], kk == 0, kk == KT - 1)
                if final:
                    last.then_inc(used, 1)

            def transpose_h(src, nt):
                for t in range(nt):
                    for k in range(2):
                        last = nc.tensor.transpose(bank[:, 6 + t, k * P:(k + 1) * P], src(t, k), ident[:])
                last.then_inc(hT_ps, 1)

            def dense():
                for t in range(NT):
                    transpose_x(1, t)
                    split_ready(1, t)
                    for half in range(2):
                        piece(MIXP + half)
                        gate_up((MIXP + half) % SPLIT, half, xTh, xTl, [t], t == NT - 1)
                for i, (kind, c) in enumerate(FFORDER):
                    if i < 2:
                        continue
                    p = MIXP + i
                    piece(p)
                    if kind == "A" and c:
                        pe.wait_ge(h_rdy, c)
                    if kind == "D":
                        pe.wait_ge(hTl_rdy, c + 1)
                        down(p, hth, htl, 0, c == 0, c == NCH - 1, NT)
                    else:
                        gate_up(p % SPLIT, "AB".index(kind), xTh, xTl, range(NT), True)
                    if i in T_AFTER:
                        pe.wait_ge(h_rdy, T_AFTER[i] + 1)
                        if T_AFTER[i]:
                            pe.wait_ge(hTl_rdy, T_AFTER[i])
                        transpose_h(lambda t, k: hs[:, t, k * P:(k + 1) * P], NT)

            def gather(b):
                for k in range(4):
                    kk = 4 * b + k
                    for n, (t, a) in enumerate(((0, xnh), (0, xnl), (1, xnh), (1, xnl))):
                        last = nc.tensor.matmul(bank[:, 4 + b, k * P:(k + 1) * P], a[:, t, kk * P:(kk + 1) * P],
                                                S[:, t, :], start=(n == 0), stop=(n == 3))
                last.then_inc(xg_ps, 1)

            def scatter(t, n, b):
                nc.tensor.matmul(bank[:, b, :], ST[:, t, :], yh[:, n * 512:(n + 1) * 512], start=True, stop=False)
                nc.tensor.matmul(bank[:, b, :], ST[:, t, :], yl[:, n * 512:(n + 1) * 512], start=False,
                                 stop=True).then_inc(sc_ps, 1)

            def router():
                for t in range(NT):
                    transpose_x(3, t)
                    split_ready(3, t)
                    if t == 0:
                        pe.wait_ge(rw_l, 1)
                    for k in range(KT):
                        e8 = slice(k * NE, (k + 1) * NE)
                        last = three(bank[:, 2, t * NE:(t + 1) * NE], xTh[:, k, t * P:(t + 1) * P],
                                     xTl[:, k, t * P:(t + 1) * P], rwh[:, e8], rwl[:, e8], k == 0, k == KT - 1)
                    last.then_inc(lg_ps, 1)
                pe.wait_ge(mk_rdy, 1)
                nc.tensor.matmul(bank[:, 3, 0:NE], tri, mk[:, 0, :], start=True, stop=True)
                nc.tensor.matmul(bank[:, 3, NE:2 * NE], ones, mk[:, 0, :], start=True, stop=False)
                nc.tensor.matmul(bank[:, 3, NE:2 * NE], tri, mk[:, 1, :], start=False, stop=True)
                nc.tensor.matmul(bank[:, 3, 2 * NE:3 * NE], ones, mk[:, 0, :], start=True, stop=False)
                nc.tensor.matmul(bank[:, 3, 2 * NE:3 * NE], ones, mk[:, 1, :], start=False,
                                 stop=True).then_inc(pos_ps, 1)

            mixer(0)
            dense()
            mixer(1)
            router()
            pe.wait_ge(S_rdy, 1)
            pe.wait_ge(xn_l, 2)
            gather(0)
            gather(1)
            pe.wait_ge(tab_rdy, 1)
            njob = pe.value_load(njob_i[0:1, 0:1], min_val=NE, max_val=2 * NE)
            hb = NCH
            with pe.Fori(0, njob) as j:
                pe.wait_ge(xgl_rdy, j + 1)
                for i, (kind, c) in enumerate(FFORDER):
                    slot = (STREAM + i) % SPLIT
                    pe.wait_ge(lo_rdy, j * FFP + (STREAM + i + 1))
                    if kind == "A" and c:
                        pe.wait_ge(h_rdy, j * NCH + (hb + c))
                    if kind == "D":
                        if c == 0:
                            pe.wait_ge(yl_sb, j + 1)
                        pe.wait_ge(hTl_rdy, j * NCH + (hb + c + 1))
                        downmm(whi[:, slot, :].rearrange("p (k n) -> p k n", k=2),
                               wlo[:, slot, :].rearrange("p (k n) -> p k n", k=2),
                               hth, htl, 0, c == 0, c == NCH - 1, 1)
                    else:
                        gate_up(slot, "AB".index(kind), xgh, xgl, [0], True)
                    if i in SCAT_AFTER:
                        t = SCAT_AFTER[i]
                        if t == 0:
                            pe.wait_ge(yl_sb, j + 1)
                            pe.wait_ge(st_sb, j + 1)
                        else:
                            pe.wait_ge(acc_rdy, j * 4 + 2)
                        scatter(t, 0, 7)
                        scatter(t, 1, 1)
                    if i in T_AFTER:
                        pe.wait_ge(h_rdy, j * NCH + (hb + T_AFTER[i] + 1))
                        pe.wait_ge(hTl_rdy, j * NCH + (hb + T_AFTER[i]))
                        transpose_h(lambda t, k: he[:, k * P:(k + 1) * P], 1)
                    if i == ST_AFTER:
                        pe.wait_ge(acc_rdy, j * 4 + 4)
                        for t in range(NT):
                            last = nc.tensor.transpose(bank[:, 7, t * P:(t + 1) * P], S[:, t, :].bitcast(F32), ident[:])
                        last.then_inc(st_ps, 1)
                    if i in GATHER_AFTER:
                        pe.wait_ge(S_rdy, j + 2)
                        gather(GATHER_AFTER[i])
            pe.wait_ge(st_sb, njob + 1)
            for n in range(2):
                pe.wait_ge(yl_last, n + 1)
                for t in range(NT):
                    scatter(t, n, LB[2 * n + t])

        @block.scalar
        def _(act):
            def hi(p):
                act.wait_ge(raw_in[p % RING], 16 * (p // RING + 1))
                if p >= SPLIT:
                    act.wait_ge(used, p - SPLIT + 1)
                nc.scalar.activation(whi[:, p % SPLIT, :], raw[:, p % RING, :], ACT.Copy).then_inc(hi_rdy, 1)

            def split_x(ph, t):
                for g in range(2):
                    act.wait_ge(xT_ps, 4 * ph + 2 * t + g + 1)
                    nc.scalar.activation(xTh[:, 4 * g:4 * g + 4, t * P:(t + 1) * P],
                                         bank[:, xbank(t, g), :].rearrange("p (k t) -> p k t", k=4),
                                         ACT.Copy).then_inc(xTh_rdy, 1)

            def std(ph, split):
                for t in range(NT):
                    act.wait_ge(var_rdy, NT * ph + t + 1)
                    nc.scalar.activation(rstd[:, t:t + 1], mv[:, t, 1:2], ACT.Sqrt).then_inc(std_rdy, 1)
                    if split:
                        split_x(ph + 1, t)

            def mixer(l):
                p0 = l * (MIXP + FFP)
                if l == 0:
                    act.wait_ge(nsp_rdy, 1)
                    nc.scalar.activation(nsp[:, 2], nsp[:, 1], ACT.Exp, scale=-1.0).then_inc(nsp_e, 1)
                    split_x(0, 0)
                    hi(0)
                    split_x(0, 1)
                    hi(1)
                hi(p0 + 2)

                def rows_out(j, b, o):
                    act.wait_ge(used, p0 + j + 1)
                    nc.scalar.activation(qkv[:, :, o * 256:(o + 1) * 256],
                                         bank[:, b, :].rearrange("p (t n) -> p t n", t=NT),
                                         ACT.Copy).then_inc(qkv_sb, 1)
                    hi(p0 + j + 3)

                def sigmoids(cp):
                    for g in range(2):
                        b = cp if g == 0 else 7 - cp
                        act.wait_ge(gate_ps, 4 * l + 2 * cp + g + 1)
                        for c in range(2):
                            o = TAPS * CT + (1 + g) * CT + 2 * cp + c
                            last = nc.scalar.activation(ri[:, g, 2 * cp + c, :], bank[:, b, c * T:(c + 1) * T],
                                                        ACT.Sigmoid, bias=par[:, l, o:o + 1])
                        last.then_inc(sig_rdy, 1)

                rows_out(0, 2, 0)
                for j in range(2):
                    act.wait_ge(used, p0 + j + 2)
                    nc.scalar.activation(up[:, 2 * j:2 * j + 2, TAPS:TAPS + T],
                                         bank[:, j, :].rearrange("p (c t) -> p c t", c=2), ACT.Copy).then_inc(u_sb, 1)
                    hi(p0 + 4 + j)
                rows_out(3, 3, 1)
                sigmoids(0)
                rows_out(4, 4, 2)
                sigmoids(1)
                act.wait_ge(nsp_rdy, 2)
                act.wait_ge(sig_rdy, 4 * (l + 1))
                for c in range(CT):
                    nc.scalar.activation(avec[:, c, :], ri[:, 0, c, :], ACT.Exp, scale=nsp[:, 0, l, c:c + 1])
                for c in range(CT):
                    last = nc.scalar.activation(tmp[:, c, :], ri[:, 0, c, :], ACT.Tanh, scale=nsp[:, 1, l, c:c + 1])
                last.then_inc(at_rdy, 1)
                hi(p0 + 8)
                for b in range(2):
                    act.wait_ge(qT_ps, 3 * l + b + 1)
                    nc.scalar.activation(qT[:, 2 * b:2 * b + 2, :], bank[:, 3 + b, :].rearrange("p (r t) -> p r t", r=2),
                                         ACT.Copy).then_inc(qT_sb, 1)
                act.wait_ge(qT_ps, 3 * l + 3)
                nc.scalar.activation(kT[:, :, CH:CH + T], bank[:, 2, :].rearrange("p (g t) -> p g t", g=NKV),
                                     ACT.Copy).then_inc(qT_sb, 1)
                act.wait_ge(v_rdy, l + 1)
                nc.scalar.activation(ri[:, 0], tmp[:], ACT.Sqrt).then_inc(sq_rdy, 1)
                for j in range(2):
                    act.wait_ge(used, p0 + 6 + j)
                    nc.scalar.activation(gel[:, 2 * j:2 * j + 2, :],
                                         bank[:, 5 + j, :].rearrange("p (c t) -> p c t", c=2),
                                         ACT.Gelu_apprx_tanh).then_inc(gelu_rdy, 1)
                hi(p0 + 9)
                act.wait_ge(ylru_rdy, l + 1)
                act.wait_ge(used, p0 + 7)
                nc.scalar.activation(ah[:, 0:CT * T], tmp[:].rearrange("p c t -> p (c t)"), ACT.Copy).then_inc(yh_rdy, 1)
                for b in range(4):
                    act.wait_ge(s_max, 5 * l + b + 1)
                    for r in range(4):
                        n = 4 * b + r
                        last = nc.scalar.activation(pr[:, b, r, :], bank[:, SB[b], r * P:(r + 1) * P], ACT.Exp,
                                                    bias=sm[:, 1, n:n + 1], scale=0.125, accum_out=sm[:, 2, n:n + 1])
                    last.then_inc(s_exp, 1)
                    if b == 0:
                        act.wait_ge(s_max, 5 * l + 5)
                        nc.scalar.activation(sm[:, 3, :], sm[:, 3, :], ACT.Exp).then_inc(es_rdy, 1)
                for b in range(4):
                    act.wait_ge(pt_ps, 4 * l + b + 1)
                    nc.scalar.activation(pt[:, b], bank[:, SB[b], :].rearrange("p (r q) -> p r q", r=4),
                                         ACT.Copy).then_inc(pt_sb, 1)
                for g in range(2):
                    act.wait_ge(o_ps, 2 * l + g + 1)
                    nc.scalar.activation(xTh[:, 4 + 2 * g:6 + 2 * g, :],
                                         bank[:, g, :].rearrange("p (r t) -> p r t", r=2), ACT.Copy).then_inc(yh_rdy, 1)
                for j in range(3):
                    hi(p0 + 10 + j)
                if l == DEPTH - 1:
                    act.wait_ge(rt_in, 16)
                    nc.scalar.activation(rwh, rw, ACT.Copy).then_inc(rw_h, 1)
                std(2 * l, True)

            def dense():
                for i in range(FFP):
                    if i in H_AT:
                        c = H_AT[i]
                        act.wait_ge(used, MIXP + STEP[("B", c)] + 1)
                        if c:
                            act.wait_ge(hT_ps, c)
                        for t in range(NT):
                            nc.scalar.activation(hs[:, t, :], bank[:, t, 0:FC], ACT.Silu).then_inc(silu_rdy, 1)
                    if i in HT_AT:
                        c = HT_AT[i]
                        act.wait_ge(hT_ps, c + 1)
                        if c:
                            act.wait_ge(used, MIXP + STEP[("D", c - 1)] + 1)
                        nc.scalar.activation(hth[:], bank[:, 6:8, 0:FC], ACT.Copy).then_inc(hTh_rdy, 1)
                    hi(MIXP + i + 2)
                std(1, True)

            mixer(0)
            dense()
            mixer(1)
            for t in range(NT):
                act.wait_ge(x_rdy, 3 * NT - NT + t + 1)
                nc.scalar.activation(xnh[:, t, :], x[:, t, :], ACT.Copy).then_inc(xn_h, 1)
            act.wait_ge(tw_in, 1)
            nc.scalar.activation(tw[:, 1, :], tw[:, 0, :], ACT.Exp).then_inc(tw_e, 1)

            def split_rows(j):
                act.wait_ge(xg_ps, 2 * j + 2)
                nc.scalar.activation(xgh, bank[:, 4:6, :].rearrange("p b (k s) -> p (b k) s", k=4),
                                     ACT.Copy).then_inc(xgh_rdy, 1)

            split_rows(0)
            act.wait_ge(tab_rdy, 1)
            njob = act.value_load(njob_i[0:1, 0:1], min_val=NE, max_val=2 * NE)
            hb = NCH
            with act.Fori(0, njob) as j:
                for i in range(FFP):
                    if i == 0:
                        act.wait_ge(used, j * FFP + STREAM)
                        nc.scalar.activation(yh[:], bank[:, 2:4, :].rearrange("p b n -> p (b n)"),
                                             ACT.Copy).then_inc(yh_sb, 1)
                    if i in H_AT:
                        c = H_AT[i]
                        act.wait_ge(used, j * FFP + (STREAM + STEP[("B", c)] + 1))
                        act.wait_ge(hT_ps, j * NCH + (hb + c))
                        nc.scalar.activation(he[:], bank[:, 0, 0:FC], ACT.Silu).then_inc(silu_rdy, 1)
                    if i in HT_AT:
                        c = HT_AT[i]
                        act.wait_ge(hT_ps, j * NCH + (hb + c + 1))
                        nc.scalar.activation(hth[:, 0, :], bank[:, 6, 0:FC], ACT.Copy).then_inc(hTh_rdy, 1)
                    if i == ST_AT:
                        act.wait_ge(st_ps, j + 1)
                        nc.scalar.activation(ST[:], bank[:, 7, 0:2 * P].rearrange("p (t n) -> p t n", t=NT),
                                             ACT.Copy).then_inc(st_sb, 1)
                    if i == XG_AT:
                        split_rows(j + 1)
                    q = STREAM + i + 2
                    act.wait_ge(raw_in[q % RING], j * (16 * FFP // RING) + 16 * (q // RING + 1))
                    act.wait_ge(used, j * FFP + (q - SPLIT + 1))
                    nc.scalar.activation(whi[:, q % SPLIT, :], raw[:, q % RING, :], ACT.Copy).then_inc(hi_rdy, 1)
            act.wait_ge(used, njob * FFP + STREAM)
            for n in range(2):
                nc.scalar.activation(yh[:, n * 512:(n + 1) * 512], bank[:, 2 + n, :], ACT.Copy).then_inc(yh_last, 1)
            std(3, False)

        @block.vector
        def _(dve):
            chain = Steps(dve, dve_step)
            link = chain.link
            V = nc.vector

            def lo(p):
                dve.wait_ge(hi_rdy, p + 1)
                V.tensor_tensor(wlo[:, p % SPLIT, :], raw[:, p % RING, :], whi[:, p % SPLIT, :].bitcast(F32),
                                ALU.subtract).then_inc(lo_rdy, 1)

            def split_x(ph, t):
                for g in range(2):
                    dve.wait_ge(xTh_rdy, 4 * ph + 2 * t + g + 1)
                    V.tensor_tensor(xTl[:, 4 * g:4 * g + 4, t * P:(t + 1) * P],
                                    bank[:, xbank(t, g), :].rearrange("p (k t) -> p k t", k=4),
                                    xTh[:, 4 * g:4 * g + 4, t * P:(t + 1) * P].bitcast(F32),
                                    ALU.subtract).then_inc(xTl_rdy, 1)

            def norm(ph, last_piece):
                src, g2 = (acc, gbx) if ph == 3 else (x, gb)

                def stats(t):
                    marks = []
                    if ph < 3:
                        if t == 0:
                            dve.wait_ge(y0_ps, ph + 1)
                        else:
                            dve.wait_ge(used, last_piece)
                        for n in range(2):
                            sl = x[:, t, n * 512:(n + 1) * 512]
                            V.scalar_tensor_tensor(sl, sl, ALPHA, bank[:, 2 + 2 * t + n, :], ALU.mult,
                                                   ALU.add).then_inc(chain.sem, 1)
                            chain.k += 1
                            marks.append(chain.base + chain.k)
                    for n in range(2):
                        if marks:
                            dve.wait_ge(chain.sem, marks[n])
                        V.bn_stats(bnst[:, t, n, :], src[:, t, n * 512:(n + 1) * 512]).then_inc(chain.sem, 1)
                        chain.k += 1
                    dve.wait_ge(chain.sem, chain.base + chain.k)
                    link(V.bn_aggr(mv[:, t, :], bnst[:, t].rearrange("p a b -> p (a b)")))
                    V.tensor_scalar_add(mv[:, t, 1:2], mv[:, t, 1:2], EPS).then_inc(var_rdy, 1)

                def scale(t):
                    dve.wait_ge(gb_in, 16 * (ph + 1))
                    link(V.scalar_tensor_tensor(src[:, t, :], src[:, t, :], mv[:, t, 0:1], g2[:, 0, :],
                                                ALU.subtract, ALU.mult))
                    dve.wait_ge(std_rdy, NT * ph + t + 1)
                    link(V.reciprocal(rstd[:, t:t + 1], rstd[:, t:t + 1]))
                    V.scalar_tensor_tensor(src[:, t, :], src[:, t, :], rstd[:, t:t + 1], g2[:, 1, :],
                                           ALU.mult, ALU.add).then_inc(x_rdy, 1)

                stats(0)
                scale(0)
                stats(1)
                if ph < 3:
                    split_x(ph + 1, 0)
                scale(1)
                if ph < 3:
                    split_x(ph + 1, 1)

            def softplus():
                dve.wait_ge(par_in, 16)
                lam = par[:, :, TAPS * CT + 3 * CT:TAPS * CT + 4 * CT]
                link(V.tensor_scalar(nsp[:, 0], lam, -1.0, None, ALU.mult))
                V.tensor_tensor(nsp[:, 1], nsp[:, 0], lam, ALU.max).then_inc(nsp_rdy, 1)
                dve.wait_ge(nsp_e, 1)
                y, s, s2, q = nsp[:, 2], nsp[:, 3], nsp[:, 4], nsp[:, 1]
                link(V.tensor_scalar(s2, y, 2.0, None, ALU.add))
                link(V.reciprocal(s2, s2))
                link(V.tensor_tensor(s, y, s2, ALU.mult))
                link(V.tensor_tensor(s2, s, s, ALU.mult))
                link(V.tensor_scalar(q, s2, 1.0 / 17.0, 1.0 / 15.0, ALU.mult, ALU.add))
                for n in (13, 11, 9, 7, 5, 3, 1):
                    link(V.tensor_tensor(q, q, s2, ALU.mult))
                    link(V.tensor_scalar(q, q, 1.0 / n, None, ALU.add))
                link(V.tensor_tensor(q, q, s, ALU.mult))
                link(V.tensor_scalar(s, nsp[:, 0], 0.0, 8.0, ALU.max, ALU.mult))
                link(V.scalar_tensor_tensor(q, q, 16.0, s, ALU.mult, ALU.add))
                V.tensor_scalar(nsp[:, 0], q, -1.0, None, ALU.mult).then_inc(nsp_rdy, 1)

            def mixer(l):
                p0 = l * (MIXP + FFP)
                pl = par[:, l, :]
                V.memset(up[:, :, 0:TAPS], 0.0).then_inc(dve_step, 1)
                V.memset(kT[:, :, 0:CH], 0.0).then_inc(dve_step, 1)
                V.memset(ve[CH:P, 0, :], 0.0).then_inc(dve_step, 1)
                chain.k += 3
                dve.wait_ge(dve_step, chain.base + chain.k)
                if l == 0:
                    softplus()
                    split_x(0, 0)
                    lo(0)
                    split_x(0, 1)
                    lo(1)
                lo(p0 + 2)
                lo(p0 + 3)
                for j in range(2):
                    dve.wait_ge(u_sb, 2 * l + j + 1)
                    for tap in range(TAPS):
                        for c in (2 * j, 2 * j + 1):
                            w = pl[:, tap * CT + c:tap * CT + c + 1]
                            src = up[:, c, 1 + tap:1 + tap + T]
                            if tap == 0:
                                V.tensor_scalar(uc[:, c, :], src, w, pl[:, TAPS * CT + c:TAPS * CT + c + 1],
                                                ALU.mult, ALU.add).then_inc(chain.sem, 1)
                                chain.k += 1
                            else:
                                dve.wait_ge(chain.sem, chain.base + chain.k - 1)
                                ins = V.scalar_tensor_tensor(uc[:, c, :], src, w, uc[:, c, :], ALU.mult, ALU.add)
                                if tap == TAPS - 1:
                                    ins.then_inc(uc_rdy, 1)
                                    if c % 2 == 0:
                                        dve.wait_ge(chain.sem, chain.base + chain.k)
                                else:
                                    ins.then_inc(chain.sem, 1)
                                    chain.k += 1
                    lo(p0 + 4 + j)
                lo(p0 + 6)
                if l == 0:
                    dve.wait_ge(cs_in, 16)
                dve.wait_ge(qkv_sb, 3 * (l + 1))
                heads = qkv[:, :, 0:10 * HD].rearrange("p t (h d) -> p t h d", h=10)
                for t in range(NT):
                    for a, dst in ((0, ropa), (1, ropb)):
                        tab = cs[:, t, a, :].unsqueeze(1).broadcast_to([P, 10, ROT])
                        link(V.tensor_tensor(dst[:, t], heads[:, t, :, 0:ROT], tab, ALU.mult))
                for t in range(NT):
                    link(V.tensor_tensor(heads[:, t, :, 0:8], ropa[:, t, :, 0:8], ropb[:, t, :, 8:16], ALU.subtract))
                    link(V.tensor_tensor(heads[:, t, :, 8:16], ropa[:, t, :, 8:16], ropb[:, t, :, 0:8], ALU.add))
                    for g in range(NKV):
                        src = qkv[:, t, 512 + g * HD:512 + (g + 1) * HD].unsqueeze(1).broadcast_to([P, 2, HD])
                        link(V.tensor_copy(kd[:, t, g, :].rearrange("p (a d) -> p a d", a=2), src))
                link(V.tensor_copy(vo[:], qkv[:, :, 640:768]))
                link(V.tensor_copy(ve[0:CH, :, :], qkv[0:CH, :, 640:768]))
                V.tensor_copy(ve[CH:P, 1, :], qkv[CH:P, 0, 640:768]).then_inc(rope_rdy, 1)
                lo(p0 + 7)
                dve.wait_ge(sig_rdy, 4 * (l + 1))
                link(V.tensor_tensor(ri[:, 1], ri[:, 1], uc[:], ALU.mult))
                dve.wait_ge(at_rdy, l + 1)
                link(V.tensor_tensor(ri[:, 0], avec[:], avec[:], ALU.mult))
                V.scalar_tensor_tensor(tmp.rearrange("p c t -> p (c t)"), ri[:, 0].rearrange("p c t -> p (c t)"), 1.0,
                                       tmp.rearrange("p c t -> p (c t)"), ALU.add, ALU.mult).then_inc(v_rdy, 1)
                lo(p0 + 8)
                dve.wait_ge(sq_rdy, l + 1)
                link(V.tensor_tensor(ri[:, 1], ri[:, 1], ri[:, 0], ALU.mult))
                for c in range(CT):
                    V.tensor_tensor_scan(tmp[:, c, :], avec[:, c, :], ri[:, 1, c, :], 0.0, ALU.mult,
                                         ALU.add).then_inc(chain.sem, 1)
                    chain.k += 1
                dve.wait_ge(chain.sem, chain.base + chain.k)
                dve.wait_ge(gelu_rdy, 2 * (l + 1))
                V.tensor_tensor(tmp[:], tmp[:], gel[:], ALU.mult).then_inc(ylru_rdy, 1)
                sink = pl[:, CHANW:CHANW + 16]
                for b in range(4):
                    sc = bank[:, SB[b], :].rearrange("p (r k) -> p r k", r=4)
                    dve.wait_ge(s_ps, 4 * l + b + 1)
                    if b < 2:
                        link(V.memset(sc[0:CH, :, CH:P], -8.0e30))
                    m = sm[:, 0, 4 * b:4 * b + 4]
                    link(V.tensor_reduce(m, sc, AX, ALU.max))
                    link(V.scalar_tensor_tensor(m, m, 0.125, sink[:, 4 * b:4 * b + 4], ALU.mult, ALU.max))
                    V.tensor_scalar(sm[:, 1, 4 * b:4 * b + 4], m, -1.0, None, ALU.mult).then_inc(s_max, 1)
                V.tensor_tensor(sm[:, 3, :], sink, sm[:, 0, :], ALU.subtract).then_inc(s_max, 1)
                lo(p0 + 9)
                dve.wait_ge(yh_rdy, 3 * l + 1)
                V.tensor_tensor(al[:, 0:CT * T], tmp[:].rearrange("p c t -> p (c t)"), ah[:, 0:CT * T].bitcast(F32),
                                ALU.subtract).then_inc(yl_rdy, 1)
                dve.wait_ge(es_rdy, l + 1)
                for b in range(4):
                    dve.wait_ge(s_exp, 4 * l + b + 1)
                    d = sm[:, 2, 4 * b:4 * b + 4]
                    link(V.tensor_tensor(d, d, sm[:, 3, 4 * b:4 * b + 4], ALU.add))
                    link(V.reciprocal(d, d))
                    V.tensor_tensor(pr[:, b], pr[:, b], d.unsqueeze(2).broadcast_to([P, 4, P]),
                                    ALU.mult).then_inc(p_rdy, 1)
                for g in range(2):
                    dve.wait_ge(yh_rdy, 3 * l + 2 + g)
                    V.tensor_tensor(xTl[:, 4 + 2 * g:6 + 2 * g, :], bank[:, g, :].rearrange("p (r t) -> p r t", r=2),
                                    xTh[:, 4 + 2 * g:6 + 2 * g, :].bitcast(F32), ALU.subtract).then_inc(yl_rdy, 1)
                for j in range(3):
                    lo(p0 + 10 + j)
                if l == DEPTH - 1:
                    dve.wait_ge(rw_h, 1)
                    V.tensor_tensor(rwl, rw, rwh.bitcast(F32), ALU.subtract).then_inc(rw_l, 1)
                norm(2 * l, p0 + MIXP)

            def dense():
                for i in range(FFP):
                    if i in H_AT:
                        c = H_AT[i]
                        for t in range(NT):
                            dve.wait_ge(silu_rdy, NT * c + t + 1)
                            ins = V.tensor_tensor(hs[:, t, :], hs[:, t, :], bank[:, t, FC:2 * FC], ALU.mult)
                        ins.then_inc(h_rdy, 1)
                    if i in HT_AT:
                        c = HT_AT[i]
                        dve.wait_ge(hTh_rdy, c + 1)
                        V.tensor_tensor(htl[:], bank[:, 6:8, 0:FC], hth[:].bitcast(F32), ALU.subtract).then_inc(hTl_rdy, 1)
                    lo(MIXP + i + 2)
                norm(1, MIXP + FFP)

            mixer(0)
            dense()
            mixer(1)
            V.memset(ST[:].bitcast(F32), 0.0).then_inc(st_sb, 1)
            V.memset(wt[:], 0.0).then_inc(dve_step, 1)
            V.memset(ps_[:], 4 * BIG).then_inc(dve_step, 1)
            chain.k += 2
            dve.wait_ge(dve_step, chain.base + chain.k)
            dve.wait_ge(lg_ps, NT)
            link(V.tensor_tensor(lg[:], bank[:, 2, 0:2 * NE].rearrange("p (t e) -> p t e", t=NT),
                                 rb.unsqueeze(1).broadcast_to([P, NT, NE]), ALU.add))
            for t in range(NT):
                link(V.max(mx8[:, t, :], lg[:, t, :]))
                link(V.max_index(ix8[:, t, :].bitcast(U32), mx8[:, t, :], lg[:, t, :]))
            V.tensor_tensor(tw[:, 0, :], mx8[:, :, 1], mx8[:, :, 0], ALU.subtract).then_inc(tw_in, 1)
            link(V.tensor_copy(ixf[:], ix8[:].bitcast(U32)))
            for a in range(2):
                for t in range(NT):
                    link(V.tensor_scalar(oh[:, a, t, :], iota[:, 0:NE], ixf[:, t, a:a + 1], None, ALU.is_equal))
            V.tensor_tensor(mk[:], oh[:, 0], oh[:, 1], ALU.add).then_inc(mk_rdy, 1)
            dve.wait_ge(mk_rdy, 1)
            link(V.tensor_scalar(far[:], mk[:], -BIG, BIG, ALU.mult, ALU.add))
            dve.wait_ge(pos_ps, 1)
            link(V.tensor_tensor(ps_[:, :, 0:NE], bank[:, 3, 0:2 * NE].rearrange("p (t e) -> p t e", t=NT),
                                 far[:], ALU.add))

            def tables():
                dve.wait_ge(tw_e, 1)
                link(V.tensor_scalar(tw[:, 2, :], tw[:, 1, :], 1.0, None, ALU.add))
                link(V.reciprocal(tw[:, 2, :], tw[:, 2, :]))
                link(V.tensor_tensor(tw[:, 3, :], tw[:, 1, :], tw[:, 2, :], ALU.mult))
                for t in range(NT):
                    link(V.tensor_scalar(wt[:, t, 1:1 + NE], oh[:, 0, t, :], tw[:, 2, t:t + 1], None, ALU.mult))
                    link(V.scalar_tensor_tensor(wt[:, t, 1:1 + NE], oh[:, 1, t, :], tw[:, 3, t:t + 1],
                                                wt[:, t, 1:1 + NE], ALU.mult, ALU.add))
                link(V.tensor_copy(wt[:, :, 1 + NE:1 + 2 * NE], wt[:, :, 1:1 + NE]))
                link(V.tensor_scalar(ps_[:, :, NE:2 * NE], ps_[:, :, 0:NE], -float(P), None, ALU.add))
                link(V.tensor_reduce(cm[:, 0:1], bank[:, 3, 2 * NE:3 * NE], AX, ALU.max))
                link(V.tensor_scalar(cm[:, 0:1], cm[:, 0:1], float(P), float(NE), ALU.is_gt, ALU.mult))
                link(V.tensor_scalar(cm[:, 0:1], cm[:, 0:1], float(NE), None, ALU.add))
                V.tensor_copy(njob_i[:], cm[:, 0:1]).then_inc(tab_rdy, 1)

            def one_hot(j):
                link(V.tensor_copy(pc.unsqueeze(2), ps_[:, :, bass.ds(j, 1)]))
                for t in range(NT):
                    ins = V.tensor_scalar(S[:, t, :], iota, pc[:, t:t + 1], None, ALU.is_equal)
                ins.then_inc(S_rdy, 1)

            def split_rows(j):
                dve.wait_ge(xgh_rdy, j + 1)
                V.tensor_tensor(xgl, bank[:, 4:6, :].rearrange("p b (k s) -> p (b k) s", k=4), xgh.bitcast(F32),
                                ALU.subtract).then_inc(xgl_rdy, 1)

            def add_up(count, t, n, b):
                dve.wait_ge(sc_ps, count)
                sl = acc[:, t, n * 512:(n + 1) * 512]
                V.scalar_tensor_tensor(sl, bank[:, b, :], wc[:, t:t + 1], sl, ALU.mult, ALU.add).then_inc(acc_rdy, 1)

            one_hot(0)
            for t in range(NT):
                dve.wait_ge(xn_h, t + 1)
                V.tensor_tensor(xnl[:, t, :], x[:, t, :], xnh[:, t, :].bitcast(F32), ALU.subtract).then_inc(xn_l, 1)
            tables()
            split_rows(0)
            for t in range(NT):
                V.tensor_scalar(acc[:, t, :], x[:, t, :], ALPHA, None, ALU.mult).then_inc(acc0_rdy, 1)
            dve.wait_ge(acc0_rdy, NT)
            dve.wait_ge(tab_rdy, 1)
            njob = dve.value_load(njob_i[0:1, 0:1], min_val=NE, max_val=2 * NE)
            hb, sb0 = NCH, NT * NCH
            c0 = chain.k
            LINKS = 2
            with dve.Fori(0, njob) as j:
                chain.base, chain.k = j * LINKS + c0, 0
                for i in range(FFP):
                    if i == 0:
                        dve.wait_ge(yh_sb, j + 1)
                        V.tensor_tensor(yl[:], bank[:, 2:4, :].rearrange("p b n -> p (b n)"), yh[:].bitcast(F32),
                                        ALU.subtract).then_inc(yl_sb, 1)
                    if i == 1:
                        link(V.tensor_copy(wc.unsqueeze(2), wt[:, :, bass.ds(j, 1)]))
                    if i in H_AT:
                        c = H_AT[i]
                        dve.wait_ge(silu_rdy, j * NCH + (sb0 + c + 1))
                        V.tensor_tensor(he[:], he[:], bank[:, 0, FC:2 * FC], ALU.mult).then_inc(h_rdy, 1)
                    if i in HT_AT:
                        c = HT_AT[i]
                        dve.wait_ge(hTh_rdy, j * NCH + (hb + c + 1))
                        V.tensor_tensor(htl[:, 0, :], bank[:, 6, 0:FC], hth[:, 0, :].bitcast(F32),
                                        ALU.subtract).then_inc(hTl_rdy, 1)
                    if i in ACC_AT:
                        t = ACC_AT[i]
                        add_up(j * 4 + (2 * t + 1), t, 0, 7)
                        add_up(j * 4 + (2 * t + 2), t, 1, 1)
                    if i == S_AT:
                        dve.wait_ge(st_ps, j + 1)
                        one_hot(j + 1)
                    if i == XG_AT:
                        split_rows(j + 1)
                    for ii in ([i] if i < FFP - 2 else [] if i == FFP - 2 else [i - 1, i]):
                        q = STREAM + ii + 2
                        dve.wait_ge(hi_rdy, j * FFP + (q + 1))
                        V.tensor_tensor(wlo[:, q % SPLIT, :], raw[:, q % RING, :], whi[:, q % SPLIT, :].bitcast(F32),
                                        ALU.subtract).then_inc(lo_rdy, 1)
                assert chain.k == LINKS
            chain.sem, chain.base, chain.k = dve_tail, 0, 0
            link(V.tensor_copy(wc.unsqueeze(2), wt[:, :, bass.ds(njob, 1)]))
            for n in range(2):
                dve.wait_ge(yh_last, n + 1)
                V.tensor_tensor(yl[:, n * 512:(n + 1) * 512], bank[:, 2 + n, :], yh[:, n * 512:(n + 1) * 512].bitcast(F32),
                                ALU.subtract).then_inc(yl_last, 1)
            for n in range(2):
                for t in range(NT):
                    add_up(njob * 4 + (2 * n + t + 1), t, n, LB[2 * n + t])
            dve.wait_ge(acc_rdy, njob * 4 + 4)
            link(V.memset(rstd[:], 0.0))
            norm(3, None)


def pack_weights(v):
    W = np.empty((NPIECE, P, PW), np.float32)
    at = 0

    def ff(wg, wu, wd, at):
        g = wg.reshape(2, 4, P, NCH, FC)
        u = wu.reshape(2, 4, P, NCH, FC)
        d = wd.reshape(NCH, 2, P, D)
        for i, (kind, c) in enumerate(FFORDER):
            if kind == "D":
                W[at + i] = d[c].transpose(1, 0, 2).reshape(P, PW)
            else:
                h = "AB".index(kind)
                dst = W[at + i].reshape(P, 4, 2, FC)
                dst[:, :, 0] = g[h, :, :, c].transpose(1, 0, 2)
                dst[:, :, 1] = u[h, :, :, c].transpose(1, 0, 2)

    for l in range(DEPTH):
        wi = v["w_in"][l].reshape(KT, P, 7, 256)
        for j in (4, 0, 1, 5, 6, 2, 3):
            W[at] = wi[:, :, j].transpose(1, 0, 2).reshape(P, PW)
            at += 1
        wo = v["w_out"][l].reshape(4, 2, P, D)
        for j in range(4):
            W[at] = wo[j].transpose(1, 0, 2).reshape(P, PW)
            at += 1
        if l == 0:
            ff(v["ffn_w_gate"][0], v["ffn_w_up"][0], v["ffn_w_down"][0], at)
            at += FFP
        else:
            for e in range(NE):
                ff(v["exp_w_gate"][0, e], v["exp_w_up"][0, e], v["exp_w_down"][0, e], at)
                at += FFP
    return W


def kernel(**inputs):
    import concourse.bacc as bacc
    from concourse.bass_utils import run_bass_kernel_spmd as run

    v = {k: np.asarray(a) for k, a in inputs.items()}
    W = pack_weights(v)
    x = v["x"].reshape(NT, P, D)
    par = np.zeros((P, DEPTH, PARW), np.float32)
    wbd = np.zeros((DEPTH, P, 2, CT, P), np.float32)
    for l in range(DEPTH):
        cols = [v["conv_w"][l].reshape(TAPS * CT, P), v["conv_b"][l].reshape(CT, P), v["lru_ba"][l].reshape(CT, P),
                v["lru_bx"][l].reshape(CT, P), v["lru_lambda"][l].reshape(CT, P)]
        par[:, l, 0:CHANW] = np.concatenate(cols, 0).T
        s = v["attn_sink"][l].reshape(4, 2).T.reshape(8)
        par[:, l, CHANW:CHANW + 8] = s
        par[:, l, CHANW + 8:CHANW + 16] = s
        for g, name in enumerate(("lru_wa", "lru_wx")):
            for h in range(8):
                r = 64 * (h % 2)
                wbd[l, r:r + 64, g, h // 2, r:r + 64] = v[name][l, h]
    gb = np.empty((2 * DEPTH, P, 2, D), np.float32)
    for l in range(DEPTH):
        for a in range(2):
            gb[2 * l + a, :, 0] = v[f"ln{a + 1}_g"][l]
            gb[2 * l + a, :, 1] = v[f"ln{a + 1}_b"][l]
    cst = np.zeros((P, P + 64), np.float32)
    cst[:, 0:P] = np.eye(P)
    inv = (500000.0 ** (-np.arange(0, ROT, 2, dtype=np.float32) / np.float32(ROT))).astype(np.float32)
    ang = (np.arange(T, dtype=np.float32)[:, None] * inv[None, :]).reshape(NT, P, ROT // 2)
    tab = cst[:, P:].reshape(P, NT, 2, 2, ROT // 2)
    for a, fn in enumerate((np.cos, np.sin)):
        tab[:, :, a] = fn(ang).transpose(1, 0, 2)[:, :, None, :]
    rt = np.zeros((P, 3 * P + KT * NE + NE), np.float32)
    rt[:, 0:P] = np.triu(np.ones((P, P)), 1)
    rt[:, P:2 * P] = 1.0
    rt[:, 2 * P:3 * P] = np.arange(P)
    rt[:, 3 * P:3 * P + KT * NE] = v["router_w"][0].reshape(KT, P, NE).transpose(1, 0, 2).reshape(P, KT * NE)
    rt[:, 3 * P + KT * NE:] = v["router_b"][0]

    nc = bacc.Bacc("TRN2", target_bir_lowering=False, num_devices=1)
    arrays = {"W": W, "x_d": x, "par_d": par, "wbd_d": wbd.reshape(DEPTH, P, 1024),
              "gb_d": gb.reshape(2 * DEPTH, P, 2 * D), "cst_d": cst, "rt_d": rt}
    arrays = {k: np.ascontiguousarray(a) for k, a in arrays.items()}
    aps = [nc.dram_tensor(k, a.shape, F32, kind="ExternalInput").ap() for k, a in arrays.items()]
    out = nc.dram_tensor("out_d", (NT, P, D), F32, kind="ExternalOutput").ap()
    build(nc, *aps, out)
    r = run(nc, [arrays], core_ids=[0])
    return r.results[0]["out_d"].reshape(1, T, D)
```

```python
from contextlib import ExitStack

import numpy as np

import concourse.bass as bass
from concourse import mybir

F32 = mybir.dt.float32
F32R = mybir.dt.float32r
I32 = mybir.dt.int32
U32 = mybir.dt.uint32
ALU = mybir.AluOpType
ACT = mybir.ActivationFunctionType
AX = mybir.AxisListType.X

P = 128
T = 256
NT = T // P
D = 1024
KT = D // P
DEPTH = 2
DLRU = 512
CT = DLRU // P
TAPS = 4
HD = 64
NH = 8
NKV = 2
CH = 64
ROT = 16
F = 2816
FC = 256
NCH = F // FC
NE = 8
ALPHA = float((2 * DEPTH) ** 0.25)
EPS = 1e-5
BIG = 1.0e6

PW = 2048
RING = 11
SPLIT = 3
HW = PW // 2
MIXP = 11
FFP = 3 * NCH
STREAM = 2 * MIXP + FFP
NPIECE = STREAM + NE * FFP

FFORDER = [("A", 0), ("B", 0)]
for _c in range(1, NCH):
    FFORDER += [("A", _c), ("B", _c), ("D", _c - 1)]
FFORDER += [("D", NCH - 1)]
STEP = {kc: i for i, kc in enumerate(FFORDER)}
H_AT = {STEP[("B", c)] + 1: c for c in range(NCH)}
T_AFTER = {(STEP[("A", 1)] if c == 0 else STEP[("D", c - 1)]): c for c in range(NCH - 1)}
HT_AT = {i + 1: c for i, c in T_AFTER.items()}
T_MID = STEP[("D", NCH - 2)]

SCAT_AFTER = {3: 0, 9: 1}
ACC_AT = {4: (0, 0), 7: (0, 1), 10: (1, 0), 13: (1, 1)}
ST_AFTER = 10
ST_AT = 11
S_AT = 14
GATHER_AFTER = {17: 0, 20: 1}
XG_AT = FFP - 1

WARM = {"start": 8, "mixer": 2, "dense": 12, "last_mixer": 18, "tile": 20, "split": 9, "rank": 10, "slots": 5}

POOL_PIECES = (MIXP + 1, MIXP + FFP + 1)

CHANW = TAPS * CT + 4 * CT
PARW = CHANW + 2 * NH


class Steps:

    def __init__(self, eng, sem):
        self.eng, self.sem, self.base, self.k = eng, sem, 0, 0

    def link(self, ins):
        self.mark(ins)
        self.settle()

    def mark(self, ins):
        self.k += 1
        ins.then_inc(self.sem, 1)

    def settle(self):
        self.eng.wait_ge(self.sem, self.base + self.k)


def build(nc, W, x_d, par_d, wbd_d, gb_d, cst_d, rt_d, out_d):
    with ExitStack() as ctx:
        def sb(name, shape, dt=F32):
            return ctx.enter_context(nc.sbuf_tensor(name, shape, dt))

        def sem(name):
            return ctx.enter_context(nc.semaphore(name))

        raw = sb("raw", [P, RING, PW])
        whi = sb("whi", [P, SPLIT, PW], F32R)
        wlo = sb("wlo", [P, SPLIT, PW], F32R)
        x = sb("x", [P, NT, D])
        ah = sb("ah", [P, KT * T], F32R)
        al = sb("al", [P, KT * T], F32R)
        hth = sb("hth", [P, NT, FC], F32R)
        htl = sb("htl", [P, NT, FC], F32R)
        ident = sb("ident", [P, P])
        par = sb("par", [P, DEPTH, PARW])
        cs = sb("cs", [P, NT, 2, ROT])
        nsp = sb("nsp", [P, 5, DEPTH, CT])
        sm = sb("sm", [P, 4, 16])
        bnst = sb("bnst", [P, NT, 2, 6])
        mv = sb("mv", [P, NT, 2])
        rstd = sb("rstd", [P, NT])
        njob_i = sb("njob_i", [P, 1], I32)
        junk = sb("junk", [P, 9])
        with nc.sbuf_tensor("scr", [P, 10384], F32) as scr:
            pass
        rtab = sb("rtab", [P, 3 * P + KT * NE + NE])
        msc = sb("msc", [P, 224])
        S = sb("S", [P, NT, P], F32R)
        ST = sb("ST", [P, NT, P], F32R)
        xnh = sb("xnh", [P, NT, D], F32R)
        xnl = sb("xnl", [P, NT, D], F32R)
        he = sb("he", [P, FC])
        yh = sb("yh", [P, D], F32R)
        acc = sb("acc", [P, NT, D])
        yl = sb("yl", [P, D], F32R)

        xTh = ah[:, :].rearrange("p (k t) -> p k t", k=KT)
        xTl = al[:, :].rearrange("p (k t) -> p k t", k=KT)
        xgh = ah[:, 0:KT * P].rearrange("p (k s) -> p k s", k=KT)
        xgl = al[:, 0:KT * P].rearrange("p (k s) -> p k s", k=KT)

        def region(first, n, pat=None, **kw):
            r = scr[:, first:first + n]
            return r.rearrange(pat, **kw) if pat else r
        wbd = region(0, 1024, pat="p (g c n) -> p g c n", g=2, c=CT)
        avec = region(0, 1024, pat="p (c t) -> p c t", c=CT)
        up = region(1024, 1040, pat="p (c t) -> p c t", c=CT)
        tmp = region(1024, 1024, pat="p (c t) -> p c t", c=CT)
        uc = region(2064, 1024, pat="p (c t) -> p c t", c=CT)
        ri = region(3088, 2048, pat="p (g c t) -> p g c t", g=2, c=CT)
        pt = region(3088, 2048, pat="p (b r q) -> p b r q", b=4, r=4)
        gel = region(5136, 1024, pat="p (c t) -> p c t", c=CT)
        qkv = region(6160, 1536, pat="p (t n) -> p t n", t=NT)
        kd = region(7696, 512, pat="p (t g n) -> p t g n", t=NT, g=NKV)
        pr = region(6160, 2048, pat="p (b r k) -> p b r k", b=4, r=4)
        gb = region(6160, 2048, pat="p (a n) -> p a n", a=2)
        qT = region(8208, 1024, pat="p (r t) -> p r t", r=4)
        ropa = region(8208, 320, pat="p (t h n) -> p t h n", t=NT, h=10)
        ropb = region(8528, 320, pat="p (t h n) -> p t h n", t=NT, h=10)
        kT = region(9232, 640, pat="p (g t) -> p g t", g=NKV)
        vo = region(9872, 256, pat="p (t n) -> p t n", t=NT)
        ve = region(10128, 256, pat="p (t n) -> p t n", t=NT)
        hs = region(0, NT * FC, pat="p (t n) -> p t n", t=NT)
        tri = rtab[:, 0:P]
        ones = rtab[:, P:2 * P]
        iota = rtab[:, 2 * P:3 * P]
        rw = rtab[:, 3 * P:3 * P + KT * NE]
        rb = rtab[:, 3 * P + KT * NE:]
        rw2 = hth[:, 0, 0:KT * 2 * NE].rearrange("p (k a e) -> p k a e", k=KT, a=2)

        def small(first, n, pat=None, **kw):
            r = msc[:, first:first + n]
            return r.rearrange(pat, **kw) if pat else r
        lgs = he
        lg = small(0, 16, "p (t e) -> p t e", t=NT)
        mx8 = small(16, 16, "p (t e) -> p t e", t=NT)
        ix8 = small(32, 16, "p (t e) -> p t e", t=NT)
        ixf = small(48, 16, "p (t e) -> p t e", t=NT)
        oh = small(64, 32, "p (a t e) -> p a t e", a=2, t=NT)
        mk = small(96, 16, "p (t e) -> p t e", t=NT)
        tw = small(112, 8, "p (a t) -> p a t", a=4)
        wt = small(120, 2 * 18, "p (t e) -> p t e", t=NT)
        ps_ = small(156, 2 * 18, "p (t e) -> p t e", t=NT)
        wc = small(192, 2)
        pc = small(194, 2)
        cm = small(196, 2)
        far = small(200, 16, "p (t e) -> p t e", t=NT)
        hbuf = ((hth[:, :, :], htl[:, :, :]),
                tuple(a[:, 0:NT * FC].rearrange("p (t n) -> p t n", t=NT) for a in (yh, yl)))
        ysc = raw[:, RING - 1, D:2 * D]
        y32 = raw[:, RING - 1, 0:D]
        gbx = x[:, :, :]

        bank = ctx.enter_context(nc.psum_tensor("bank", [P, 8, 512], F32))

        raw_in = [sem(f"raw_in{s}") for s in range(RING)]
        first_in = sem("first_in")
        hi_rdy = sem("hi_rdy")
        lo_rdy = sem("lo_rdy")
        pool_lo = sem("pool_lo")
        used = sem("piece_used")
        x_in = [sem(f"x_in{t}") for t in range(NT)]
        ident_in = sem("ident_in")
        cs_in = sem("cs_in")
        par_in = sem("par_in")
        wbd_in = sem("wbd_in")
        gb_in = sem("gb_in")
        rt_in = sem("rt_in")
        warm_rdy = sem("warm_rdy")
        x_rdy = sem("x_rdy")
        xT_ps = sem("xT_ps")
        xTh_rdy = sem("xTh_rdy")
        xTl_rdy = sem("xTl_rdy")
        u_sb = sem("u_sb")
        uc_rdy = sem("uc_rdy")
        qkv_sb = sem("qkv_sb")
        gate_ps = sem("gate_ps")
        sig_rdy = sem("sig_rdy")
        gelu_rdy = sem("gelu_rdy")
        nsp_e = sem("nsp_e")
        nsp_rdy = sem("nsp_rdy")
        rope_rdy = sem("rope_rdy")
        qT_ps = sem("qT_ps")
        qT_sb = sem("qT_sb")
        at_rdy = sem("at_rdy")
        v_rdy = sem("v_rdy")
        sq_rdy = sem("sq_rdy")
        ylru_rdy = sem("ylru_rdy")
        yh_rdy = sem("yh_rdy")
        yl_rdy = sem("yl_rdy")
        s_ps = sem("s_ps")
        s_max = sem("s_max")
        s_exp = sem("s_exp")
        es_rdy = sem("es_rdy")
        y0_ps = sem("y0_ps")
        rw_h = sem("rw_h")
        rw_l = sem("rw_l")
        yh_sb = sem("yh_sb")
        xn_h = sem("xn_h")
        xn_l = sem("xn_l")
        acc0_rdy = sem("acc0_rdy")
        p_rdy = sem("p_rdy")
        pt_ps = sem("pt_ps")
        pt_sb = sem("pt_sb")
        o_ps = sem("o_ps")
        acc_done = sem("acc_done")
        wc_rdy = sem("wc_rdy")
        ysc_rdy = sem("ysc_rdy")
        acc1_rdy = sem("acc1_rdy")
        rs_rdy = sem("rs_rdy")
        xc_rdy = sem("xc_rdy")
        xs_rdy = sem("xs_rdy")
        xb_rdy = sem("xb_rdy")
        var_rdy = sem("var_rdy")
        std_rdy = sem("std_rdy")
        gu0_ps = sem("gu0_ps")
        silu_rdy = sem("silu_rdy")
        h_rdy = sem("h_rdy")
        hT_ps = sem("hT_ps")
        hTh_rdy = sem("hTh_rdy")
        hTl_rdy = sem("hTl_rdy")
        lgT_ps = sem("lgT_ps")
        lgT_sb = sem("lgT_sb")
        lg_ps = sem("lg_ps")
        tw_in = sem("tw_in")
        tw_e = sem("tw_e")
        mk_rdy = sem("mk_rdy")
        pos_ps = sem("pos_ps")
        tab_rdy = sem("tab_rdy")
        S_rdy = sem("S_rdy")
        xg_ps = sem("xg_ps")
        xgh_rdy = sem("xgh_rdy")
        xgl_rdy = sem("xgl_rdy")
        st_ps = sem("st_ps")
        st_sb = sem("st_sb")
        yl_sb = sem("yl_sb")
        sc_ps = sem("sc_ps")
        acc_rdy = sem("acc_rdy")
        dve_step = sem("dve_step")
        dve_tail = sem("dve_tail")
        yh_last = sem("yh_last")
        out_done = sem("out_done")

        block = ctx.enter_context(nc.Block())

        SB = (0, 1, 7, 6)
        LB = (7, 1, 0, 6)

        def xbank(t, g):
            return 6 * t + g

        @block.sync
        def _(sp):
            sp.dma_start(x[:, 0, :], x_d[0]).then_inc(x_in[0], 16)
            sp.dma_start(ident[:], cst_d[:, 0:P]).then_inc(ident_in, 16)
            sp.dma_start(raw[:, 0, 0:HW], W[0][:, 0:HW]).then_inc(first_in, 16)
            sp.dma_start(x[:, 1, :], x_d[1]).then_inc(x_in[1], 16)
            sp.dma_start(raw[:, 0, HW:PW], W[0][:, HW:PW]).then_inc(raw_in[0], 16)
            for s in range(1, RING):
                sp.dma_start(raw[:, s, :], W[s]).then_inc(raw_in[s], 16)
            rounds = NPIECE // RING
            with sp.Fori(1, rounds) as r:
                for s in range(RING):
                    sp.wait_ge(lo_rdy, r * (2 * RING) + 2 * (s + 1 - RING))
                    sp.dma_start(raw[:, s, :], W[bass.ds(r * RING + s, 1)].rearrange("a p n -> (a p) n")
                                 ).then_inc(raw_in[s], 16)
            sp.wait_ge(tab_rdy, 1)
            njob = sp.value_load(njob_i[0:1, 0:1], min_val=NE, max_val=2 * NE)
            with sp.If(njob > NE):
                with sp.Fori(rounds, njob * (FFP // RING) + STREAM // RING) as r:
                    for s in range(RING):
                        sp.wait_ge(lo_rdy, r * (2 * RING) + 2 * (s + 1 - RING))
                        sp.dma_start(raw[:, s, :],
                                     W[bass.ds(r * RING + (s - NE * FFP), 1)].rearrange("a p n -> (a p) n")
                                     ).then_inc(raw_in[s], 16)
            for s in range(2):
                sp.wait_ge(lo_rdy, njob * (2 * FFP) + 2 * (STREAM + s + 1 - RING))
                sp.dma_start(raw[:, s, 0:16], W[STREAM + s][:, 0:16]).then_inc(raw_in[s], 16)
            for t in range(NT):
                for n in range(2):
                    if t == 0:
                        sp.wait_ge(xb_rdy, n + 1)
                    else:
                        sp.wait_ge(x_rdy, 2 * (2 * DEPTH - 1) * NT + n + 1)
                    sp.dma_start(out_d[t][:, n * 512:(n + 1) * 512],
                                 acc[:, t, n * 512:(n + 1) * 512]).then_inc(out_done, 16)
            sp.wait_ge(out_done, 16 * 2 * NT)

        @block.gpsimd
        def _(pool):
            pool.dma_start(par[:], par_d).then_inc(par_in, 16)
            pool.dma_start(cs[:], cst_d[:, P:P + 64].rearrange("p (t a n) -> p t a n", t=NT, a=2)).then_inc(cs_in, 16)

            def low(p):
                for h in range(2):
                    pool.wait_ge(hi_rdy, 2 * p + h + 1)
                    nc.gpsimd.tensor_tensor(wlo[:, p % SPLIT, h * HW:(h + 1) * HW], raw[:, p % RING, h * HW:(h + 1) * HW],
                                            whi[:, p % SPLIT, h * HW:(h + 1) * HW].bitcast(F32),
                                            ALU.subtract).then_inc(pool_lo, 1)

            for l in range(DEPTH):
                if l:
                    pool.wait_ge(x_rdy, 4 * l * NT)
                pool.dma_start(scr[:, 0:1024], wbd_d[l]).then_inc(wbd_in, 16)
                if l == DEPTH - 1:
                    pool.wait_ge(ylru_rdy, 2 * DEPTH)
                    pool.dma_start(rtab[:], rt_d).then_inc(rt_in, 16)
                pool.wait_ge(pt_ps, 4 * (l + 1))
                pool.dma_start(gb.rearrange("p a n -> p (a n)"), gb_d[2 * l]).then_inc(gb_in, 16)
                if l == 0:
                    low(POOL_PIECES[0])
                pool.wait_ge(x_rdy, 2 * NT * (2 * l + 1))
                if l == 0:
                    pool.dma_start(gb.rearrange("p a n -> p (a n)"), gb_d[1]).then_inc(gb_in, 16)
                    low(POOL_PIECES[1])
                else:
                    pool.wait_ge(acc0_rdy, NT)
                    pool.dma_start(gbx.rearrange("p a n -> p (a n)"), gb_d[3]).then_inc(gb_in, 16)
                    pool.wait_ge(gb_in, 16 * 4)
                    for n in range(2):
                        pool.wait_ge(acc_done, 1)
                        pool.wait_ge(ysc_rdy, n + 1)
                        sl = acc[:, 1, n * 512:(n + 1) * 512]
                        nc.gpsimd.tensor_tensor(sl, sl, ysc[:, n * 512:(n + 1) * 512], ALU.add).then_inc(acc1_rdy, 1)
                    for n in range(2):
                        pool.wait_ge(xs_rdy, n + 1)
                        sl = acc[:, 0, n * 512:(n + 1) * 512]
                        nc.gpsimd.tensor_tensor(sl, sl, gbx[:, 1, n * 512:(n + 1) * 512], ALU.add).then_inc(xb_rdy, 1)

        @block.tensor
        def _(pe):
            def piece(p, h=1):
                if p in POOL_PIECES:
                    pe.wait_ge(pool_lo, 2 * POOL_PIECES.index(p) + h + 1)
                else:
                    pe.wait_ge(lo_rdy, 2 * p + h + 1)

            def transpose_x(ph, t):
                for g in range(2):
                    if ph == 0:
                        pe.wait_ge(x_in[t], 16)
                        pe.wait_ge(ident_in, 16)
                    else:
                        pe.wait_ge(x_rdy, 2 * (NT * (ph - 1) + t) + g + 1)
                    for k in range(4):
                        last = nc.tensor.transpose(bank[:, xbank(t, g), k * P:(k + 1) * P],
                                                   x[:, t, (4 * g + k) * P:(4 * g + k + 1) * P], ident[:])
                    last.then_inc(xT_ps, 1)

            def keep_warm(n, b, src=ah[:, 4 * T:4 * T + 512]):
                for _ in range(n):
                    nc.tensor.matmul(bank[:, b, :], src[:, 0:P], src, start=True, stop=True)

            def split_ready(ph, t, g):
                pe.wait_ge(xTl_rdy, 4 * ph + 2 * t + g + 1)

            def three(out, sh, sl, mh, ml, first, last):
                nc.tensor.matmul(out, sh, mh, start=first, stop=False, skip_group_check=True)
                nc.tensor.matmul(out, sh, ml, start=False, stop=False, skip_group_check=True)
                return nc.tensor.matmul(out, sl, mh, start=False, stop=last, skip_group_check=True)

            def mixer(l):
                p0 = l * (MIXP + FFP)

                def wslot(p):
                    s = p % SPLIT
                    return (whi[:, s, :].rearrange("p (k n) -> p k n", k=KT),
                            wlo[:, s, :].rearrange("p (k n) -> p k n", k=KT))

                def channels(p, b):
                    piece(p)
                    wh, wl = wslot(p)
                    for c in range(2):
                        for k in range(KT):
                            last = three(bank[:, b, c * T:(c + 1) * T], wh[:, k, c * P:(c + 1) * P],
                                         wl[:, k, c * P:(c + 1) * P], xTh[:, k, :], xTl[:, k, :], k == 0, k == KT - 1)
                            if c and k % 4 == 3:
                                last.then_inc(used, 1)

                def rows(p, b, t, first=False):
                    wh, wl = wslot(p)
                    for k in range(KT):
                        if k % 4 == 0:
                            if first:
                                split_ready(2 * l, t, k // 4)
                            piece(p, k // 4)
                        last = three(bank[:, b, t * 256:(t + 1) * 256], xTh[:, k, t * P:(t + 1) * P],
                                     xTl[:, k, t * P:(t + 1) * P], wh[:, k, :], wl[:, k, :], k == 0, k == KT - 1)
                        if t == NT - 1 and k % 4 == 3:
                            last.then_inc(used, 1)

                def gates(cp):
                    pe.wait_ge(wbd_in, 16 * (l + 1))
                    pe.wait_ge(uc_rdy, CT * l + 2 * cp + 2)
                    for g in range(2):
                        b = cp if g == 0 else 7 - cp
                        for c in range(2):
                            last = nc.tensor.matmul(bank[:, b, c * T:(c + 1) * T], wbd[:, g, 2 * cp + c, :],
                                                    uc[:, 2 * cp + c, :], start=True, stop=True)
                        last.then_inc(gate_ps, 1)

                if l == 0:
                    pe.wait_ge(warm_rdy, 1)
                    keep_warm(WARM["start"], 6)
                else:
                    keep_warm(WARM["dense"], 6)
                transpose_x(2 * l, 0)
                if l == 0:
                    transpose_x(0, 1)
                rows(p0, 2, 0, True)
                if l:
                    transpose_x(2 * l, 1)
                rows(p0, 2, 1, True)
                channels(p0 + 1, 0)
                channels(p0 + 2, 1)
                def heads(j):
                    return lambda t, k: (xTh[:, 2 * j + k, t * P:(t + 1) * P], xTl[:, 2 * j + k, t * P:(t + 1) * P])

                for t in range(NT):
                    rows(p0 + 3, 3, t)
                gates(0)
                for t in range(NT):
                    rows(p0 + 4, 4, t)
                gates(1)
                channels(p0 + 5, 5)
                pe.wait_ge(rope_rdy, l + 1)
                for b in range(2):
                    for r in range(2):
                        for t in range(NT):
                            last = nc.tensor.transpose(bank[:, 3 + b, r * T + t * P:r * T + (t + 1) * P],
                                                       qkv[:, t, (2 * b + r) * P:(2 * b + r + 1) * P], ident[:])
                    last.then_inc(qT_ps, 1)
                for g in range(NKV):
                    for t in range(NT):
                        last = nc.tensor.transpose(bank[:, 2, g * T + t * P:g * T + (t + 1) * P],
                                                   kd[:, t, g, :], ident[:])
                last.then_inc(qT_ps, 1)
                pe.wait_ge(sig_rdy, 4 * (l + 1))
                channels(p0 + 6, 6)
                pe.wait_ge(qT_sb, 3 * (l + 1))
                for b in range(4):
                    t, s = b // 2, b % 2
                    d0 = s * HD
                    if SB[b] == 6:
                        pe.wait_ge(gelu_rdy, 2 * (l + 1))
                    for r in range(4):
                        g = r // 2
                        q = 2 * t
                        dst = bank[:, SB[b], r * P:(r + 1) * P]
                        nc.tensor.matmul(dst[0:64, 0:64], qT[d0:d0 + HD, r, q * CH:(q + 1) * CH],
                                         kT[d0:d0 + HD, g, (q + 1) * CH:(q + 2) * CH],
                                         start=True, stop=True)
                        if t:
                            nc.tensor.matmul(dst[0:64, 64:128], qT[d0:d0 + HD, r, q * CH:(q + 1) * CH],
                                             kT[d0:d0 + HD, g, q * CH:(q + 1) * CH],
                                             start=True, stop=True)
                        last = nc.tensor.matmul(dst[64:128, :], qT[d0:d0 + HD, r, (q + 1) * CH:(q + 2) * CH],
                                                kT[d0:d0 + HD, g, (q + 1) * CH:(q + 3) * CH],
                                                start=True, stop=True)
                    last.then_inc(s_ps, 1)
                pe.wait_ge(gelu_rdy, 2 * l + 1)
                for j in range(2):
                    pe.wait_ge(yl_rdy, 4 * l + j + 1)
                    for t in range(NT):
                        down(p0 + 7 + j, heads(j), j == 0, False, t)
                for b in range(4):
                    pe.wait_ge(p_rdy, 4 * l + b + 1)
                    for r in range(4):
                        last = nc.tensor.transpose(bank[:, SB[b], r * P:(r + 1) * P], pr[:, b, r, :], ident[:])
                    last.then_inc(pt_ps, 1)
                for g in range(NKV):
                    for t in range(NT):
                        for s in range(2):
                            if g == 0:
                                pe.wait_ge(pt_sb, 4 * l + 2 * t + s + 1)
                            for half, v in ((0, ve), (1, vo)):
                                dst = bank[s * HD:(s + 1) * HD, g, :].rearrange("p (r t) -> p r t", r=2)
                                c0 = t * P + half * CH
                                last = nc.tensor.matmul(dst[:, :, c0:c0 + CH], v[:, t, g * HD:(g + 1) * HD],
                                                        pt[:, 2 * t + s, 2 * g:2 * g + 2, half * CH:(half + 1) * CH],
                                                        start=True, stop=True)
                    last.then_inc(o_ps, 1)
                for t in range(NT):
                    for j in range(2, 4):
                        pe.wait_ge(yl_rdy, 4 * l + j + 1)
                        down(p0 + 7 + j, heads(j), False, j == 3, t)

            def down(p, act_t, first, last_piece, t):
                for k in range(2):
                    piece(p, k)
                    last = downmm(p % SPLIT, k, act_t(t, k), first and k == 0, last_piece and k == 1, t)
                    if t == NT - 1:
                        last.then_inc(used, 1)
                if last_piece and t == 0:
                    last.then_inc(y0_ps, 1)

            def downmm(slot, k, parts, st, en, t):
                sh, sl = parts
                wh = whi[:, slot, k * HW:(k + 1) * HW]
                wl = wlo[:, slot, k * HW:(k + 1) * HW]
                for n in range(2):
                    nc.tensor.matmul(bank[:, 2 + 2 * t + n, :], sh, wh[:, n * 512:(n + 1) * 512], start=st, stop=False,
                                     skip_group_check=True)
                for n in range(2):
                    nc.tensor.matmul(bank[:, 2 + 2 * t + n, :], sh, wl[:, n * 512:(n + 1) * 512], start=False,
                                     stop=False, skip_group_check=True)
                for n in range(2):
                    last = nc.tensor.matmul(bank[:, 2 + 2 * t + n, :], sl, wh[:, n * 512:(n + 1) * 512], start=False,
                                            stop=en, skip_group_check=True)
                return last

            def gate_up(slot, half, k, th, tl, t, b):
                wh = whi[:, slot, k * 512:(k + 1) * 512]
                wl = wlo[:, slot, k * 512:(k + 1) * 512]
                kk = 4 * half + k
                return three(bank[:, b, :], th[:, kk, t * P:(t + 1) * P], tl[:, kk, t * P:(t + 1) * P],
                             wh, wl, kk == 0, kk == KT - 1)

            def transpose_h(src, nt):
                for t in range(nt):
                    for k in range(2):
                        last = nc.tensor.transpose(bank[:, 6 + t, k * P:(k + 1) * P], src(t, k), ident[:])
                last.then_inc(hT_ps, 1)

            def dense():
                def gate_up_tile(i, half, t):
                    for k in range(4):
                        if k % 2 == 0:
                            piece(MIXP + i, k // 2)
                        last = gate_up((MIXP + i) % SPLIT, half, k, xTh, xTl, t, t)
                        if i == 1 and t == 0:
                            if k == 1:
                                transpose_x(1, 1)
                            if k == 3:
                                last.then_inc(gu0_ps, 1)
                        if t == NT - 1 and k % 2:
                            last.then_inc(used, 1)

                def turn_h(c):
                    pe.wait_ge(h_rdy, NT * (c + 1))
                    if c:
                        pe.wait_ge(hTl_rdy, c)
                    transpose_h(lambda t, k: hs[:, t, k * P:(k + 1) * P], NT)

                keep_warm(WARM["mixer"], 6)
                for t in range(NT):
                    if t == 0:
                        transpose_x(1, t)
                    for half in range(2):
                        split_ready(1, t, half)
                        gate_up_tile(half, half, t)
                for i, (kind, c) in enumerate(FFORDER):
                    if i < 2:
                        continue
                    for t in range(NT):
                        if kind == "D":
                            if t == 0:
                                pe.wait_ge(hTl_rdy, c + 1)
                            hh, hl = hbuf[c % 2]
                            down(MIXP + i, lambda t, k: (hh[:, t, k * P:(k + 1) * P], hl[:, t, k * P:(k + 1) * P]),
                                 c == 0, c == NCH - 1, t)
                        else:
                            if kind == "A":
                                pe.wait_ge(h_rdy, NT * (c - 1) + t + 1)
                            gate_up_tile(i, "AB".index(kind), t)
                        if i == T_MID and t == 0:
                            turn_h(NCH - 1)
                    if i in T_AFTER:
                        turn_h(T_AFTER[i])

            def gather(b):
                for k in range(4):
                    kk = 4 * b + k
                    for n, (t, a) in enumerate(((0, xnh), (0, xnl), (1, xnh), (1, xnl))):
                        last = nc.tensor.matmul(bank[:, 4 + b, k * P:(k + 1) * P], a[:, t, kk * P:(kk + 1) * P],
                                                S[:, t, :], start=(n == 0), stop=(n == 3))
                last.then_inc(xg_ps, 1)

            def scatter(t, n, b):
                nc.tensor.matmul(bank[:, b, :], ST[:, t, :], yh[:, n * 512:(n + 1) * 512], start=True, stop=False)
                nc.tensor.matmul(bank[:, b, :], ST[:, t, :], yl[:, n * 512:(n + 1) * 512], start=False,
                                 stop=True).then_inc(sc_ps, 1)

            def router():
                keep_warm(WARM["last_mixer"], 6)
                transpose_x(3, 0)
                keep_warm(WARM["tile"], 6, htl[:, :, :].rearrange("p t n -> p (t n)"))
                transpose_x(3, 1)
                keep_warm(WARM["split"], 3, htl[:, :, :].rearrange("p t n -> p (t n)"))
                split_ready(3, 1, 1)
                pe.wait_ge(rw_l, 1)
                for k in range(KT):
                    nc.tensor.matmul(bank[0:2 * NE, 2, 0:T], rw2[:, k].rearrange("p a e -> p (a e)"), xTh[:, k, :],
                                     start=k == 0, stop=False, skip_group_check=True)
                    last = nc.tensor.matmul(bank[0:NE, 2, 0:T], rw2[:, k, 0, :], xTl[:, k, :], start=False,
                                            stop=k == KT - 1, skip_group_check=True)
                last.then_inc(lgT_ps, 1)
                pe.wait_ge(lgT_sb, 1)
                for t in range(NT):
                    nc.tensor.transpose(bank[:, 3, 3 * NE + 2 * t * NE:3 * NE + 2 * (t + 1) * NE],
                                        lgs[0:2 * NE, t * P:(t + 1) * P], ident[0:2 * NE, 0:2 * NE]).then_inc(lg_ps, 1)
                keep_warm(WARM["rank"], 4)
                pe.wait_ge(mk_rdy, 1)
                nc.tensor.matmul(bank[:, 3, 0:NE], tri, mk[:, 0, :], start=True, stop=True)
                nc.tensor.matmul(bank[:, 3, NE:2 * NE], ones, mk[:, 0, :], start=True, stop=False)
                nc.tensor.matmul(bank[:, 3, NE:2 * NE], tri, mk[:, 1, :], start=False, stop=True)
                nc.tensor.matmul(bank[:, 3, 2 * NE:3 * NE], ones, mk[:, 0, :], start=True, stop=False)
                nc.tensor.matmul(bank[:, 3, 2 * NE:3 * NE], ones, mk[:, 1, :], start=False,
                                 stop=True).then_inc(pos_ps, 1)
                keep_warm(WARM["slots"], 4)

            mixer(0)
            dense()
            mixer(1)
            router()
            pe.wait_ge(S_rdy, 1)
            pe.wait_ge(xn_l, 2)
            gather(0)
            gather(1)
            pe.wait_ge(tab_rdy, 1)
            njob = pe.value_load(njob_i[0:1, 0:1], min_val=NE, max_val=2 * NE)
            hb, sb0 = NCH, NT * NCH
            with pe.Fori(0, njob) as j:
                def turn_h(c):
                    pe.wait_ge(h_rdy, j * NCH + (sb0 + c + 1))
                    pe.wait_ge(hTl_rdy, j * NCH + (hb + c))
                    transpose_h(lambda t, k: he[:, k * P:(k + 1) * P], 1)

                for i, (kind, c) in enumerate(FFORDER):
                    slot = (STREAM + i) % SPLIT
                    for h in range(2):
                        pe.wait_ge(lo_rdy, j * (2 * FFP) + (2 * (STREAM + i) + h + 1))
                        if kind == "D":
                            if h == 0:
                                if c == 0:
                                    pe.wait_ge(yl_sb, j + 1)
                                pe.wait_ge(hTl_rdy, j * NCH + (hb + c + 1))
                            last = downmm(slot, h, (hth[:, c % 2, h * P:(h + 1) * P], htl[:, c % 2, h * P:(h + 1) * P]),
                                          c == 0 and h == 0, c == NCH - 1 and h == 1, 0)
                        else:
                            if c == 0 and h == 0:
                                pe.wait_ge(xgl_rdy, 2 * j + ("AB".index(kind) + 1))
                            for k in (2 * h, 2 * h + 1):
                                last = gate_up(slot, "AB".index(kind), k, xgh, xgl, 0, c % 2)
                        last.then_inc(used, 1)
                        if i == T_MID and h == 0:
                            turn_h(NCH - 1)
                    if i in T_AFTER:
                        turn_h(T_AFTER[i])
                    if i in SCAT_AFTER:
                        t = SCAT_AFTER[i]
                        if t == 0:
                            pe.wait_ge(yl_sb, j + 1)
                            pe.wait_ge(st_sb, j + 1)
                        else:
                            pe.wait_ge(acc_rdy, j * 4 + 2)
                        scatter(t, 0, 4)
                        scatter(t, 1, 5)
                    if i == ST_AFTER:
                        for t in range(NT):
                            last = nc.tensor.transpose(bank[:, 7, t * P:(t + 1) * P], S[:, t, :].bitcast(F32), ident[:])
                        last.then_inc(st_ps, 1)
                    if i in GATHER_AFTER:
                        pe.wait_ge(acc_rdy, j * 4 + 4)
                        pe.wait_ge(S_rdy, j + 2)
                        gather(GATHER_AFTER[i])
            pe.wait_ge(st_sb, njob + 1)
            for t in range(NT):
                for n in range(2):
                    if t == 0:
                        pe.wait_ge(yh_last, n + 1)
                    nc.tensor.matmul(bank[:, LB[2 * t + n], :], ST[:, t, :].bitcast(F32), y32[:, n * 512:(n + 1) * 512],
                                     start=True, stop=True).then_inc(sc_ps, 1)

        @block.scalar
        def _(act):
            def hi_half(p, h):
                if p == 0 and h == 0:
                    act.wait_ge(first_in, 16)
                elif p == 0 or h == 0:
                    act.wait_ge(raw_in[p % RING], 16 * (p // RING + 1))
                if p >= SPLIT:
                    act.wait_ge(used, 2 * (p - SPLIT) + h + 1)
                nc.scalar.activation(whi[:, p % SPLIT, h * HW:(h + 1) * HW], raw[:, p % RING, h * HW:(h + 1) * HW],
                                     ACT.Copy).then_inc(hi_rdy, 1)

            def hi(p):
                for h in range(2):
                    hi_half(p, h)

            def split_x(ph, t):
                for g in range(2):
                    act.wait_ge(xT_ps, 4 * ph + 2 * t + g + 1)
                    nc.scalar.activation(xTh[:, 4 * g:4 * g + 4, t * P:(t + 1) * P],
                                         bank[:, xbank(t, g), :].rearrange("p (k t) -> p k t", k=4),
                                         ACT.Copy).then_inc(xTh_rdy, 1)

            def std(ph, split):
                if ph % 2:
                    nc.scalar.activation(junk[:, ph:ph + 1], ident[:, 0:1], ACT.Sqrt)
                for t in range(NT):
                    act.wait_ge(var_rdy, NT * ph + t + 1)
                    nc.scalar.activation(rstd[:, t:t + 1], mv[:, t, 1:2], ACT.Sqrt).then_inc(std_rdy, 1)
                    if split:
                        split_x(ph + 1, t)
                    if ph == 2:
                        act.wait_ge(x_rdy, 2 * (2 * NT + t + 1))
                        nc.scalar.activation(xnh[:, t, :], x[:, t, :], ACT.Copy).then_inc(xn_h, 1)

            def mixer(l):
                p0 = l * (MIXP + FFP)
                if l == 0:
                    act.wait_ge(nsp_rdy, 1)
                    nc.scalar.activation(nsp[:, 2], nsp[:, 1], ACT.Exp, scale=-1.0).then_inc(nsp_e, 1)
                    split_x(0, 0)
                    hi_half(0, 0)
                    split_x(0, 1)
                    hi_half(0, 1)
                    hi(1)
                hi(p0 + 2)

                def rows_out(j, b, o):
                    act.wait_ge(used, 2 * (p0 + j + 1))
                    nc.scalar.activation(qkv[:, :, o * 256:(o + 1) * 256],
                                         bank[:, b, :].rearrange("p (t n) -> p t n", t=NT),
                                         ACT.Copy).then_inc(qkv_sb, 1)
                    hi(p0 + j + 3)

                def sigmoids(cp):
                    for g in range(2):
                        b = cp if g == 0 else 7 - cp
                        act.wait_ge(gate_ps, 4 * l + 2 * cp + g + 1)
                        for c in range(2):
                            o = TAPS * CT + (1 + g) * CT + 2 * cp + c
                            last = nc.scalar.activation(ri[:, g, 2 * cp + c, :], bank[:, b, c * T:(c + 1) * T],
                                                        ACT.Sigmoid, bias=par[:, l, o:o + 1])
                        last.then_inc(sig_rdy, 1)

                rows_out(0, 2, 0)
                for j in range(2):
                    act.wait_ge(used, 2 * (p0 + j + 2))
                    nc.scalar.activation(up[:, 2 * j:2 * j + 2, TAPS:TAPS + T],
                                         bank[:, j, :].rearrange("p (c t) -> p c t", c=2), ACT.Copy).then_inc(u_sb, 1)
                    hi(p0 + 4 + j)
                rows_out(3, 3, 1)
                sigmoids(0)
                rows_out(4, 4, 2)
                sigmoids(1)
                act.wait_ge(nsp_rdy, 2)
                act.wait_ge(sig_rdy, 4 * (l + 1))
                for c in range(CT):
                    nc.scalar.activation(avec[:, c, :], ri[:, 0, c, :], ACT.Exp, scale=nsp[:, 0, l, c:c + 1])
                for c in range(CT):
                    last = nc.scalar.activation(tmp[:, c, :], ri[:, 0, c, :], ACT.Tanh, scale=nsp[:, 1, l, c:c + 1])
                last.then_inc(at_rdy, 1)
                nc.scalar.activation(junk[:, 7 + l:8 + l], ident[:, 0:1], ACT.Sqrt)

                def gelu(j):
                    act.wait_ge(used, 2 * (p0 + 6 + j))
                    nc.scalar.activation(gel[:, 2 * j:2 * j + 2, :],
                                         bank[:, 5 + j, :].rearrange("p (c t) -> p c t", c=2),
                                         ACT.Gelu_apprx_tanh).then_inc(gelu_rdy, 1)
                for b in range(2):
                    act.wait_ge(qT_ps, 3 * l + b + 1)
                    nc.scalar.activation(qT[:, 2 * b:2 * b + 2, :], bank[:, 3 + b, :].rearrange("p (r t) -> p r t", r=2),
                                         ACT.Copy).then_inc(qT_sb, 1)
                act.wait_ge(qT_ps, 3 * l + 3)
                nc.scalar.activation(kT[:, :, CH:CH + T], bank[:, 2, :].rearrange("p (g t) -> p g t", g=NKV),
                                     ACT.Copy).then_inc(qT_sb, 1)
                act.wait_ge(v_rdy, l + 1)
                nc.scalar.activation(ri[:, 0], tmp[:], ACT.Sqrt).then_inc(sq_rdy, 1)
                gelu(0)
                act.wait_ge(used, 2 * (p0 + 7))
                for g in range(2):
                    act.wait_ge(ylru_rdy, 2 * l + g + 1)
                    nc.scalar.activation(xTh[:, 2 * g:2 * g + 2, :], tmp[:, 2 * g:2 * g + 2, :],
                                         ACT.Copy).then_inc(yh_rdy, 1)
                    if g == 0:
                        gelu(1)
                hi(p0 + 8)
                for b in range(4):
                    act.wait_ge(s_max, 5 * l + b + 1)
                    for r in range(4):
                        n = 4 * b + r
                        last = nc.scalar.activation(pr[:, b, r, :], bank[:, SB[b], r * P:(r + 1) * P], ACT.Exp,
                                                    bias=sm[:, 1, n:n + 1], scale=0.125, accum_out=sm[:, 2, n:n + 1])
                    last.then_inc(s_exp, 1)
                    if b == 0:
                        act.wait_ge(s_max, 5 * l + 5)
                        nc.scalar.activation(sm[:, 3, :], sm[:, 3, :], ACT.Exp).then_inc(es_rdy, 1)
                hi(p0 + 9)
                for b in range(4):
                    act.wait_ge(pt_ps, 4 * l + b + 1)
                    nc.scalar.activation(pt[:, b], bank[:, SB[b], :].rearrange("p (r q) -> p r q", r=4),
                                         ACT.Copy).then_inc(pt_sb, 1)
                for g in range(2):
                    act.wait_ge(o_ps, 2 * l + g + 1)
                    nc.scalar.activation(xTh[:, 4 + 2 * g:6 + 2 * g, :],
                                         bank[:, g, :].rearrange("p (r t) -> p r t", r=2), ACT.Copy).then_inc(yh_rdy, 1)
                for j in range(2):
                    hi(p0 + 10 + j)
                nc.scalar.activation(junk[:, 2 * l:2 * l + 1], ident[:, 0:1], ACT.Sqrt)
                hi(p0 + 12)
                if l == DEPTH - 1:
                    act.wait_ge(rt_in, 16)
                    nc.scalar.activation(rw2[:, :, 0, :], rw.rearrange("p (k e) -> p k e", k=KT),
                                         ACT.Copy).then_inc(rw_h, 1)
                std(2 * l, True)

            def dense():
                def high_h(c):
                    act.wait_ge(hT_ps, c + 1)
                    nc.scalar.activation(hbuf[c % 2][0], bank[:, 6:8, 0:FC], ACT.Copy).then_inc(hTh_rdy, 1)

                nc.scalar.activation(junk[:, 4:5], ident[:, 0:1], ACT.Silu)
                for i in range(FFP):
                    if i == 0:
                        act.wait_ge(gu0_ps, 1)
                        nc.scalar.activation(hs[:, 0, :], bank[:, 0, 0:FC], ACT.Silu).then_inc(silu_rdy, 1)
                    if i in H_AT:
                        c = H_AT[i]
                        act.wait_ge(used, 2 * (MIXP + STEP[("B", c)] + 1))
                        if c:
                            act.wait_ge(hT_ps, c)
                        for t in range(0 if c else 1, NT):
                            nc.scalar.activation(hs[:, t, :], bank[:, t, 0:FC], ACT.Silu).then_inc(silu_rdy, 1)
                    if i in HT_AT:
                        high_h(HT_AT[i])
                    hi_half(MIXP + i + 2, 0)
                    if i == T_MID:
                        high_h(NCH - 1)
                    hi_half(MIXP + i + 2, 1)
                std(1, True)

            mixer(0)
            dense()
            mixer(1)
            act.wait_ge(lgT_ps, 1)
            nc.scalar.activation(lgs[0:2 * NE, :], bank[0:2 * NE, 2, 0:T], ACT.Copy).then_inc(lgT_sb, 1)
            nc.scalar.activation(junk[:, 6:7], ident[:, 0:1], ACT.Exp)
            act.wait_ge(tw_in, 1)
            nc.scalar.activation(tw[:, 1, :], tw[:, 0, :], ACT.Exp).then_inc(tw_e, 1)
            for t in range(NT):
                nc.scalar.activation(acc[:, t, :], x[:, t, :], ACT.Copy, scale=ALPHA).then_inc(acc0_rdy, 1)

            def split_rows(j):
                for b in range(2):
                    act.wait_ge(xg_ps, 2 * j + (b + 1))
                    nc.scalar.activation(xgh[:, 4 * b:4 * b + 4], bank[:, 4 + b, :].rearrange("p (k s) -> p k s", k=4),
                                         ACT.Copy).then_inc(xgh_rdy, 1)

            split_rows(0)
            act.wait_ge(tab_rdy, 1)
            njob = act.value_load(njob_i[0:1, 0:1], min_val=NE, max_val=2 * NE)
            hb = NCH
            with act.Fori(0, njob) as j:
                def high_h(c):
                    act.wait_ge(hT_ps, j * NCH + (hb + c + 1))
                    nc.scalar.activation(hth[:, c % 2, :], bank[:, 6, 0:FC], ACT.Copy).then_inc(hTh_rdy, 1)

                def silu(c):
                    act.wait_ge(used, j * (2 * FFP) + 2 * (STREAM + STEP[("B", c)] + 1))
                    act.wait_ge(hT_ps, j * NCH + (hb + c))
                    nc.scalar.activation(he[:], bank[:, c % 2, 0:FC], ACT.Silu).then_inc(silu_rdy, 1)

                nc.scalar.activation(junk[:, 5:6], ident[:, 0:1], ACT.Silu)
                for i in range(FFP):
                    if i == 0:
                        act.wait_ge(used, j * (2 * FFP) + 2 * STREAM)
                        nc.scalar.activation(yh[:], bank[:, 2:4, :].rearrange("p b n -> p (b n)"),
                                             ACT.Copy).then_inc(yh_sb, 1)
                    if i in H_AT and H_AT[i]:
                        silu(H_AT[i])
                    if i in HT_AT:
                        high_h(HT_AT[i])
                    if i == ST_AT:
                        act.wait_ge(st_ps, j + 1)
                        nc.scalar.activation(ST[:], bank[:, 7, 0:2 * P].rearrange("p (t n) -> p t n", t=NT),
                                             ACT.Copy).then_inc(st_sb, 1)
                    if i == XG_AT:
                        split_rows(j + 1)
                    q = STREAM + i + 2
                    act.wait_ge(raw_in[q % RING], j * (16 * FFP // RING) + 16 * (q // RING + 1))
                    for h in range(2):
                        act.wait_ge(used, j * (2 * FFP) + (2 * (q - SPLIT) + h + 1))
                        nc.scalar.activation(whi[:, q % SPLIT, h * HW:(h + 1) * HW],
                                             raw[:, q % RING, h * HW:(h + 1) * HW], ACT.Copy).then_inc(hi_rdy, 1)
                        if i == T_MID and h == 0:
                            high_h(NCH - 1)
                        if i == 1 and h == 0:
                            silu(0)
            act.wait_ge(used, njob * (2 * FFP) + 2 * STREAM)
            for n in range(2):
                nc.scalar.activation(y32[:, n * 512:(n + 1) * 512], bank[:, 2 + n, :], ACT.Copy).then_inc(yh_last, 1)
            nc.scalar.activation(junk[:, 3:4], ident[:, 0:1], ACT.Sqrt)
            for n in range(2):
                act.wait_ge(sc_ps, njob * 4 + (2 + n + 1))
                act.wait_ge(wc_rdy, 1)
                nc.scalar.activation(ysc[:, n * 512:(n + 1) * 512], bank[:, LB[2 + n], :], ACT.Copy,
                                     scale=wc[:, 1:2]).then_inc(ysc_rdy, 1)
            act.wait_ge(var_rdy, 3 * NT + 1)
            nc.scalar.activation(rstd[:, 0:1], mv[:, 0, 1:2], ACT.Sqrt).then_inc(std_rdy, 1)
            act.wait_ge(rs_rdy, 1)
            for n in range(2):
                act.wait_ge(xc_rdy, n + 1)
                sl = acc[:, 0, n * 512:(n + 1) * 512]
                nc.scalar.activation(sl, sl, ACT.Copy, scale=rstd[:, 0:1]).then_inc(xs_rdy, 1)
            act.wait_ge(var_rdy, 3 * NT + 2)
            nc.scalar.activation(rstd[:, 1:2], mv[:, 1, 1:2], ACT.Sqrt).then_inc(std_rdy, 1)

        @block.vector
        def _(dve):
            chain = Steps(dve, dve_step)
            link = chain.link
            V = nc.vector

            def lo_half(p, h):
                after_pool = h == 0 and p - 1 in POOL_PIECES
                if after_pool:
                    dve.wait_ge(pool_lo, 2 * POOL_PIECES.index(p - 1) + 2)
                dve.wait_ge(hi_rdy, 2 * p + h + 1)
                V.tensor_tensor(wlo[:, p % SPLIT, h * HW:(h + 1) * HW], raw[:, p % RING, h * HW:(h + 1) * HW],
                                whi[:, p % SPLIT, h * HW:(h + 1) * HW].bitcast(F32),
                                ALU.subtract).then_inc(lo_rdy, 3 if after_pool else 1)

            def lo(p):
                for h in range(2):
                    lo_half(p, h)

            def split_x(ph, t):
                for g in range(2):
                    dve.wait_ge(xTh_rdy, 4 * ph + 2 * t + g + 1)
                    V.tensor_tensor(xTl[:, 4 * g:4 * g + 4, t * P:(t + 1) * P],
                                    bank[:, xbank(t, g), :].rearrange("p (k t) -> p k t", k=4),
                                    xTh[:, 4 * g:4 * g + 4, t * P:(t + 1) * P].bitcast(F32),
                                    ALU.subtract).then_inc(xTl_rdy, 1)

            def low_x(t):
                dve.wait_ge(xn_h, t + 1)
                V.tensor_tensor(xnl[:, t, :], x[:, t, :], xnh[:, t, :].bitcast(F32), ALU.subtract).then_inc(xn_l, 1)

            def norm(ph, last_piece):
                src, g2 = (acc, gbx) if ph == 3 else (x, gb)

                def residual(t):
                    if t == 0:
                        dve.wait_ge(y0_ps, ph + 1)
                    else:
                        dve.wait_ge(used, 2 * last_piece)
                    marks = []
                    for n in range(2):
                        sl = x[:, t, n * 512:(n + 1) * 512]
                        V.scalar_tensor_tensor(sl, sl, ALPHA, bank[:, 2 + 2 * t + n, :], ALU.mult,
                                               ALU.add).then_inc(chain.sem, 1)
                        chain.k += 1
                        marks.append(chain.base + chain.k)
                    return marks

                def stats(t, marks):
                    for n in range(2):
                        if marks:
                            dve.wait_ge(chain.sem, marks[n])
                        V.bn_stats(bnst[:, t, n, :], src[:, t, n * 512:(n + 1) * 512]).then_inc(chain.sem, 1)
                        chain.k += 1
                    dve.wait_ge(chain.sem, chain.base + chain.k)
                    link(V.bn_aggr(mv[:, t, :], bnst[:, t].rearrange("p a b -> p (a b)")))
                    V.tensor_scalar_add(mv[:, t, 1:2], mv[:, t, 1:2], EPS).then_inc(var_rdy, 1)

                def scale(t):
                    dve.wait_ge(gb_in, 16 * (ph + 1))
                    marks = []
                    for n in range(2):
                        sl = src[:, t, n * 512:(n + 1) * 512]
                        V.scalar_tensor_tensor(sl, sl, mv[:, t, 0:1], g2[:, 0, n * 512:(n + 1) * 512],
                                               ALU.subtract, ALU.mult).then_inc(chain.sem, 1)
                        chain.k += 1
                        marks.append(chain.base + chain.k)
                    dve.wait_ge(std_rdy, NT * ph + t + 1)
                    link(V.reciprocal(rstd[:, t:t + 1], rstd[:, t:t + 1]))
                    for n in range(2):
                        sl = src[:, t, n * 512:(n + 1) * 512]
                        dve.wait_ge(chain.sem, marks[n])
                        V.scalar_tensor_tensor(sl, sl, rstd[:, t:t + 1], g2[:, 1, n * 512:(n + 1) * 512],
                                               ALU.mult, ALU.add).then_inc(x_rdy, 1)

                if ph == 3:
                    return stats, scale
                stats(0, residual(0))
                scale(0)
                marks = residual(1)
                if ph < 2:
                    split_x(ph + 1, 0)
                stats(1, marks)
                scale(1)
                if ph == 2:
                    split_x(ph + 1, 0)
                split_x(ph + 1, 1)
                if ph == 2:
                    for t in range(NT):
                        low_x(t)

            def softplus():
                dve.wait_ge(par_in, 16)
                lam = par[:, :, TAPS * CT + 3 * CT:TAPS * CT + 4 * CT]
                link(V.tensor_scalar(nsp[:, 0], lam, -1.0, None, ALU.mult))
                V.tensor_tensor(nsp[:, 1], nsp[:, 0], lam, ALU.max).then_inc(nsp_rdy, 1)

            def softplus_series():
                dve.wait_ge(nsp_e, 1)
                y, s, s2, q = nsp[:, 2], nsp[:, 3], nsp[:, 4], nsp[:, 1]
                link(V.tensor_scalar(s2, y, 2.0, None, ALU.add))
                link(V.reciprocal(s2, s2))
                link(V.tensor_tensor(s, y, s2, ALU.mult))
                link(V.tensor_tensor(s2, s, s, ALU.mult))
                link(V.tensor_scalar(q, s2, 1.0 / 17.0, 1.0 / 15.0, ALU.mult, ALU.add))
                for n in (13, 11, 9, 7, 5, 3, 1):
                    link(V.tensor_tensor(q, q, s2, ALU.mult))
                    link(V.tensor_scalar(q, q, 1.0 / n, None, ALU.add))
                link(V.tensor_tensor(q, q, s, ALU.mult))
                link(V.tensor_scalar(s, nsp[:, 0], 0.0, 8.0, ALU.max, ALU.mult))
                link(V.scalar_tensor_tensor(q, q, 16.0, s, ALU.mult, ALU.add))
                V.tensor_scalar(nsp[:, 0], q, -1.0, None, ALU.mult).then_inc(nsp_rdy, 1)

            def mixer(l):
                p0 = l * (MIXP + FFP)
                pl = par[:, l, :]
                if l == 0:
                    V.memset(ah[:, 4 * T:4 * T + 512].bitcast(F32), 0.0).then_inc(warm_rdy, 1)
                V.memset(up[:, :, 0:TAPS], 0.0).then_inc(dve_step, 1)
                V.memset(kT[:, :, 0:CH], 0.0).then_inc(dve_step, 1)
                V.memset(ve[CH:P, 0, :], 0.0).then_inc(dve_step, 1)
                chain.k += 3
                dve.wait_ge(dve_step, chain.base + chain.k)
                if l == 0:
                    softplus()
                    split_x(0, 0)
                    lo_half(0, 0)
                    split_x(0, 1)
                    lo_half(0, 1)
                    lo(1)
                lo(p0 + 2)
                if l == 0:
                    softplus_series()
                lo(p0 + 3)
                for j in range(2):
                    dve.wait_ge(u_sb, 2 * l + j + 1)
                    for tap in range(TAPS):
                        for c in (2 * j, 2 * j + 1):
                            w = pl[:, tap * CT + c:tap * CT + c + 1]
                            src = up[:, c, 1 + tap:1 + tap + T]
                            if tap == 0:
                                V.tensor_scalar(uc[:, c, :], src, w, pl[:, TAPS * CT + c:TAPS * CT + c + 1],
                                                ALU.mult, ALU.add).then_inc(chain.sem, 1)
                                chain.k += 1
                            else:
                                dve.wait_ge(chain.sem, chain.base + chain.k - 1)
                                ins = V.scalar_tensor_tensor(uc[:, c, :], src, w, uc[:, c, :], ALU.mult, ALU.add)
                                if tap == TAPS - 1:
                                    ins.then_inc(uc_rdy, 1)
                                    if c % 2 == 0:
                                        dve.wait_ge(chain.sem, chain.base + chain.k)
                                else:
                                    ins.then_inc(chain.sem, 1)
                                    chain.k += 1
                    lo(p0 + 4 + j)
                lo(p0 + 6)
                if l == 0:
                    dve.wait_ge(cs_in, 16)
                dve.wait_ge(qkv_sb, 3 * (l + 1))
                heads = qkv[:, :, 0:10 * HD].rearrange("p t (h d) -> p t h d", h=10)
                for t in range(NT):
                    for a, dst in ((0, ropa), (1, ropb)):
                        tab = cs[:, t, a, :].unsqueeze(1).broadcast_to([P, 10, ROT])
                        link(V.tensor_tensor(dst[:, t], heads[:, t, :, 0:ROT], tab, ALU.mult))
                for t in range(NT):
                    link(V.tensor_tensor(heads[:, t, :, 0:8], ropa[:, t, :, 0:8], ropb[:, t, :, 8:16], ALU.subtract))
                    link(V.tensor_tensor(heads[:, t, :, 8:16], ropa[:, t, :, 8:16], ropb[:, t, :, 0:8], ALU.add))
                    for g in range(NKV):
                        src = qkv[:, t, 512 + g * HD:512 + (g + 1) * HD].unsqueeze(1).broadcast_to([P, 2, HD])
                        link(V.tensor_copy(kd[:, t, g, :].rearrange("p (a d) -> p a d", a=2), src))
                link(V.tensor_copy(vo[:], qkv[:, :, 640:768]))
                link(V.tensor_copy(ve[0:CH, :, :], qkv[0:CH, :, 640:768]))
                V.tensor_copy(ve[CH:P, 1, :], qkv[CH:P, 0, 640:768]).then_inc(rope_rdy, 1)
                lo(p0 + 7)
                dve.wait_ge(sig_rdy, 4 * (l + 1))
                link(V.tensor_tensor(ri[:, 1], ri[:, 1], uc[:], ALU.mult))
                dve.wait_ge(at_rdy, l + 1)
                link(V.tensor_tensor(ri[:, 0], avec[:], avec[:], ALU.mult))
                V.scalar_tensor_tensor(tmp.rearrange("p c t -> p (c t)"), ri[:, 0].rearrange("p c t -> p (c t)"), 1.0,
                                       tmp.rearrange("p c t -> p (c t)"), ALU.add, ALU.mult).then_inc(v_rdy, 1)
                def low_y(g):
                    dve.wait_ge(yh_rdy, 4 * l + g + 1)
                    V.tensor_tensor(xTl[:, 2 * g:2 * g + 2, :], tmp[:, 2 * g:2 * g + 2, :],
                                    xTh[:, 2 * g:2 * g + 2, :].bitcast(F32), ALU.subtract).then_inc(yl_rdy, 1)

                dve.wait_ge(sq_rdy, l + 1)
                link(V.tensor_tensor(ri[:, 1], ri[:, 1], ri[:, 0], ALU.mult))
                for g in range(2):
                    for c in (2 * g, 2 * g + 1):
                        V.tensor_tensor_scan(tmp[:, c, :], avec[:, c, :], ri[:, 1, c, :], 0.0, ALU.mult,
                                             ALU.add).then_inc(chain.sem, 1)
                        chain.k += 1
                    if g:
                        low_y(0)
                    dve.wait_ge(chain.sem, chain.base + chain.k)
                    dve.wait_ge(gelu_rdy, 2 * l + g + 1)
                    V.tensor_tensor(tmp[:, 2 * g:2 * g + 2, :], tmp[:, 2 * g:2 * g + 2, :], gel[:, 2 * g:2 * g + 2, :],
                                    ALU.mult).then_inc(ylru_rdy, 1)
                sink = pl[:, CHANW:CHANW + 16]
                for b in range(4):
                    if b == 1:
                        low_y(1)
                        lo(p0 + 8)
                    sc = bank[:, SB[b], :].rearrange("p (r k) -> p r k", r=4)
                    dve.wait_ge(s_ps, 4 * l + b + 1)
                    if b < 2:
                        link(V.memset(sc[0:CH, :, CH:P], -8.0e30))
                    m = sm[:, 0, 4 * b:4 * b + 4]
                    link(V.tensor_reduce(m, sc, AX, ALU.max))
                    link(V.scalar_tensor_tensor(m, m, 0.125, sink[:, 4 * b:4 * b + 4], ALU.mult, ALU.max))
                    V.tensor_scalar(sm[:, 1, 4 * b:4 * b + 4], m, -1.0, None, ALU.mult).then_inc(s_max, 1)
                V.tensor_tensor(sm[:, 3, :], sink, sm[:, 0, :], ALU.subtract).then_inc(s_max, 1)
                dve.wait_ge(es_rdy, l + 1)
                for b in range(4):
                    dve.wait_ge(s_exp, 4 * l + b + 1)
                    d = sm[:, 2, 4 * b:4 * b + 4]
                    link(V.tensor_tensor(d, d, sm[:, 3, 4 * b:4 * b + 4], ALU.add))
                    link(V.reciprocal(d, d))
                    V.tensor_tensor(pr[:, b], pr[:, b], d.unsqueeze(2).broadcast_to([P, 4, P]),
                                    ALU.mult).then_inc(p_rdy, 1)
                lo(p0 + 9)
                if l == DEPTH - 1:
                    V.memset(ST[:].bitcast(F32), 0.0).then_inc(st_sb, 1)
                    chain.mark(V.memset(wt[:], 0.0))
                    link(V.memset(ps_[:], 4 * BIG))
                for g in range(2):
                    dve.wait_ge(yh_rdy, 4 * l + 3 + g)
                    V.tensor_tensor(xTl[:, 4 + 2 * g:6 + 2 * g, :], bank[:, g, :].rearrange("p (r t) -> p r t", r=2),
                                    xTh[:, 4 + 2 * g:6 + 2 * g, :].bitcast(F32), ALU.subtract).then_inc(yl_rdy, 1)
                for j in range(2):
                    lo(p0 + 10 + j)
                if l == DEPTH - 1:
                    dve.wait_ge(rw_h, 1)
                    V.tensor_tensor(rw2[:, :, 1, :], rw.rearrange("p (k e) -> p k e", k=KT),
                                    rw2[:, :, 0, :].bitcast(F32), ALU.subtract).then_inc(rw_l, 1)
                norm(2 * l, p0 + MIXP)

            def dense():
                def low_h(c):
                    dve.wait_ge(hTh_rdy, c + 1)
                    hh, hl = hbuf[c % 2]
                    V.tensor_tensor(hl, bank[:, 6:8, 0:FC], hh.bitcast(F32), ALU.subtract).then_inc(hTl_rdy, 1)

                for i in range(FFP):
                    tiles = [0] if i == 0 else [] if i not in H_AT else range(0 if H_AT[i] else 1, NT)
                    for t in tiles:
                        dve.wait_ge(silu_rdy, NT * H_AT.get(i, 0) + t + 1)
                        V.tensor_tensor(hs[:, t, :], hs[:, t, :], bank[:, t, FC:2 * FC], ALU.mult).then_inc(h_rdy, 1)
                    if i in HT_AT:
                        low_h(HT_AT[i])
                    if MIXP + i + 2 in POOL_PIECES:
                        continue
                    lo_half(MIXP + i + 2, 0)
                    if i == T_MID:
                        low_h(NCH - 1)
                    lo_half(MIXP + i + 2, 1)
                norm(1, MIXP + FFP)

            mixer(0)
            dense()
            mixer(1)
            dve.wait_ge(lg_ps, NT)
            parts = bank[:, 3, 3 * NE:7 * NE].rearrange("p (t a e) -> p t a e", t=NT, a=2)
            link(V.tensor_tensor(lg[:], parts[:, :, 1], rb.unsqueeze(1).broadcast_to([P, NT, NE]), ALU.add))
            link(V.tensor_tensor(lg[:], parts[:, :, 0], lg[:], ALU.add))
            for t in range(NT):
                chain.mark(V.max(mx8[:, t, :], lg[:, t, :]))
            chain.settle()
            for t in range(NT):
                chain.mark(V.max_index(ix8[:, t, :].bitcast(U32), mx8[:, t, :], lg[:, t, :]))
            chain.settle()
            V.tensor_tensor(tw[:, 0, :], mx8[:, :, 1], mx8[:, :, 0], ALU.subtract).then_inc(tw_in, 1)
            link(V.tensor_copy(ixf[:], ix8[:].bitcast(U32)))
            for a in range(2):
                for t in range(NT):
                    chain.mark(V.tensor_scalar(oh[:, a, t, :], iota[:, 0:NE], ixf[:, t, a:a + 1], None, ALU.is_equal))
            chain.settle()
            V.tensor_tensor(mk[:], oh[:, 0], oh[:, 1], ALU.add).then_inc(mk_rdy, 1)
            dve.wait_ge(mk_rdy, 1)
            link(V.tensor_scalar(far[:], mk[:], -BIG, BIG, ALU.mult, ALU.add))
            dve.wait_ge(pos_ps, 1)
            link(V.tensor_tensor(ps_[:, :, 0:NE], bank[:, 3, 0:2 * NE].rearrange("p (t e) -> p t e", t=NT),
                                 far[:], ALU.add))

            def tables():
                dve.wait_ge(tw_e, 1)
                link(V.tensor_scalar(tw[:, 2, :], tw[:, 1, :], 1.0, None, ALU.add))
                link(V.reciprocal(tw[:, 2, :], tw[:, 2, :]))
                link(V.tensor_tensor(tw[:, 3, :], tw[:, 1, :], tw[:, 2, :], ALU.mult))
                for t in range(NT):
                    link(V.tensor_scalar(wt[:, t, 1:1 + NE], oh[:, 0, t, :], tw[:, 2, t:t + 1], None, ALU.mult))
                    link(V.scalar_tensor_tensor(wt[:, t, 1:1 + NE], oh[:, 1, t, :], tw[:, 3, t:t + 1],
                                                wt[:, t, 1:1 + NE], ALU.mult, ALU.add))
                link(V.tensor_copy(wt[:, :, 1 + NE:1 + 2 * NE], wt[:, :, 1:1 + NE]))
                link(V.tensor_scalar(ps_[:, :, NE:2 * NE], ps_[:, :, 0:NE], -float(P), None, ALU.add))
                link(V.tensor_reduce(cm[:, 0:1], bank[:, 3, 2 * NE:3 * NE], AX, ALU.max))
                link(V.tensor_scalar(cm[:, 0:1], cm[:, 0:1], float(P), float(NE), ALU.is_gt, ALU.mult))
                link(V.tensor_scalar(cm[:, 0:1], cm[:, 0:1], float(NE), None, ALU.add))
                V.tensor_copy(njob_i[:], cm[:, 0:1]).then_inc(tab_rdy, 1)

            def one_hot(j):
                link(V.tensor_copy(pc.unsqueeze(2), ps_[:, :, bass.ds(j, 1)]))
                for t in range(NT):
                    ins = V.tensor_scalar(S[:, t, :], iota, pc[:, t:t + 1], None, ALU.is_equal)
                ins.then_inc(S_rdy, 1)

            def split_rows(j):
                for b in range(2):
                    dve.wait_ge(xgh_rdy, 2 * j + (b + 1))
                    V.tensor_tensor(xgl[:, 4 * b:4 * b + 4], bank[:, 4 + b, :].rearrange("p (k s) -> p k s", k=4),
                                    xgh[:, 4 * b:4 * b + 4].bitcast(F32), ALU.subtract).then_inc(xgl_rdy, 1)

            def add_up(count, t, n, b):
                dve.wait_ge(sc_ps, count)
                sl = acc[:, t, n * 512:(n + 1) * 512]
                V.scalar_tensor_tensor(sl, bank[:, b, :], wc[:, t:t + 1], sl, ALU.mult, ALU.add).then_inc(acc_rdy, 1)

            one_hot(0)
            tables()
            split_rows(0)
            lo(STREAM + 1)
            dve.wait_ge(acc0_rdy, NT)
            dve.wait_ge(tab_rdy, 1)
            njob = dve.value_load(njob_i[0:1, 0:1], min_val=NE, max_val=2 * NE)
            hb, sb0 = NCH, NT * NCH
            c0 = chain.k
            LINKS = 2
            with dve.Fori(0, njob) as j:
                chain.base, chain.k = j * LINKS + c0, 0
                def make_h(c):
                    dve.wait_ge(silu_rdy, j * NCH + (sb0 + c + 1))
                    V.tensor_tensor(he[:], he[:], bank[:, c % 2, FC:2 * FC], ALU.mult).then_inc(h_rdy, 1)

                def low_h(c):
                    dve.wait_ge(hTh_rdy, j * NCH + (hb + c + 1))
                    V.tensor_tensor(htl[:, c % 2, :], bank[:, 6, 0:FC], hth[:, c % 2, :].bitcast(F32),
                                    ALU.subtract).then_inc(hTl_rdy, 1)

                for i in range(FFP):
                    if i == 0:
                        dve.wait_ge(yh_sb, j + 1)
                        V.tensor_tensor(yl[:], bank[:, 2:4, :].rearrange("p b n -> p (b n)"), yh[:].bitcast(F32),
                                        ALU.subtract).then_inc(yl_sb, 1)
                    if i == 3:
                        link(V.tensor_copy(wc.unsqueeze(2), wt[:, :, bass.ds(j, 1)]))
                    if i in H_AT and H_AT[i]:
                        make_h(H_AT[i])
                    if i in HT_AT:
                        low_h(HT_AT[i])
                    if i == S_AT:
                        dve.wait_ge(st_ps, j + 1)
                        one_hot(j + 1)
                    if i == XG_AT:
                        split_rows(j + 1)
                    q = STREAM + i + 2
                    for h in range(2):
                        dve.wait_ge(hi_rdy, j * (2 * FFP) + (2 * q + h + 1))
                        V.tensor_tensor(wlo[:, q % SPLIT, h * HW:(h + 1) * HW], raw[:, q % RING, h * HW:(h + 1) * HW],
                                        whi[:, q % SPLIT, h * HW:(h + 1) * HW].bitcast(F32),
                                        ALU.subtract).then_inc(lo_rdy, 1)
                        if i == T_MID and h == 0:
                            low_h(NCH - 1)
                        if i == 1 and h == 0:
                            make_h(0)
                    if i in ACC_AT:
                        t, n = ACC_AT[i]
                        add_up(j * 4 + (2 * t + n + 1), t, n, 4 + n)
                assert chain.k == LINKS
            chain.sem, chain.base, chain.k = dve_tail, 0, 0
            V.tensor_copy(wc.unsqueeze(2), wt[:, :, bass.ds(njob, 1)]).then_inc(wc_rdy, 1)
            dve.wait_ge(wc_rdy, 1)
            dve.wait_ge(acc_rdy, njob * 4)
            V.memset(rstd[:], 0.0).then_inc(acc_done, 1)
            stats, scale = norm(3, None)
            for n in range(2):
                add_up(njob * 4 + (n + 1), 0, n, LB[n])
            dve.wait_ge(acc_rdy, njob * 4 + 2)
            link(V.memset(mv[:], 0.0))
            stats(0, None)
            dve.wait_ge(gb_in, 16 * 4)
            for n in range(2):
                sl = acc[:, 0, n * 512:(n + 1) * 512]
                V.scalar_tensor_tensor(sl, sl, mv[:, 0, 0:1], gbx[:, 0, n * 512:(n + 1) * 512],
                                       ALU.subtract, ALU.mult).then_inc(xc_rdy, 1)
                if n == 0:
                    dve.wait_ge(std_rdy, 3 * NT + 1)
                    V.reciprocal(rstd[:, 0:1], rstd[:, 0:1]).then_inc(rs_rdy, 1)
            dve.wait_ge(acc1_rdy, NT)
            stats(1, None)
            scale(1)


def pack_weights(v):
    W = np.empty((NPIECE, P, PW), np.float32)
    at = 0

    def ff(wg, wu, wd, at):
        g = wg.reshape(2, 4, P, NCH, FC)
        u = wu.reshape(2, 4, P, NCH, FC)
        d = wd.reshape(NCH, 2, P, D)
        for i, (kind, c) in enumerate(FFORDER):
            if kind == "D":
                W[at + i] = d[c].transpose(1, 0, 2).reshape(P, PW)
            else:
                h = "AB".index(kind)
                dst = W[at + i].reshape(P, 4, 2, FC)
                dst[:, :, 0] = g[h, :, :, c].transpose(1, 0, 2)
                dst[:, :, 1] = u[h, :, :, c].transpose(1, 0, 2)

    for l in range(DEPTH):
        wi = v["w_in"][l].reshape(KT, P, 7, 256)
        for j in (4, 0, 1, 5, 6, 2, 3):
            W[at] = wi[:, :, j].transpose(1, 0, 2).reshape(P, PW)
            at += 1
        wo = v["w_out"][l].reshape(4, 2, P, D)
        for j in range(4):
            W[at] = wo[j].transpose(1, 0, 2).reshape(P, PW)
            at += 1
        if l == 0:
            ff(v["ffn_w_gate"][0], v["ffn_w_up"][0], v["ffn_w_down"][0], at)
            at += FFP
        else:
            for e in range(NE):
                ff(v["exp_w_gate"][0, e], v["exp_w_up"][0, e], v["exp_w_down"][0, e], at)
                at += FFP
    return W


def kernel(**inputs):
    import concourse.bacc as bacc
    from concourse.bass_utils import run_bass_kernel_spmd as run

    v = {k: np.asarray(a) for k, a in inputs.items()}
    W = pack_weights(v)
    x = v["x"].reshape(NT, P, D)
    par = np.zeros((P, DEPTH, PARW), np.float32)
    wbd = np.zeros((DEPTH, P, 2, CT, P), np.float32)
    for l in range(DEPTH):
        cols = [v["conv_w"][l].reshape(TAPS * CT, P), v["conv_b"][l].reshape(CT, P), v["lru_ba"][l].reshape(CT, P),
                v["lru_bx"][l].reshape(CT, P), v["lru_lambda"][l].reshape(CT, P)]
        par[:, l, 0:CHANW] = np.concatenate(cols, 0).T
        s = v["attn_sink"][l].reshape(4, 2).T.reshape(8)
        par[:, l, CHANW:CHANW + 8] = s
        par[:, l, CHANW + 8:CHANW + 16] = s
        for g, name in enumerate(("lru_wa", "lru_wx")):
            for h in range(8):
                r = 64 * (h % 2)
                wbd[l, r:r + 64, g, h // 2, r:r + 64] = v[name][l, h]
    gb = np.empty((2 * DEPTH, P, 2, D), np.float32)
    for l in range(DEPTH):
        for a in range(2):
            gb[2 * l + a, :, 0] = v[f"ln{a + 1}_g"][l]
            gb[2 * l + a, :, 1] = v[f"ln{a + 1}_b"][l]
    cst = np.zeros((P, P + 64), np.float32)
    cst[:, 0:P] = np.eye(P)
    inv = (500000.0 ** (-np.arange(0, ROT, 2, dtype=np.float32) / np.float32(ROT))).astype(np.float32)
    ang = (np.arange(T, dtype=np.float32)[:, None] * inv[None, :]).reshape(NT, P, ROT // 2)
    tab = cst[:, P:].reshape(P, NT, 2, 2, ROT // 2)
    for a, fn in enumerate((np.cos, np.sin)):
        tab[:, :, a] = fn(ang).transpose(1, 0, 2)[:, :, None, :]
    rt = np.zeros((P, 3 * P + KT * NE + NE), np.float32)
    rt[:, 0:P] = np.triu(np.ones((P, P)), 1)
    rt[:, P:2 * P] = 1.0
    rt[:, 2 * P:3 * P] = np.arange(P)
    rt[:, 3 * P:3 * P + KT * NE] = v["router_w"][0].reshape(KT, P, NE).transpose(1, 0, 2).reshape(P, KT * NE)
    rt[:, 3 * P + KT * NE:] = v["router_b"][0]

    nc = bacc.Bacc("TRN2", target_bir_lowering=False, num_devices=1)
    arrays = {"W": W, "x_d": x, "par_d": par, "wbd_d": wbd.reshape(DEPTH, P, 1024),
              "gb_d": gb.reshape(2 * DEPTH, P, 2 * D), "cst_d": cst, "rt_d": rt}
    arrays = {k: np.ascontiguousarray(a) for k, a in arrays.items()}
    aps = [nc.dram_tensor(k, a.shape, F32, kind="ExternalInput").ap() for k, a in arrays.items()]
    out = nc.dram_tensor("out_d", (NT, P, D), F32, kind="ExternalOutput").ap()
    build(nc, *aps, out)
    r = run(nc, [arrays], core_ids=[0])
    return r.results[0]["out_d"].reshape(1, T, D)
```
